# Optimizing a Trainium2 kernel written in Bass

```python
import jax, jax.numpy as jnp
from jax import lax
import numpy as np

D_MODEL = 2048
BATCH = 1
SEQ = 256
DEPTH = 2

HEAD_DIM = 128
Q_BLOCK = 128
EPS = 1e-6
ATTN_SCALE = HEAD_DIM ** -0.5
FOX_HEADS = 8
FOX_GATE_BIAS = 4.0
HGRN_HEADS = 8
HGRN_KDIM = 128
HGRN_VDIM = 128
HGRN_CHUNK = 64
NSA_HEADS = 16
NSA_KV_HEADS = 4
NSA_GROUP = NSA_HEADS // NSA_KV_HEADS
CMP_BLOCK = 32
CMP_STRIDE = 16
CMP_HIDDEN = 256
SLC_BLOCK = 64
SLC_TOPK = 16
SLC_Q_CHUNK = 16
WINDOW = 512
MEM_LEN = 256
MEM_HEADS = 4
MEM_W = MEM_HEADS * HEAD_DIM
FFN_HIDDEN = -(-8 * D_MODEL // (3 * 256)) * 256

FOX_W = FOX_HEADS * HEAD_DIM
HGRN_KW = HGRN_HEADS * HGRN_KDIM
HGRN_VW = HGRN_HEADS * HGRN_VDIM
EVEN_SIZES = [FOX_W, FOX_W, FOX_W, FOX_HEADS, HGRN_KW, HGRN_KW, HGRN_VW, HGRN_VW]
EVEN_IN = sum(EVEN_SIZES)
EVEN_SPLITS = [int(v) for v in np.cumsum(EVEN_SIZES)[:-1]]
EVEN_OUT = FOX_W + HGRN_VW
NSA_QW = NSA_HEADS * HEAD_DIM
NSA_KVW = NSA_KV_HEADS * HEAD_DIM
ODD_SIZES = [NSA_QW] + [NSA_KVW] * 6 + [3 * NSA_HEADS]
ODD_IN = sum(ODD_SIZES)
ODD_SPLITS = [int(v) for v in np.cumsum(ODD_SIZES)[:-1]]

kernel_name = 'fox_hgrn2_nsa_hybrid'

def rms_norm(x, gain):
    xf = x.astype(jnp.float32)
    y = xf * lax.rsqrt(jnp.mean(xf * xf, axis=-1, keepdims=True) + EPS)
    return (y * gain.astype(jnp.float32)).astype(x.dtype)

def split_heads(t, n):
    B, T, _ = t.shape
    return t.reshape(B, T, n, -1).transpose(0, 2, 1, 3)

def merge_heads(t):
    B, n, T, d = t.shape
    return t.transpose(0, 2, 1, 3).reshape(B, T, n * d)

def alibi_slopes(n):
    return 2.0 ** (-8.0 * jnp.arange(1, n + 1, dtype=jnp.float32) / n)

def masked_softmax(s, mask):
    s = jnp.where(mask, s.astype(jnp.float32), -jnp.inf)
    m = jnp.max(s, axis=-1, keepdims=True)
    m = jnp.where(jnp.isfinite(m), m, 0.0)
    p = jnp.exp(s - m)
    z = jnp.sum(p, axis=-1, keepdims=True)
    return p / jnp.where(z > 0, z, 1.0)

def forgetting_attention(q, k, v, log_f):
    B, H, T, d = q.shape
    c = jnp.cumsum(log_f, axis=-1)
    nb = T // Q_BLOCK
    qb = jnp.moveaxis(q.reshape(B, H, nb, Q_BLOCK, d), 2, 0)
    cb = jnp.moveaxis(c.reshape(B, H, nb, Q_BLOCK), 2, 0)
    kpos = jnp.arange(T)

    def block(args):
        qi, ci, i = args
        tq = i * Q_BLOCK + jnp.arange(Q_BLOCK)
        s = jnp.einsum('bhqd,bhkd->bhqk', qi, k, preferred_element_type=jnp.float32) * ATTN_SCALE
        s = s + ci[..., :, None] - c[..., None, :]
        s = jnp.where(tq[:, None] >= kpos[None, :], s, -jnp.inf)
        p = jax.nn.softmax(s, axis=-1)
        return jnp.einsum('bhqk,bhkd->bhqd', p, v.astype(jnp.float32))

    o = lax.map(block, (qb, cb, jnp.arange(nb)))
    return jnp.moveaxis(o, 0, 2).reshape(B, H, T, d)

def hgrn2_recurrence(q, k, v, log_f):
    B, H, T, dk = q.shape
    dv = v.shape[-1]
    C = HGRN_CHUNK
    nc = T // C

    def to_chunks(t):
        return jnp.moveaxis(t.reshape(B, H, nc, C, t.shape[-1]), 2, 0)

    causal = jnp.tril(jnp.ones((C, C), dtype=bool))[:, :, None]

    def step(S, inp):
        qi, ki, vi, gi = inp
        b = jnp.cumsum(gi, axis=2)
        diff = b[:, :, :, None, :] - b[:, :, None, :, :]
        decay = jnp.exp(jnp.where(causal, diff, -jnp.inf))
        A = jnp.einsum('bhtk,bhtsk,bhsk->bhts', qi, decay, ki)
        o = jnp.einsum('bhts,bhsv->bhtv', A, vi) + jnp.einsum('bhtk,bhkv->bhtv', qi * jnp.exp(b), S)
        b_last = b[:, :, -1:, :]
        S = jnp.exp(b_last[:, :, 0, :])[..., None] * S + jnp.einsum('bhsk,bhsv->bhkv', ki * jnp.exp(b_last - b), vi)
        return S, o

    S0 = jnp.zeros((B, H, dk, dv), jnp.float32)
    _, o = lax.scan(step, S0, tuple(to_chunks(t) for t in (q, k, v, log_f)))
    return jnp.moveaxis(o, 0, 2).reshape(B, H, T, dv)

def even_mixer(h, w_in, w_out, f_bias, q_gain, k_gain, lb, o_gain):
    f32 = jnp.float32
    fq, fk, fv, ff, hq, hf, hi, hg = jnp.split(h @ w_in, EVEN_SPLITS, axis=-1)
    q = rms_norm(split_heads(fq, FOX_HEADS), q_gain)
    k = rms_norm(split_heads(fk, FOX_HEADS), k_gain)
    v = split_heads(fv, FOX_HEADS)
    log_f_fox = jax.nn.log_sigmoid(ff.astype(f32) + f_bias.astype(f32)).transpose(0, 2, 1)
    o_fox = forgetting_attention(q, k, v, log_f_fox)
    z = split_heads(hf, HGRN_HEADS).astype(f32)
    lb_h = lb.astype(f32).reshape(HGRN_HEADS, 1, HGRN_KDIM)
    log_f = jnp.logaddexp(jnp.log(lb_h), jnp.log1p(-lb_h) + jax.nn.log_sigmoid(z))
    k_h = (1.0 - lb_h) * jax.nn.sigmoid(-z)
    q_h = jax.nn.silu(split_heads(hq, HGRN_HEADS).astype(f32))
    o_h = hgrn2_recurrence(q_h, k_h, split_heads(hi, HGRN_HEADS).astype(f32), log_f)
    o_h = rms_norm(o_h, o_gain) * jax.nn.silu(split_heads(hg, HGRN_HEADS).astype(f32))
    o = jnp.concatenate([merge_heads(o_fox), merge_heads(o_h)], axis=-1).astype(h.dtype)
    return o @ w_out

def compress_blocks(t, pe, w1, w2):
    T = t.shape[2]
    n_cmp = (T - CMP_BLOCK) // CMP_STRIDE + 1
    idx = (jnp.arange(n_cmp) * CMP_STRIDE)[:, None] + jnp.arange(CMP_BLOCK)[None, :]
    blocks = t[:, :, idx, :] + pe
    hid = jax.nn.gelu(jnp.einsum('bgnld,ldm->bgnm', blocks, w1))
    return jnp.einsum('bgnm,md->bgnd', hid, w2)

def nsa_mixer(h, w_in, w_out, q_gain, k_gain, pe_k, w1_k, w2_k, pe_v, w1_v, w2_v):
    B, T, _ = h.shape
    G, J, d = NSA_KV_HEADS, NSA_GROUP, HEAD_DIM
    f32 = jnp.float32
    q, kc, vc, ks, vs, kw, vw, gt = jnp.split(h @ w_in, ODD_SPLITS, axis=-1)
    q = rms_norm(q.reshape(B, T, G, J, d).transpose(0, 2, 3, 1, 4), q_gain)

    def kv_heads(t):
        return t.reshape(B, T, G, d).transpose(0, 2, 1, 3)

    k_cmp = rms_norm(compress_blocks(kv_heads(kc), pe_k, w1_k, w2_k), k_gain[0])
    v_cmp = compress_blocks(kv_heads(vc), pe_v, w1_v, w2_v).astype(f32)
    k_slc = rms_norm(kv_heads(ks), k_gain[1])
    v_slc = kv_heads(vs)
    k_win = rms_norm(kv_heads(kw), k_gain[2])
    v_win = kv_heads(vw)
    gates = jax.nn.sigmoid(gt.astype(f32)).reshape(B, T, G, J, 3).transpose(0, 2, 3, 1, 4)
    sl5 = alibi_slopes(NSA_HEADS).reshape(G, J)[None, :, :, None, None]

    n_cmp = (T - CMP_BLOCK) // CMP_STRIDE + 1
    cmp_start = jnp.arange(n_cmp) * CMP_STRIDE
    cmp_end = cmp_start + CMP_BLOCK - 1
    cmp_mid = cmp_start.astype(f32) + 0.5 * (CMP_BLOCK - 1)
    n_slc = T // SLC_BLOCK
    slc_start = jnp.arange(n_slc) * SLC_BLOCK
    overlap = ((cmp_start[:, None] <= slc_start[None, :] + SLC_BLOCK - 1)
               & (cmp_end[:, None] >= slc_start[None, :])).astype(f32)
    n_sel = min(SLC_TOPK, n_slc)
    k_win_p = jnp.pad(k_win, ((0, 0), (0, 0), (WINDOW, 0), (0, 0)))
    v_win_p = jnp.pad(v_win, ((0, 0), (0, 0), (WINDOW, 0), (0, 0))).astype(f32)
    band = jnp.arange(WINDOW + Q_BLOCK)
    blk = jnp.arange(n_slc)

    def query_block(i):
        t = i * Q_BLOCK + jnp.arange(Q_BLOCK)
        qi = lax.dynamic_slice_in_dim(q, i * Q_BLOCK, Q_BLOCK, axis=3)
        s = jnp.einsum('bgjqd,bgnd->bgjqn', qi, k_cmp, preferred_element_type=f32) * ATTN_SCALE
        s = s - sl5 * (t[:, None].astype(f32) - cmp_mid[None, :])
        p_cmp = masked_softmax(s, cmp_end[None, :] <= t[:, None])
        o_cmp = jnp.einsum('bgjqn,bgnd->bgjqd', p_cmp, v_cmp)
        imp = jnp.einsum('bgjqn,nm->bgqm', p_cmp, overlap)
        imp = jnp.where(slc_start[None, :] > t[:, None], -jnp.inf, imp)
        imp = jnp.where((blk[None, :] == (t // SLC_BLOCK)[:, None]) | (blk[None, :] == 0), jnp.inf, imp)
        _, idx = lax.top_k(imp, n_sel)
        kwi = lax.dynamic_slice_in_dim(k_win_p, i * Q_BLOCK, WINDOW + Q_BLOCK, axis=2)
        vwi = lax.dynamic_slice_in_dim(v_win_p, i * Q_BLOCK, WINDOW + Q_BLOCK, axis=2)
        kpos = i * Q_BLOCK - WINDOW + band
        dist = t[:, None] - kpos[None, :]
        s = jnp.einsum('bgjqd,bgkd->bgjqk', qi, kwi, preferred_element_type=f32) * ATTN_SCALE
        s = s - sl5 * dist.astype(f32)
        p_win = masked_softmax(s, (dist >= 0) & (dist < WINDOW) & (kpos[None, :] >= 0))
        o_win = jnp.einsum('bgjqk,bgkd->bgjqd', p_win, vwi)
        return o_cmp, o_win, idx.astype(jnp.int32)

    nb = T // Q_BLOCK
    o_cmp, o_win, idx = lax.map(query_block, jnp.arange(nb))
    o_cmp = jnp.moveaxis(o_cmp, 0, 3).reshape(B, G, J, T, d)
    o_win = jnp.moveaxis(o_win, 0, 3).reshape(B, G, J, T, d)
    idx = jnp.moveaxis(idx, 0, 2).reshape(B, G, T, n_sel)

    c = SLC_Q_CHUNK
    n_sc = T // c
    ks_blocks = k_slc.reshape(B, G, n_slc, SLC_BLOCK, d)
    vs_blocks = v_slc.reshape(B, G, n_slc, SLC_BLOCK, d)
    q_ch = jnp.moveaxis(q.reshape(B, G, J, n_sc, c, d), 3, 0)
    idx_ch = jnp.moveaxis(idx.reshape(B, G, n_sc, c, n_sel), 2, 0)
    bi = jnp.arange(B)[:, None, None, None]
    gi = jnp.arange(G)[None, :, None, None]
    inner = jnp.arange(SLC_BLOCK)
    M = n_sel * SLC_BLOCK

    def select_chunk(args):
        qj, ij, j = args
        t = j * c + jnp.arange(c)
        kg = ks_blocks[bi, gi, ij].reshape(B, G, c, M, d)
        vg = vs_blocks[bi, gi, ij].reshape(B, G, c, M, d).astype(f32)
        kpos = (ij[..., None] * SLC_BLOCK + inner).reshape(B, G, c, M)
        dist = t[None, None, :, None] - kpos
        s = jnp.einsum('bgjcd,bgcmd->bgjcm', qj, kg, preferred_element_type=f32) * ATTN_SCALE
        s = s - sl5 * dist[:, :, None].astype(f32)
        p = masked_softmax(s, (dist >= 0)[:, :, None])
        return jnp.einsum('bgjcm,bgcmd->bgjcd', p, vg)

    o_slc = lax.map(select_chunk, (q_ch, idx_ch, jnp.arange(n_sc)))
    o_slc = jnp.moveaxis(o_slc, 0, 3).reshape(B, G, J, T, d)

    o = gates[..., 0:1] * o_cmp + gates[..., 1:2] * o_slc + gates[..., 2:3] * o_win
    o = o.transpose(0, 3, 1, 2, 4).reshape(B, T, NSA_QW).astype(h.dtype)
    return o @ w_out

def memory_attention(h, mem_n, wq, wkv, wo, q_gain, k_gain):
    q = rms_norm(split_heads(h @ wq, MEM_HEADS), q_gain)
    k, v = jnp.split(mem_n @ wkv, 2, axis=-1)
    k = rms_norm(split_heads(k, MEM_HEADS), k_gain)
    v = split_heads(v, MEM_HEADS).astype(jnp.float32)
    s = jnp.einsum('bhqd,bhkd->bhqk', q, k, preferred_element_type=jnp.float32) * ATTN_SCALE
    p = jax.nn.softmax(s, axis=-1)
    o = jnp.einsum('bhqk,bhkd->bhqd', p, v)
    return merge_heads(o).astype(h.dtype) @ wo

def swiglu(h, w1, w3, w2):
    return (jax.nn.silu(h @ w1) * (h @ w3)) @ w2

def setup_inputs(seed: int = 0) -> dict:
    key = jax.random.key(seed)
    keys = iter(jax.random.split(key, 64))
    f32 = jnp.float32
    n_even = (DEPTH + 1) // 2
    n_odd = DEPTH // 2

    def dense(shape, fan_in):
        return jax.random.normal(next(keys), shape, f32) * (fan_in ** -0.5)

    def gain(shape):
        return 1.0 + 0.02 * jax.random.normal(next(keys), shape, f32)

    def small(shape, scale):
        return scale * jax.random.normal(next(keys), shape, f32)

    return {
        'x': jax.random.normal(next(keys), (BATCH, SEQ, D_MODEL), f32),
        'mem': jax.random.normal(next(keys), (BATCH, MEM_LEN, D_MODEL), f32),
        'norm_mix': gain((DEPTH, D_MODEL)),
        'norm_mem': gain((DEPTH, D_MODEL)),
        'norm_ffn': gain((DEPTH, D_MODEL)),
        'mem_in_gain': gain((DEPTH, D_MODEL)),
        'even_w_in': dense((n_even, D_MODEL, EVEN_IN), D_MODEL),
        'even_w_out': dense((n_even, EVEN_OUT, D_MODEL), EVEN_OUT),
        'fox_f_bias': FOX_GATE_BIAS + small((n_even, FOX_HEADS), 1.0),
        'fox_q_gain': gain((n_even, HEAD_DIM)),
        'fox_k_gain': gain((n_even, HEAD_DIM)),
        'hgrn_lb_logits': small((n_even, HGRN_KW), 1.0),
        'hgrn_o_gain': gain((n_even, HGRN_VDIM)),
        'odd_w_in': dense((n_odd, D_MODEL, ODD_IN), D_MODEL),
        'odd_w_out': dense((n_odd, NSA_QW, D_MODEL), NSA_QW),
        'nsa_q_gain': gain((n_odd, HEAD_DIM)),
        'nsa_k_gain': gain((n_odd, 3, HEAD_DIM)),
        'cmp_pe_k': small((n_odd, CMP_BLOCK, HEAD_DIM), 0.02),
        'cmp_w1_k': dense((n_odd, CMP_BLOCK, HEAD_DIM, CMP_HIDDEN), CMP_BLOCK * HEAD_DIM),
        'cmp_w2_k': dense((n_odd, CMP_HIDDEN, HEAD_DIM), CMP_HIDDEN),
        'cmp_pe_v': small((n_odd, CMP_BLOCK, HEAD_DIM), 0.02),
        'cmp_w1_v': dense((n_odd, CMP_BLOCK, HEAD_DIM, CMP_HIDDEN), CMP_BLOCK * HEAD_DIM),
        'cmp_w2_v': dense((n_odd, CMP_HIDDEN, HEAD_DIM), CMP_HIDDEN),
        'mem_wq': dense((DEPTH, D_MODEL, MEM_W), D_MODEL),
        'mem_wkv': dense((DEPTH, D_MODEL, 2 * MEM_W), D_MODEL),
        'mem_wo': dense((DEPTH, MEM_W, D_MODEL), MEM_W),
        'mem_q_gain': gain((DEPTH, HEAD_DIM)),
        'mem_k_gain': gain((DEPTH, HEAD_DIM)),
        'ffn_w1': dense((DEPTH, D_MODEL, FFN_HIDDEN), D_MODEL),
        'ffn_w3': dense((DEPTH, D_MODEL, FFN_HIDDEN), D_MODEL),
        'ffn_w2': dense((DEPTH, FFN_HIDDEN, D_MODEL), FFN_HIDDEN),
    }

def reference(x, mem, norm_mix, norm_mem, norm_ffn, mem_in_gain, even_w_in, even_w_out, fox_f_bias,
              fox_q_gain, fox_k_gain, hgrn_lb_logits, hgrn_o_gain, odd_w_in, odd_w_out, nsa_q_gain,
              nsa_k_gain, cmp_pe_k, cmp_w1_k, cmp_w2_k, cmp_pe_v, cmp_w1_v, cmp_w2_v, mem_wq, mem_wkv,
              mem_wo, mem_q_gain, mem_k_gain, ffn_w1, ffn_w3, ffn_w2):
    lb_cum = jnp.cumsum(jax.nn.softmax(hgrn_lb_logits.astype(jnp.float32), axis=0), axis=0)
    hgrn_lb = lb_cum - lb_cum[0:1]
    for layer in range(DEPTH):
        h = rms_norm(x, norm_mix[layer])
        if layer % 2 == 0:
            e = layer // 2
            mix = even_mixer(h, even_w_in[e], even_w_out[e], fox_f_bias[e], fox_q_gain[e], fox_k_gain[e],
                             hgrn_lb[e], hgrn_o_gain[e])
        else:
            o = layer // 2
            mix = nsa_mixer(h, odd_w_in[o], odd_w_out[o], nsa_q_gain[o], nsa_k_gain[o], cmp_pe_k[o],
                            cmp_w1_k[o], cmp_w2_k[o], cmp_pe_v[o], cmp_w1_v[o], cmp_w2_v[o])
        x = x + mix.astype(x.dtype)
        h = rms_norm(x, norm_mem[layer])
        mem_n = rms_norm(mem, mem_in_gain[layer])
        x = x + memory_attention(h, mem_n, mem_wq[layer], mem_wkv[layer], mem_wo[layer],
                                 mem_q_gain[layer], mem_k_gain[layer]).astype(x.dtype)
        h = rms_norm(x, norm_ffn[layer])
        x = x + swiglu(h, ffn_w1[layer], ffn_w3[layer], ffn_w2[layer]).astype(x.dtype)
    return x


_drawn_inputs = setup_inputs


def setup_inputs(seed=0):
    import zlib

    import numpy as np

    out = dict(_drawn_inputs(seed))
    spreads = {}
    factors = {'norm_mix': 3.141,
     'norm_mem': 8.0,
     'norm_ffn': 2.965,
     'mem_in_gain': 8.0,
     'fox_q_gain': 8.0,
     'fox_k_gain': 8.0,
     'hgrn_o_gain': 6.467,
     'nsa_q_gain': 8.0,
     'nsa_k_gain': 8.0,
     'cmp_pe_k': 8.0,
     'cmp_pe_v': 21.761,
     'mem_q_gain': 8.0,
     'mem_k_gain': 8.0}
    for name, (base, spread) in spreads.items():
        noise = np.random.default_rng([zlib.crc32(name.encode()), seed]).standard_normal(out[name].shape)
        drawn = base * np.exp(spread * noise) if base else spread * noise
        out[name] = __import__('jax').numpy.asarray(drawn.astype(out[name].dtype))
    for name, factor in factors.items():
        out[name] = (out[name] * factor).astype(out[name].dtype)
    return out
```

```python
import concourse.bass as bass
from concourse import mybir
from contextlib import ExitStack

F32 = mybir.dt.float32
F32R = mybir.dt.float32r
U8 = mybir.dt.uint8
ALU = mybir.AluOpType
ACT = mybir.ActivationFunctionType
AX_X = mybir.AxisListType.X

P = 128
T = 256
D = 2048
KT = D // P
HD = 128
NB = 512
LEAD = 4
RAW = 4
FFN = 5632
FB = FFN // NB
FT = FFN // P
EPS = 1e-6
NEG = -1e30
FOX_HEADS = 8
HG_HEADS = 8
NSA_HEADS = 16
MEM_HEADS = 4
CMP_L = 32
CMP_S = 16
N_CMP = (T - CMP_L) // CMP_S + 1
CMP_COLS = 4 * N_CMP
LEVELS = 9

SECTIONS = [("kv0", 2, 16), ("in0", 14, 112), ("out0", 4, 32), ("wq0", 1, 8), ("wo0", 4, 8),
            ("up0", 22, 176), ("dn0", 4, 88),
            ("kcvc", 2, 16), ("cmp", 2, 16), ("kvs", 4, 32), ("q", 4, 32), ("kv1", 2, 16),
            ("out1", 4, 32), ("wq1", 1, 8), ("wo1", 4, 8), ("up1", 22, 176), ("dn1", 4, 88)]
TICK, BLOCK = {}, {}
_t = _b = 0
for _name, _nb, _nt in SECTIONS:
    TICK[_name], BLOCK[_name] = _t, _b
    _t += _nt
    _b += _nb
TICKS = _t

IN0 = ["hq", "hq", "hf", "hf", "hi", "hi", "hg", "hg", "fq", "fq", "fk", "fk", "fv", "fv"]
IN0_COL = {"fq": 0, "fk": 1024, "fv": 2048, "hq": 3080, "hf": 4104, "hi": 5128, "hg": 6152}
FF_COL = 3072
ODD_COL = {"q": 0, "kc": 2048, "vc": 2560, "ks": 3072, "vs": 3584, "kw": 4096, "vw": 4608}
GT_COL = 5120
HG_START = 38
HG_TICKS = 2 * (4 * LEVELS - 1) + 10

S_PEK, S_PEV, S_FQ, S_FK, S_HO, S_NQ, S_NK, S_MQ, S_MK = 0, 32, 64, 65, 66, 67, 68, 71, 73
S_ROWS = 75
G_MIX, G_MEM, G_FFN, G_IN = 0, 32, 64, 96


def trunk(nc, A, out, stop=None, dbg=None):
    ctx = ExitStack()
    with ctx:
        def sem(name):
            return ctx.enter_context(nc.semaphore(name))

        base = (nc.sbuf_base + 63) // 64 * 64
        top = [base]

        def place(name, shape, dt=F32):
            n = 1
            for s in shape[1:]:
                n *= s
            at = top[0]
            top[0] += (n * (1 if dt == U8 else 4) + 31) // 32 * 32
            return nc.alloc_sbuf_tensor_at(name, shape, dt, offset=at)

        raw = place("raw", [P, RAW, 4, NB])
        w_hi = place("w_hi", [P, LEAD, 2, NB], F32R)
        w_lo = place("w_lo", [P, LEAD, 2, NB], F32R)
        xT = place("xT", [P, KT, T])
        h_hi_at = top[0]
        h_hi = place("h_hi", [P, KT, T], F32R)
        h_lo = place("h_lo", [P, KT, T], F32R)
        tmp = place("tmp", [P, 4, T])
        ident = place("ident", [P, P])
        ones = place("ones", [P, P])
        G = place("G", [P, P])
        S = place("S", [P, S_ROWS])
        rinv = place("rinv", [P, T])
        cneg = place("cneg", [FOX_HEADS, T])
        eps = place("eps", [P, 2])
        R = top[0]
        K = 1024

        def at(name, shape, off, dt=F32):
            return nc.alloc_sbuf_tensor_at(name, shape, dt, offset=R + off)

        hid_hi = at("hid_hi", [P, FT, T], 0, F32R)
        hid_lo = at("hid_lo", [P, FT, T], 44 * K, F32R)
        mk = at("mk", [P, MEM_HEADS, T], 0)
        mv = at("mv", [P, 2, NB], 4 * K)
        hq = at("hq", [P, 8, T], 8 * K)
        hz = at("hz", [P, 8, T], 16 * K)
        hb = at("hb", [P, 8, T], 24 * K)
        hv = at("hv", [P, 2, 1024], 32 * K)
        hg = at("hg", [P, 8, T], 40 * K)
        fq = at("fq", [P, 8, T], 48 * K)
        fk = at("fk", [P, 8, T], 56 * K)
        fv = at("fv", [P, 2, 1024], 64 * K)
        decay = at("decay", [P, 2, 512], 72 * K)
        kd = at("kd", [P, 2, 512], 76 * K)
        qd = at("qd", [P, 2, 512], 80 * K)
        AT = at("AT", [P, 6, P], 84 * K)
        lmask = at("lmask", [P, 8, P], 87 * K, U8)
        memn = [(at("memn_hi0", [P, KT, T], 24 * K, F32R), at("memn_lo0", [P, KT, T], 40 * K, F32R)),
                (at("memn_hi1", [P, KT, T], 56 * K, F32R), at("memn_lo1", [P, KT, T], 72 * K, F32R))]
        mtok = [at("mtok0", [P, 2, D], 56 * K), at("mtok1", [P, 2, D], 8 * K)]
        xtok = at("xtok", [P, 2, D], 8 * K)
        maskf = at("maskf", [P, 8, P], 72 * K)
        g_rows = at("g_rows", [P, P], 80 * K)
        s_rows = at("s_rows", [S_ROWS, P], 81 * K)
        mss = at("mss", [P, 4], 82 * K)
        upper = at("upper", [P, P], 56 * K)
        wff = at("wff", [P, KT, 8], 64 * K)
        wff_hi = at("wff_hi", [P, KT, 8], 64 * K + 512, F32R)
        wff_lo = at("wff_lo", [P, KT, 8], 65 * K, F32R)
        fbias = at("fbias", [1, 8], 65 * K + 512)
        lf = at("lf", [P, 4, 16], 65 * K + 576)
        fp = at("fp", [P, 2, 384], 72 * K)
        fpt = at("fpt", [P, 2, 384], 75 * K)
        fmask = at("fmask", [P, T], 78 * K)
        fst = at("fst", [P, 2, 8], 79 * K)
        mq = at("mq", [P, MEM_HEADS, T], 8 * K)
        mp = at("mp", [P, 2, 2, T], 12 * K)
        mpt = at("mpt", [P, 2, 2, T], 16 * K)
        mst = at("mst", [P, 2, 8], 20 * K)
        mo_hi = at("mo_hi", [P, MEM_HEADS, T], 24 * K, F32R)
        mo_lo = at("mo_lo", [P, MEM_HEADS, T], 28 * K, F32R)
        otok = nc.alloc_sbuf_tensor_at("otok", [P, 2, D], F32, offset=h_hi_at)
        nq = at("nq", [P, NSA_HEADS, T], 8 * K)
        kw = at("kw", [P, 4, T], 24 * K)
        ks = at("ks", [P, 4, T], 28 * K)
        vw = at("vw", [P, 2, NB], 32 * K)
        vs = at("vs", [P, 2, NB], 36 * K)
        kcT = at("kcT", [P, 4, T], 56 * K)
        vcT = at("vcT", [P, 4, T], 60 * K)
        xc = at("xc", [P, CMP_L, 64], 64 * K)
        xc_hi = [at("xck_hi", [P, CMP_L, 64], 24 * K, F32R), at("xcv_hi", [P, CMP_L, 64], 72 * K, F32R)]
        xc_lo = [at("xck_lo", [P, CMP_L, 64], 32 * K, F32R), at("xcv_lo", [P, CMP_L, 64], 80 * K, F32R)]
        hidc = at("hidc", [P, 2, 2, 64], 40 * K)
        w2c = at("w2c", [P, 2, 2, P], 41 * K)
        kcmp = at("kcmp", [P, 64], 43 * K)
        kcr = at("kcr", [P, 64], 43 * K + 256)
        vcmp = at("vcmp", [N_CMP, 4, P], 43 * K + 512)
        gate = at("gate", [P, 2, 48], 45 * K + 512)
        dm = at("dm", [P, 384], 46 * K)
        dmc = at("dmc", [P, 2, 16], 47 * K + 512)
        np_ = at("np_", [P, 2, 384], 48 * K)
        npc = at("npc", [P, 2, 16], 51 * K)
        npt = at("npt", [P, 2, 384], 51 * K + 512)
        nptc = at("nptc", [N_CMP, 2, P], 54 * K + 512)
        nst = at("nst", [P, 4, 8], 55 * K + 512)
        wgt = at("wgt", [P, KT, 48], 44 * K)
        wgt_hi = at("wgt_hi", [P, KT, 48], 47 * K, F32R)
        wgt_lo = at("wgt_lo", [P, KT, 48], 50 * K, F32R)

        acc = ctx.enter_context(nc.psum_tensor("acc", [P, 2, 2 * NB], F32))
        att = ctx.enter_context(nc.psum_tensor("att", [P, 4, NB], F32))

        raw_full = [sem(f"raw_full{i}") for i in range(RAW)]
        hi_ready = sem("hi_ready")
        lo_ready = sem("lo_ready")
        pieces_done = sem("pieces_done")
        acc_free = [sem("acc_free0"), sem("acc_free1")]
        consts = sem("consts")
        small_in = sem("small_in")
        mtok_in = sem("mtok_in")
        xtok_in = sem("xtok_in")
        gains_t = sem("gains_t")
        gains = sem("gains")
        m_ssq, m_rms, m_scaled = sem("m_ssq"), sem("m_rms"), sem("m_scaled")
        m_rinv = sem("m_rinv")
        m_turn, m_hi, m_ready = sem("m_turn"), sem("m_hi"), sem("m_ready")
        x_turn, x_copied, x_ready = sem("x_turn"), sem("x_copied"), sem("x_ready")
        sq_ready, sq_used = sem("sq_ready"), sem("sq_used")
        rms_ready, rinv_ready = sem("rms_ready"), sem("rinv_ready")
        h_tmp, h_hi_ready, h_ready = sem("h_tmp"), sem("h_hi_ready"), sem("h_ready")
        hn_raw, hn_sq, hn_sum = sem("hn_raw"), sem("hn_sq"), sem("hn_sum")
        hn_rms, hn_rinv, hn_out = sem("hn_rms"), sem("hn_rinv"), sem("hn_out")
        ff_w, ff_whi, ff_wlo = sem("ff_w"), sem("ff_whi"), sem("ff_wlo")
        ff_sum, ff_z, ff_l, ff_lf, ff_c, ff_cneg = (sem(n) for n in
            ("ff_sum", "ff_z", "ff_l", "ff_lf", "ff_c", "ff_cneg"))
        upper_ready, lmask_ready, fmask_ready = sem("upper_ready"), sem("lmask_ready"), sem("fmask_ready")
        maskf_ready = sem("maskf_ready")
        hg_q, hg_z, hg_abs, hg_lf, hg_kin, hg_k, hg_b, hg_v, hg_gate = (sem(n) for n in
            ("hg_q", "hg_z", "hg_abs", "hg_lf", "hg_kin", "hg_k", "hg_b", "hg_v", "hg_gate"))
        hg_diff, hg_decay, hg_kd, hg_qd, hg_scores, hg_merged, hg_zero = (sem(n) for n in
            ("hg_diff", "hg_decay", "hg_kd", "hg_qd", "hg_scores", "hg_merged", "hg_zero"))
        hg_o, hg_oraw, hg_osq, hg_osum, hg_orms, hg_orinv, hg_onorm, hg_out = (sem(n) for n in
            ("hg_o", "hg_oraw", "hg_osq", "hg_osum", "hg_orms", "hg_orinv", "hg_onorm", "hg_out"))
        f_v, f_s, f_p, f_max, f_nmax, f_exp, f_rz, f_pn, f_t, f_pt, f_o, f_out = (sem(n) for n in
            ("f_v", "f_s", "f_p", "f_max", "f_nmax", "f_exp", "f_rz", "f_pn", "f_t", "f_pt", "f_o", "f_out"))
        m_v, m_s, m_max, m_nmax, m_exp, m_rz, m_pn, m_t, m_pt, m_o, m_ohi, m_out = (sem(n) for n in
            ("m_v", "m_s", "m_max", "m_nmax", "m_exp", "m_rz", "m_pn", "m_t", "m_pt", "m_o", "m_ohi", "m_out"))
        u_silu, u_prod, u_hi, u_ready = sem("u_silu"), sem("u_prod"), sem("u_hi"), sem("u_ready")
        out_turn, out_copied, out_done = sem("out_turn"), sem("out_copied"), sem("out_done")
        n_w, n_whi, n_wlo, n_gsum, n_gate = (sem(n) for n in ("n_w", "n_whi", "n_wlo", "n_gsum", "n_gate"))
        c_in, c_x, c_hi, c_lo, c_hid, c_w2, c_k, c_v = (sem(n) for n in
            ("c_in", "c_x", "c_hi", "c_lo", "c_hid", "c_w2", "c_k", "c_v"))
        c_ksum, c_kraw, c_ksq, c_krms, c_krinv, c_kout, c_vout = (sem(n) for n in
            ("c_ksum", "c_kraw", "c_ksq", "c_krms", "c_krinv", "c_kout", "c_vout"))
        n_v, n_s, n_p, n_max, n_nmax, n_exp, n_rz, n_pn = (sem(n) for n in
            ("n_v", "n_s", "n_p", "n_max", "n_nmax", "n_exp", "n_rz", "n_pn"))
        n_t, n_pt, n_o, n_out = sem("n_t"), sem("n_pt"), sem("n_o"), sem("n_out")
        n_mask, n_rzs, n_tc, n_ptc = sem("n_mask"), sem("n_rzs"), sem("n_tc"), sem("n_ptc")
        dbg_done = sem("dbg_done")

        sections = [s for s, _, _ in SECTIONS]
        upto = len(sections) if stop is None else sections.index(stop) + 1
        last_tick = TICKS if stop is None else TICK[stop] + [n for s, _, n in SECTIONS if s == stop][0]
        run = set(sections[:upto])

        def w_rows(w):
            return w.rearrange("(k p) n -> p k n", p=P)

        w_in0 = w_rows(A["even_w_in"][0])
        w_in1 = w_rows(A["odd_w_in"][0])
        w_out = [w_rows(A["even_w_out"][0]), w_rows(A["odd_w_out"][0])]
        wq = [w_rows(A["mem_wq"][l]) for l in range(2)]
        wkv = [w_rows(A["mem_wkv"][l]) for l in range(2)]
        wo = [w_rows(A["mem_wo"][l]) for l in range(2)]
        w1 = [w_rows(A["ffn_w1"][l]) for l in range(2)]
        w3 = [w_rows(A["ffn_w3"][l]) for l in range(2)]
        w2 = [w_rows(A["ffn_w2"][l]) for l in range(2)]
        cw1 = [A[n][0].rearrange("l d m -> d l m") for n in ("cmp_w1_k", "cmp_w1_v")]

        FILL = {"in0": 0, "out0": 1, "wq0": 2, "up0": 3, "kcvc": 4, "out1": 5, "wq1": 6, "up1": 7}
        LAST_READ = {0: None, 1: TICK["out0"], 2: TICK["wq0"], 3: TICK["wo0"], 4: TICK["dn0"],
                     5: TICK["kv1"], 6: TICK["wq1"], 7: TICK["wo1"]}
        HN = {"mk0": 0, "fq0": 1, "fq1": 2, "fk0": 3, "fk1": 4, "mq0": 5, "kw": 6, "ks": 7,
              "q0": 8, "q1": 9, "q2": 10, "q3": 11, "mk1": 12, "mq1": 13}

        block = ctx.enter_context(nc.Block())

        @block.sync
        def _(sp):
            def slab(s, src, more=0):
                if s >= RAW:
                    sp.wait_ge(lo_ready, 2 * (s - RAW) + 2 + more)
                sp.dma_start(raw[:, s % RAW, :, :], src).then_inc(raw_full[s % RAW], 16)

            def block_rows(s, w, col, rows=(0, 1, 2, 3), more=0):
                for c, r in enumerate(rows):
                    slab(s + c, w[:, 4 * r:4 * r + 4, col], more)

            def cols(n, wide=NB):
                return slice(n, n + wide)

            def up(l):
                s = TICK[f"up{l}"] // 2
                with sp.Fori(0, FB) as i:
                    block_rows(s, w1[l], bass.ds(i * NB, NB), more=i * 16)
                    block_rows(s + 4, w3[l], bass.ds(i * NB, NB), more=i * 16)

            def down(l):
                for half in range(2):
                    s = TICK[f"dn{l}"] // 2 + 22 * half
                    for b in range(2):
                        slab(s + b, w2[l][:, 0:4, cols((2 * half + b) * NB)])
                    with sp.Fori(0, 5) as i:
                        for j in range(4):
                            slab(s + 2 + j, w2[l][:, bass.ds(i * 8 + 4 + j // 2 * 4, 4),
                                                  cols((2 * half + j % 2) * NB)], i * 8)

            def memory(l):
                if f"wq{l}" in run:
                    block_rows(TICK[f"wq{l}"] // 2, wq[l], cols(0))
                if f"wo{l}" in run:
                    for b in range(4):
                        slab(TICK[f"wo{l}"] // 2 + b, wo[l][:, 0:4, cols(b * NB)])
                if f"up{l}" in run:
                    up(l)
                if f"dn{l}" in run:
                    down(l)

            for b in range(2):
                block_rows(4 * b, wkv[0], cols(b * NB))
            seen = {}
            if "in0" in run:
                for b, name in enumerate(IN0):
                    n = seen.get(name, 0)
                    seen[name] = n + 1
                    block_rows(TICK["in0"] // 2 + 4 * b, w_in0, cols(IN0_COL[name] + n * NB))
            if "out0" in run:
                for b in range(4):
                    block_rows(TICK["out0"] // 2 + 4 * b, w_out[0], cols(b * NB), (2, 3, 0, 1))
            memory(0)
            if "kcvc" in run:
                for b, name in enumerate(("kc", "vc")):
                    block_rows(TICK["kcvc"] // 2 + 4 * b, w_in1, cols(ODD_COL[name]))
            if "cmp" in run:
                for b in range(2):
                    for c in range(4):
                        s = TICK["cmp"] // 2 + 4 * b + c
                        sp.wait_ge(lo_ready, 2 * (s - RAW) + 2)
                        sp.dma_start(raw[:, s % RAW, :, :].rearrange("p a (b m) -> p (a b) m", m=256),
                                     cw1[b][:, 8 * c:8 * c + 8, :]).then_inc(raw_full[s % RAW], 16)
            if "kvs" in run:
                for b, name in enumerate(("kw", "ks", "vw", "vs")):
                    block_rows(TICK["kvs"] // 2 + 4 * b, w_in1, cols(ODD_COL[name]))
            if "q" in run:
                for b in range(4):
                    block_rows(TICK["q"] // 2 + 4 * b, w_in1, cols(b * NB))
            if "kv1" in run:
                for b in range(2):
                    block_rows(TICK["kv1"] // 2 + 4 * b, wkv[1], cols(b * NB))
            if "out1" in run:
                for b in range(4):
                    block_rows(TICK["out1"] // 2 + 4 * b, w_out[1], cols(b * NB))
            memory(1)
            if dbg is not None:
                sp.wait_ge(dbg_done, 1)
                sp.dma_start(dbg.rearrange("(k p) t -> p k t", p=P), xT[:, :, :]).then_inc(out_done, 16)
                sp.wait_ge(out_done, 16)
            if stop is None:
                for b in range(4):
                    sp.wait_ge(out_copied, 2 * b + 2)
                    sp.dma_start(out[0].rearrange("(a p) f -> p a f", p=P)[:, :, cols(b * NB)],
                                 otok[:, :, b * NB:(b + 1) * NB]).then_inc(out_done, 16)
                sp.wait_ge(out_done, 64 + (16 if dbg is not None else 0))

        @block.gpsimd
        def _(pool):
            nc.gpsimd.memset(ident[:, :], 0.0).then_inc(consts, 1)
            nc.gpsimd.memset(ones[:, :], 1.0).then_inc(consts, 1)
            nc.gpsimd.memset(eps[:, 0:1], EPS).then_inc(consts, 1)
            nc.gpsimd.memset(eps[:, 1:2], EPS * HD).then_inc(consts, 1)
            nc.gpsimd.memset(maskf[:, :, :], 0.0).then_inc(consts, 1)
            pool.wait_ge(consts, 5)
            nc.gpsimd.affine_select(out=ident[:, :], in_=ident[:, :], compare_op=ALU.not_equal, fill=1.0,
                                    base=0, pattern=[[-1, P]], channel_multiplier=1).then_inc(consts, 1)
            nc.gpsimd.affine_select(out=maskf[:, 0, :], in_=maskf[:, 0, :], compare_op=ALU.not_equal, fill=1.0,
                                    base=0, pattern=[[-1, P]], channel_multiplier=1).then_inc(consts, 1)
            def right(l):
                return maskf[:, l, :].rearrange("p (n a h) -> p n a h", a=2, h=1 << (l - 1))[:, :, 1, :]

            pool.wait_ge(consts, 7)
            for l in range(1, 8):
                nc.gpsimd.memset(right(l), 1.0).then_inc(consts, 1)
            pool.wait_ge(consts, 14)
            for l in range(1, 8):
                h = 1 << (l - 1)
                nc.gpsimd.affine_select(out=right(l), in_=right(l), compare_op=ALU.is_ge, fill=0.0, base=0,
                                        pattern=[[-2 * h, P // (2 * h)], [0, h]],
                                        channel_multiplier=1).then_inc(consts, 1)
            pool.wait_ge(consts, 21)
            for l in range(1, 8):
                h = 1 << (l - 1)
                nc.gpsimd.affine_select(out=right(l), in_=right(l), compare_op=ALU.is_ge, fill=0.0, base=h - 1,
                                        pattern=[[2 * h, P // (2 * h)], [0, h]],
                                        channel_multiplier=-1).then_inc(consts, 1)
            pool.wait_ge(consts, 28)
            nc.gpsimd.tensor_copy(lmask[:, :, :], maskf[:, :, :]).then_inc(lmask_ready, 1)
            pool.wait_ge(m_turn, 8)
            nc.gpsimd.memset(upper[:, :], 1.0).then_inc(upper_ready, 1)
            pool.wait_ge(upper_ready, 1)
            nc.gpsimd.affine_select(out=upper[:, :], in_=upper[:, :], compare_op=ALU.is_ge, fill=0.0, base=0,
                                    pattern=[[1, P]], channel_multiplier=-1).then_inc(upper_ready, 1)

            if "in0" in run:
                for n in range(4 * LEVELS + 3):
                    p, l = divmod(n, LEVELS)
                    if n < 4 * LEVELS and l > 0:
                        m = p * 8 + l - 1
                        pool.wait_ge(hg_decay, m + 1)
                        if m >= 2:
                            pool.wait_ge(hg_scores, (m - 2) // 8 * 9 + (m - 2) % 8 + 2)
                        nc.gpsimd.tensor_tensor(qd[:, m % 2, :], hq[:, 2 * p:2 * p + 2, :].rearrange("p a t -> p (a t)"),
                                                decay[:, m % 2, :], ALU.mult).then_inc(hg_qd, 1)
                    if n >= LEVELS and (n - 2) % LEVELS == 0:
                        o = (n - 2) // LEVELS - 1
                        pool.wait_ge(hg_onorm, o + 1)
                        pool.wait_ge(hg_gate, o // 2 + 1)
                        nc.gpsimd.tensor_tensor(hq[:, 2 * o:2 * o + 2, :], hq[:, 2 * o:2 * o + 2, :],
                                                hg[:, 2 * o:2 * o + 2, :], ALU.mult).then_inc(hg_out, 1)
                pool.wait_ge(hg_scores, 4 * LEVELS)
                nc.gpsimd.memset(fmask[:, :], 0.0).then_inc(fmask_ready, 1)
                pool.wait_ge(fmask_ready, 1)
                nc.gpsimd.affine_select(out=fmask[:, P:T], in_=fmask[:, P:T], compare_op=ALU.is_ge, fill=NEG,
                                        base=0, pattern=[[-1, P]], channel_multiplier=1).then_inc(fmask_ready, 1)
                for u in range(FOX_HEADS):
                    pool.wait_ge(f_rz, u + 1)
                    nc.gpsimd.tensor_scalar(fp[:, u % 2, 0:P], fp[:, u % 2, 0:P], fst[:, u % 2, 6:7], None,
                                            ALU.mult)
                    nc.gpsimd.tensor_scalar(fp[:, u % 2, P:384], fp[:, u % 2, P:384], fst[:, u % 2, 7:8], None,
                                            ALU.mult).then_inc(f_pn, 1)

            def memory(l):
                for u in range(MEM_HEADS):
                    n = MEM_HEADS * l + u
                    pool.wait_ge(m_rz, n + 1)
                    for a in range(2):
                        last = nc.gpsimd.tensor_scalar(mp[:, u % 2, a, :], mp[:, u % 2, a, :],
                                                       mst[:, u % 2, 6 + a:7 + a], None, ALU.mult)
                    last.then_inc(m_pn, 1)

            def up(l):
                with pool.Fori(0, FB) as i:
                    pool.wait_ge(u_prod, i + FB * l + 1)
                    flat = hid_hi[:, :, :].rearrange("p k t -> p (k t)")
                    flat_lo = hid_lo[:, :, :].rearrange("p k t -> p (k t)")
                    nc.gpsimd.tensor_copy(flat[:, bass.ds(i * 1024, 1024)],
                                          tmp[:, :, :].rearrange("p k t -> p (k t)")).then_inc(u_hi, 1)
                    pool.wait_ge(u_hi, i + FB * l + 1)
                    nc.gpsimd.tensor_tensor(flat_lo[:, bass.ds(i * 1024, 1024)],
                                            tmp[:, :, :].rearrange("p k t -> p (k t)"),
                                            flat[:, bass.ds(i * 1024, 1024)].bitcast(F32),
                                            ALU.subtract).then_inc(u_ready, 1)

            if "wq0" in run:
                memory(0)
            if "up0" in run:
                up(0)
            if "q" in run:
                pool.wait_ge(n_gate, 1)
                nc.gpsimd.iota(dm[:, 0:P], pattern=[[1, P]], base=0, channel_multiplier=-1,
                               allow_small_or_imprecise_dtypes=True).then_inc(n_mask, 1)
                nc.gpsimd.iota(dm[:, P:384], pattern=[[1, T]], base=-P, channel_multiplier=-1,
                               allow_small_or_imprecise_dtypes=True).then_inc(n_mask, 1)
                nc.gpsimd.iota(dmc[:, :, 0:N_CMP], pattern=[[-2 * P, 2], [2 * CMP_S, N_CMP]], base=CMP_L - 1,
                               channel_multiplier=-2, allow_small_or_imprecise_dtypes=True).then_inc(n_mask, 1)
                pool.wait_ge(n_mask, 3)
                nc.gpsimd.affine_select(out=dm[:, 0:P], in_=dm[:, 0:P], compare_op=ALU.is_ge, fill=NEG, base=0,
                                        pattern=[[-1, P]], channel_multiplier=1).then_inc(n_mask, 1)
                nc.gpsimd.affine_select(out=dm[:, P:384], in_=dm[:, P:384], compare_op=ALU.is_ge, fill=NEG,
                                        base=P, pattern=[[-1, T]], channel_multiplier=1).then_inc(n_mask, 1)
                nc.gpsimd.tensor_scalar(dmc[:, :, 0:N_CMP], dmc[:, :, 0:N_CMP], 0.5, None,
                                        ALU.mult).then_inc(n_mask, 1)
                pool.wait_ge(n_mask, 6)
                nc.gpsimd.affine_select(out=dmc[:, :, 0:N_CMP], in_=dmc[:, :, 0:N_CMP], compare_op=ALU.is_ge,
                                        fill=NEG, base=-(CMP_L - 1), pattern=[[P, 2], [-CMP_S, N_CMP]],
                                        channel_multiplier=1).then_inc(n_mask, 1)
                for u in range(NSA_HEADS):
                    pool.wait_ge(n_rz, u + 1)
                    for br in range(2):
                        for a, cs in ((0, slice(0, P)), (1, slice(P, 384))):
                            c = 3 * a + 2 - br
                            nc.gpsimd.tensor_scalar(np_[:, br, cs], np_[:, br, cs], nst[:, 3, c:c + 1], None,
                                                    ALU.mult)
                    for a in range(2):
                        last = nc.gpsimd.tensor_scalar(npc[:, a, 0:N_CMP], npc[:, a, 0:N_CMP],
                                                       nst[:, 3, 3 * a:3 * a + 1], None, ALU.mult)
                    last.then_inc(n_pn, 1)
            if "wq1" in run:
                memory(1)
            if "up1" in run:
                up(1)

        @block.scalar
        def _(act):
            for v, name in enumerate(("norm_mix", "norm_mem", "norm_ffn", "mem_in_gain")):
                act.dma_start(g_rows[32 * v:32 * v + 32, :],
                              A[name].rearrange("l (k p) -> (l k) p", p=P)).then_inc(small_in, 16)
            for row, name in ((S_PEK, "cmp_pe_k"), (S_PEV, "cmp_pe_v"), (S_NK, "nsa_k_gain")):
                act.dma_start(s_rows[row:row + A[name].shape[1], :], A[name][0]).then_inc(small_in, 16)
            for row, name in ((S_FQ, "fox_q_gain"), (S_FK, "fox_k_gain"), (S_HO, "hgrn_o_gain"),
                              (S_NQ, "nsa_q_gain"), (S_MQ, "mem_q_gain"), (S_MK, "mem_k_gain")):
                act.dma_start(s_rows[row:row + A[name].shape[0], :], A[name]).then_inc(small_in, 16)

            def load_mtok(l):
                act.dma_start(mtok[l][:, :, :], A["mem"][0].rearrange("(a p) f -> p a f", p=P)).then_inc(mtok_in, 16)

            load_mtok(0)
            act.dma_start(xtok[:, :, :], A["x"][0].rearrange("(a p) f -> p a f", p=P)).then_inc(xtok_in, 16)

            def split(p, more=0):
                if isinstance(more, int) and p >= last_tick:
                    return
                if p % 2 == 0:
                    act.wait_ge(raw_full[p // 2 % RAW], 16 * (p // 2 // RAW + 1) + more * 2)
                if p >= LEAD:
                    act.wait_ge(pieces_done, p - LEAD + 1 + more)
                nc.scalar.activation(w_hi[:, p % LEAD, :, :], raw[:, p // 2 % RAW, 2 * (p % 2):2 * (p % 2) + 2, :],
                                     ACT.Copy).then_inc(hi_ready, 1)

            TMP_FREE = {1: (hg_osum, 4), 2: (hn_sum, 6), 3: (u_ready, FB), 4: (hn_sum, 13), 5: (hn_sum, 14)}

            def square(n, c):
                act.wait_ge(x_ready, 4 * n + c // 2 + 1)
                if c == 0 and n in TMP_FREE:
                    act.wait_ge(*TMP_FREE[n])
                if 8 * n + c >= 2:
                    act.wait_ge(sq_used, 8 * n + c - 1)
                nc.scalar.activation(tmp[:, 2 * (c % 2):2 * (c % 2) + 2, :], xT[:, 2 * c:2 * c + 2, :],
                                     ACT.Square).then_inc(sq_ready, 1)

            def rms(n):
                act.wait_ge(sq_used, 8 * n + 8)
                if n:
                    act.wait_ge(h_tmp, 8 * n)
                nc.scalar.activation(rinv[:, :], att[:, 3, 0:T], ACT.Sqrt, bias=eps[:, 0:1],
                                     scale=1.0 / D).then_inc(rms_ready, 1)

            def h_high(f, c, n):
                act.wait_ge(h_tmp, 8 * n + c + 1)
                nc.scalar.activation(h_hi[:, 2 * c:2 * c + 2, :], tmp[:, 2 * (c % 2):2 * (c % 2) + 2, :],
                                     ACT.Copy).then_inc(h_hi_ready, 1)

            def whole_norm(n, f):
                for c in range(8):
                    square(n, c)
                rms(n)
                for c in range(8):
                    h_high(f, c, n)

            def hn_square(i, src):
                act.wait_ge(hn_raw, i + 1)
                if i:
                    act.wait_ge(hn_sum, i)
                nc.scalar.activation(tmp[:, :, :], src, ACT.Square).then_inc(hn_sq, 1)

            def hn_root(i, b, query):
                act.wait_ge(hn_sum, i + 1)
                nc.scalar.activation(acc[:, b % 2, :], acc[:, b % 2, :], ACT.Sqrt,
                                     bias=eps[:, 1:2] if query else eps[:, 0:1],
                                     scale=1.0 if query else 1.0 / HD).then_inc(hn_rms, 1)

            def mem_norm(l):
                act.wait_ge(mtok_in, 16 * (l + 1))
                for a in range(2):
                    nc.scalar.activation(att[:, :, :].rearrange("p a n -> p (a n)"), mtok[l][:, a, :],
                                         ACT.Square, accum_out=mss[:, a:a + 1]).then_inc(m_ssq, 1)
                    act.wait_ge(m_ssq, 2 * l + a + 1)
                nc.scalar.activation(mss[:, 2:4], mss[:, 0:2], ACT.Sqrt, bias=eps[:, 0:1],
                                     scale=1.0 / D).then_inc(m_rms, 1)

            def mem_high(l, c):
                act.wait_ge(m_turn, 8 * l + c + 1)
                for k in range(2):
                    g = G_IN + KT * l + 2 * c + k
                    last = nc.scalar.activation(memn[l][0][:, 2 * c + k, :], att[:, c % 4, k * T:(k + 1) * T],
                                                ACT.Copy, scale=G[:, g:g + 1])
                last.then_inc(m_hi, 1)

            for p in range(LEAD):
                split(p)
            act.wait_ge(consts, 7)
            act.wait_ge(gains, 2)
            mem_norm(0)
            for c in range(8):
                mem_high(0, c)
            act.wait_ge(m_turn, 8)
            act.dma_start(wff[:, :, :], w_in0[:, :, FF_COL:FF_COL + 8]).then_inc(ff_w, 16)
            act.dma_start(fbias[0:1, :], A["fox_f_bias"]).then_inc(ff_w, 16)
            t = 0
            for t in range(16):
                if t < 4:
                    square(0, 2 * t)
                    square(0, 2 * t + 1)
                if t == 4:
                    rms(0)
                if 5 <= t < 7:
                    for c in range(4 * (t - 5), 4 * (t - 5) + 4):
                        h_high(0, c, 0)
                if t == 8:
                    act.wait_ge(h_ready, 8)
                    hn_square(0, mk[:, :, :])
                if t == 10:
                    hn_root(0, 0, False)
                split(t + LEAD)

            if "in0" in run:
                T0 = TICK["in0"]
                act.wait_ge(ff_w, 32)
                nc.scalar.activation(wff_hi[:, :, :], wff[:, :, :], ACT.Copy).then_inc(ff_whi, 1)

                def level(u):
                    n, r = divmod(u, 2)
                    p, l = divmod(n, LEVELS)
                    if r == 0 and n < 4 * LEVELS and l > 0:
                        m = p * 8 + l - 1
                        act.wait_ge(hg_diff, m + 1)
                        nc.scalar.activation(decay[:, m % 2, :], decay[:, m % 2, :], ACT.Exp).then_inc(hg_decay, 1)
                    if r == 1 and n >= LEVELS and n % LEVELS == 0:
                        o = n // LEVELS - 1
                        act.wait_ge(hg_oraw, o + 1)
                        act.wait_ge(hn_sum, (1, 2, 4, 5)[o])
                        nc.scalar.activation(tmp[:, 0:2, :], hq[:, 2 * o:2 * o + 2, :], ACT.Square).then_inc(hg_osq, 1)
                    if r == 1 and n >= LEVELS and n % LEVELS == 1:
                        o = n // LEVELS - 1
                        act.wait_ge(hg_osum, o + 1)
                        nc.scalar.activation(att[:, 3, :], att[:, 3, :], ACT.Sqrt, bias=eps[:, 0:1],
                                             scale=1.0 / HD).then_inc(hg_orms, 1)

                for b, name in enumerate(IN0):
                    for j in range(8):
                        t = T0 + 8 * b + j
                        done = IN0[b - 1] if b else None
                        k = b - 1 - IN0.index(done) if b else 0
                        if j == 7 and name in ("hq", "hg"):
                            k = b - IN0.index(name)
                            act.wait_ge(pieces_done, t + 1)
                            dst, ready = (hq, hg_q) if name == "hq" else (hg, hg_gate)
                            nc.scalar.activation(dst[:, 4 * k:4 * k + 4, :].rearrange("p a t -> p (a t)"),
                                                 acc[:, (b + 2) % 2, :], ACT.Silu).then_inc(ready, 1)
                        if j == 0 and done == "hf":
                            v = hb[:, 4 * k:4 * k + 4, :]
                            act.wait_ge(hg_z, k + 1)
                            nc.scalar.activation(v, hz[:, 4 * k:4 * k + 4, :], ACT.Abs).then_inc(hg_abs, 1)
                            act.wait_ge(hg_abs, 3 * k + 1)
                            nc.scalar.activation(v, v, ACT.Exp, scale=-1.0).then_inc(hg_abs, 1)
                            act.wait_ge(hg_abs, 3 * k + 2)
                            nc.scalar.activation(v, v, ACT.Ln, bias=1.0).then_inc(hg_abs, 1)
                        if j == 2 and done == "hf":
                            act.wait_ge(hg_kin, k + 1)
                            nc.scalar.activation(hz[:, 4 * k:4 * k + 4, :], hz[:, 4 * k:4 * k + 4, :],
                                                 ACT.Exp).then_inc(hg_k, 1)
                        if b == 2 and j == 0:
                            act.wait_ge(ff_z, 1)
                            nc.scalar.activation(lf[:, 1, :], lf[:, 0, :], ACT.Abs).then_inc(ff_l, 1)
                            act.wait_ge(ff_l, 1)
                            nc.scalar.activation(lf[:, 1, :], lf[:, 1, :], ACT.Exp, scale=-1.0).then_inc(ff_l, 1)
                            act.wait_ge(ff_l, 2)
                            nc.scalar.activation(lf[:, 1, :], lf[:, 1, :], ACT.Ln, bias=1.0).then_inc(ff_l, 1)
                        if done in ("fq", "fk"):
                            dst = fq if done == "fq" else fk
                            if j == 0:
                                act.wait_ge(hg_osum, {"fq0": 1, "fq1": 2, "fk0": 2, "fk1": 3}[done + str(k)])
                                hn_square(HN[done + str(k)], dst[:, 4 * k:4 * k + 4, :])
                            if j == 2:
                                hn_root(HN[done + str(k)], b + 1, done == "fq")
                        if 8 * b + j >= HG_START:
                            level(8 * b + j - HG_START)
                        split(t + LEAD)
                for u in range(112 - HG_START, HG_TICKS):
                    level(u)

            if "out0" in run:
                def fox_exp(u):
                    act.wait_ge(f_nmax, u + 1)
                    for a, cs in ((0, slice(0, P)), (1, slice(P, 384))):
                        last = nc.scalar.activation(fp[:, u % 2, cs], fp[:, u % 2, cs], ACT.Exp,
                                                    bias=fst[:, u % 2, 2 + a:3 + a],
                                                    accum_out=fst[:, u % 2, 4 + a:5 + a])
                    last.then_inc(f_exp, 1)

                def fox_pt(u):
                    act.wait_ge(f_t, u + 1)
                    if u >= 2:
                        act.wait_ge(f_o, u - 1)
                    nc.scalar.activation(fpt[:, u % 2, :], att[:, 2, 0:384], ACT.Copy).then_inc(f_pt, 1)

                for u in range(FOX_HEADS + 1):
                    if u < FOX_HEADS:
                        fox_exp(u)
                    if u >= 1:
                        fox_pt(u - 1)
                    if u % 2 == 0 and u < FOX_HEADS:
                        c = 4 + u // 2
                        act.wait_ge(hg_out, u // 2 + 1)
                        act.wait_ge(pieces_done, LAST_READ[1])
                        nc.scalar.activation(h_hi[:, 2 * c:2 * c + 2, :], hq[:, 2 * c - 8:2 * c - 6, :],
                                             ACT.Copy).then_inc(h_hi_ready, 1)
                for c in range(4):
                    act.wait_ge(f_out, 2 * c + 2)
                    nc.scalar.activation(h_hi[:, 2 * c:2 * c + 2, :], fq[:, 2 * c:2 * c + 2, :],
                                         ACT.Copy).then_inc(h_hi_ready, 1)

            def memory(l):
                n0 = 3 * l
                t0 = TICK[f"out{l}"]
                for t in range(32):
                    if t % 8 == 0 and t:
                        square(n0 + 1, t // 4 - 2)
                        square(n0 + 1, t // 4 - 1)
                    split(t0 + t + LEAD)
                square(n0 + 1, 6)
                square(n0 + 1, 7)
                rms(n0 + 1)
                for c in range(8):
                    h_high(FILL[f"wq{l}"], c, n0 + 1)
                if f"wq{l}" not in run:
                    return
                t0 = TICK[f"wq{l}"]
                for t in range(8):
                    split(t0 + t + LEAD)
                act.wait_ge(h_ready, 8 * FILL[f"wq{l}"] + 8)
                hn_square(HN[f"mq{l}"], mq[:, :, :])
                hn_root(HN[f"mq{l}"], BLOCK[f"wq{l}"], True)

                def m_exps(u):
                    act.wait_ge(m_nmax, MEM_HEADS * l + u + 1)
                    for a in range(2):
                        last = nc.scalar.activation(mp[:, u % 2, a, :], mp[:, u % 2, a, :], ACT.Exp,
                                                    bias=mst[:, u % 2, 2 + a:3 + a],
                                                    accum_out=mst[:, u % 2, 4 + a:5 + a])
                    last.then_inc(m_exp, 1)

                def m_turned(u):
                    n = MEM_HEADS * l + u
                    act.wait_ge(m_t, n + 1)
                    if u >= 2:
                        act.wait_ge(m_o, n - 1)
                    nc.scalar.activation(mpt[:, u % 2, :, :], att[:, 2, :].rearrange("p (a q) -> p a q", a=2),
                                         ACT.Copy).then_inc(m_pt, 1)

                def m_high(u):
                    n = MEM_HEADS * l + u
                    act.wait_ge(m_o, n + 1)
                    nc.scalar.activation(mo_hi[:, u, :], att[:, 3, 0:T], ACT.Copy).then_inc(m_ohi, 1)

                for u in range(MEM_HEADS + 2):
                    if u < MEM_HEADS:
                        m_exps(u)
                    if 1 <= u <= MEM_HEADS:
                        m_turned(u - 1)
                    if u >= 2:
                        m_high(u - 2)
                t0 = TICK[f"wo{l}"]
                for t in range(8):
                    if t % 2 == 0 and t:
                        square(n0 + 2, t - 2)
                        square(n0 + 2, t - 1)
                    split(t0 + t + LEAD)
                square(n0 + 2, 6)
                square(n0 + 2, 7)
                rms(n0 + 2)
                for c in range(8):
                    h_high(FILL[f"up{l}"], c, n0 + 2)
                if f"up{l}" not in run:
                    return
                t0 = TICK[f"up{l}"]
                b0 = BLOCK[f"up{l}"]
                act.wait_ge(h_ready, 8 * FILL[f"up{l}"] + 8)

                def silu(more):
                    act.wait_ge(pieces_done, t0 + 8 + more * 16)
                    if l or not isinstance(more, int):
                        act.wait_ge(u_ready, FB * l + more)
                    nc.scalar.activation(tmp[:, :, :].rearrange("p k t -> p (k t)"), acc[:, b0 % 2, :],
                                         ACT.Silu).then_inc(u_silu, 1)

                for t in range(16):
                    if t == 7:
                        silu(0)
                    split(t0 + t + LEAD)
                with act.Fori(1, FB) as i:
                    for t in range(16):
                        if t == 7:
                            silu(i)
                        split(t0 + t + LEAD, i * 16)
                if f"dn{l}" not in run:
                    return
                for half in range(2):
                    t0 = TICK[f"dn{l}"] + 44 * half
                    for t in range(4):
                        if l == 0 and half and t % 2 == 0:
                            square(3, t)
                            square(3, t + 1)
                        split(t0 + t + LEAD)
                    with act.Fori(0, 4) as i:
                        for t in range(8):
                            split(t0 + 4 + t + LEAD, i * 8)
                    for t in range(8):
                        split(t0 + 36 + t + LEAD)
                    if l == 0 and half:
                        for c in range(4, 8):
                            square(3, c)

            if "out0" in run:
                memory(0)
            if "kcvc" in run:
                rms(3)
                for c in range(8):
                    h_high(4, c, 3)
                act.wait_ge(pieces_done, TICK["kcvc"])
                load_mtok(1)
                act.dma_start(w2c[:, 0, :, :], A["cmp_w2_k"][0].rearrange("(a p) d -> p a d", p=P)).then_inc(c_w2, 16)
                act.dma_start(w2c[:, 1, :, :], A["cmp_w2_v"][0].rearrange("(a p) d -> p a d", p=P)).then_inc(c_w2, 16)
                act.dma_start(wgt[:, :, :], w_in1[:, :, GT_COL:GT_COL + 48]).then_inc(n_w, 16)
                for t in range(16):
                    split(TICK["kcvc"] + t + LEAD)
                act.wait_ge(n_w, 16)
                nc.scalar.activation(wgt_hi[:, :, :], wgt[:, :, :], ACT.Copy).then_inc(n_whi, 1)
                act.wait_ge(n_gsum, 1)
                nc.scalar.activation(gate[:, :, :].rearrange("p a n -> p (a n)"), att[:, 0, 0:96],
                                     ACT.Sigmoid).then_inc(n_gate, 1)
            if "cmp" in run:
                for v in range(2):
                    act.wait_ge(c_x, v + 1)
                    nc.scalar.activation(xc_hi[v][:, :, 0:CMP_COLS], xc[:, :, 0:CMP_COLS], ACT.Copy).then_inc(c_hi, 1)
                for t in range(16):
                    if t % 8 == 7:
                        b = BLOCK["cmp"] + t // 8
                        act.wait_ge(pieces_done, TICK["cmp"] + t + 1)
                        nc.scalar.activation(hidc[:, t // 8, :, 0:CMP_COLS],
                                             acc[:, b % 2, 0:128].rearrange("p (a n) -> p a n", a=2)[:, :, 0:CMP_COLS],
                                             ACT.Gelu_apprx_tanh).then_inc(c_hid, 1)
                    split(TICK["cmp"] + t + LEAD)
                act.wait_ge(c_kraw, 1)
                nc.scalar.activation(kcr[:, 0:CMP_COLS], kcmp[:, 0:CMP_COLS], ACT.Square).then_inc(c_ksq, 1)
                act.wait_ge(c_ksum, 2)
                nc.scalar.activation(kcr[:, 0:CMP_COLS], att[:, 2, 0:CMP_COLS], ACT.Sqrt, bias=eps[:, 0:1],
                                     scale=1.0 / HD).then_inc(c_krms, 1)
                act.wait_ge(c_vout, 1)
                mem_norm(1)
            if "kvs" in run:
                act.wait_ge(h_ready, 8 * 4 + 8)
                for t in range(32):
                    b = BLOCK["kvs"] + t // 8 - 1
                    if 1 <= t < 9:
                        mem_high(1, t - 1)
                    for k, name, dst in ((1, "kw", kw), (2, "ks", ks)):
                        if t == 8 * k:
                            hn_square(HN[name], dst[:, :, :])
                        if t == 8 * k + 2:
                            hn_root(HN[name], b, False)
                    split(TICK["kvs"] + t + LEAD)

            def nsa_exp(u):
                act.wait_ge(n_nmax, u + 1)
                for a, cs in ((0, slice(0, P)), (1, slice(P, 384))):
                    for br in range(2):
                        c = 3 * a + 2 - br
                        nc.scalar.activation(np_[:, br, cs], np_[:, br, cs], ACT.Exp, bias=nst[:, 1, c:c + 1],
                                             accum_out=nst[:, 2, c:c + 1])
                    last = nc.scalar.activation(npc[:, a, 0:N_CMP], npc[:, a, 0:N_CMP], ACT.Exp,
                                                bias=nst[:, 1, 3 * a:3 * a + 1],
                                                accum_out=nst[:, 2, 3 * a:3 * a + 1])
                last.then_inc(n_exp, 1)

            def nsa_pt(u, br):
                act.wait_ge(n_t, 2 * u + br + 1)
                if u:
                    act.wait_ge(n_o, u)
                nc.scalar.activation(npt[:, br, :], att[:, 2, 0:384], ACT.Copy).then_inc(n_pt, 1)

            def nsa(v):
                u, r = divmod(v, 3)
                if r == 0 and u:
                    nsa_pt(u - 1, 1)
                if u < NSA_HEADS:
                    if r == 0:
                        nsa_exp(u)
                    if r == 2:
                        nsa_pt(u, 0)

            if "q" in run:
                for t in range(48):
                    if t % 8 == 0 and 8 <= t <= 32:
                        hn_square(HN[f"q{t // 8 - 1}"], nq[:, t // 2 - 4:t // 2, :])
                    if t % 8 == 2 and 8 <= t <= 36:
                        hn_root(HN[f"q{t // 8 - 1}"], BLOCK["q"] + t // 8 - 1, True)
                    if t == 40:
                        hn_square(HN["mk1"], mk[:, :, :])
                    if t == 42:
                        hn_root(HN["mk1"], BLOCK["kv1"], False)
                    if t >= NSA_START:
                        nsa(t - NSA_START)
                    if TICK["q"] + t + LEAD < last_tick:
                        split(TICK["q"] + t + LEAD)
                for v in range(48 - NSA_START, 3 * NSA_HEADS + 3):
                    nsa(v)
            if "out1" in run:
                for c in range(8):
                    act.wait_ge(n_out, 2 * c + 2)
                    nc.scalar.activation(h_hi[:, 2 * c:2 * c + 2, :], nq[:, 2 * c:2 * c + 2, :],
                                         ACT.Copy).then_inc(h_hi_ready, 1)
                memory(1)
            if stop is None:
                for g in range(8):
                    act.wait_ge(out_turn, g + 1)
                    b, a = divmod(g, 2)
                    nc.scalar.activation(otok[:, a, b * NB:(b + 1) * NB], att[:, g % 4, :],
                                         ACT.Copy).then_inc(out_copied, 1)

        @block.vector
        def _(dve):
            def split(p, more=0):
                if isinstance(more, int) and p >= last_tick:
                    return
                dve.wait_ge(hi_ready, p + 1 + more)
                nc.vector.tensor_tensor(w_lo[:, p % LEAD, :, :],
                                        raw[:, p // 2 % RAW, 2 * (p % 2):2 * (p % 2) + 2, :],
                                        w_hi[:, p % LEAD, :, :].bitcast(F32), ALU.subtract).then_inc(lo_ready, 1)

            def invert(n):
                dve.wait_ge(rms_ready, n + 1)
                nc.vector.reciprocal(rinv[:, :], rinv[:, :]).then_inc(rinv_ready, 1)
                dve.wait_ge(rinv_ready, n + 1)

            def h_scaled(n, c, gain):
                for k in range(2):
                    kt = 2 * c + k
                    last = nc.vector.scalar_tensor_tensor(out=tmp[:, 2 * (c % 2) + k, :], in0=xT[:, kt, :],
                                                          scalar=G[:, gain + kt:gain + kt + 1], in1=rinv[:, :],
                                                          op0=ALU.mult, op1=ALU.mult)
                last.then_inc(h_tmp, 1)

            def h_low(f, c, src):
                dve.wait_ge(h_hi_ready, 8 * f + FILL_ORDER[f].index(c) + 1)
                nc.vector.tensor_tensor(h_lo[:, 2 * c:2 * c + 2, :], src, h_hi[:, 2 * c:2 * c + 2, :].bitcast(F32),
                                        ALU.subtract).then_inc(h_ready, 1)

            def norm(n, f, gain, lo=0, hi=8):
                if lo == 0:
                    invert(n)
                    if LAST_READ[f]:
                        dve.wait_ge(pieces_done, LAST_READ[f])
                for c in range(lo, hi + (hi == 8)):
                    if c < 8:
                        if c >= 2:
                            dve.wait_ge(h_ready, 8 * f + c - 1)
                        h_scaled(n, c, gain)
                    if c:
                        h_low(f, c - 1, tmp[:, 2 * ((c - 1) % 2):2 * ((c - 1) % 2) + 2, :])

            def hn_take(i, b, dst, last_t):
                dve.wait_ge(pieces_done, last_t + 1)
                nc.vector.tensor_copy(dst.rearrange("p a t -> p (a t)"), acc[:, b % 2, :]).then_inc(hn_raw, 1)

            def hn_scale(i, b, dst, gain):
                dve.wait_ge(hn_rms, i + 1)
                nc.vector.reciprocal(acc[:, b % 2, :], acc[:, b % 2, :]).then_inc(hn_rinv, 1)
                dve.wait_ge(hn_rinv, i + 1)
                nc.vector.scalar_tensor_tensor(out=dst.rearrange("p a t -> p (a t)"),
                                               in0=dst.rearrange("p a t -> p (a t)"), scalar=S[:, gain:gain + 1],
                                               in1=acc[:, b % 2, :], op0=ALU.mult,
                                               op1=ALU.mult).then_inc(hn_out, 1)

            def mem_scale(l):
                dve.wait_ge(m_rms, l + 1)
                nc.vector.reciprocal(mss[:, 2:4], mss[:, 2:4]).then_inc(m_rinv, 1)
                dve.wait_ge(m_rinv, l + 1)
                for a in range(2):
                    nc.vector.tensor_scalar(mtok[l][:, a, :], mtok[l][:, a, :], mss[:, 2 + a:3 + a], None,
                                            ALU.mult).then_inc(m_scaled, 1)

            def mem_low(l, c):
                dve.wait_ge(m_hi, 8 * l + c + 1)
                for k in range(2):
                    g = G_IN + KT * l + 2 * c + k
                    last = nc.vector.scalar_tensor_tensor(out=memn[l][1][:, 2 * c + k, :],
                                                          in0=att[:, c % 4, k * T:(k + 1) * T],
                                                          scalar=G[:, g:g + 1],
                                                          in1=memn[l][0][:, 2 * c + k, :].bitcast(F32),
                                                          op0=ALU.mult, op1=ALU.subtract)
                last.then_inc(m_ready, 1)

            dve.wait_ge(gains_t, 2)
            nc.vector.tensor_copy(G[:, :], att[:, 0, 0:P]).then_inc(gains, 1)
            nc.vector.tensor_copy(S[:, :], att[:, 1, 0:S_ROWS]).then_inc(gains, 1)
            for p in range(LEAD):
                split(p)
            dve.wait_ge(gains, 2)
            mem_scale(0)
            for c in range(8):
                mem_low(0, c)
            for c in range(8):
                dve.wait_ge(x_turn, c + 1)
                last = nc.vector.tensor_copy(xT[:, 2 * c:2 * c + 2, :], att[:, c % 4, :].rearrange("p (k t) -> p k t", k=2))
                last.then_inc(x_copied, 1)
                if c % 2:
                    dve.wait_ge(x_copied, c + 1)
                    dve.sem_inc(x_ready, 1)
            nc.vector.memset(AT[:, :, :], 0.0).then_inc(hg_zero, 1)
            for t in range(16):
                if t == 5:
                    norm(0, 0, G_MIX)
                if t == 7:
                    hn_take(0, 0, mk[:, :, :], 7)
                if t == 11:
                    hn_scale(0, 0, mk[:, :, :], S_MK)
                    dve.wait_ge(hn_out, 1)
                    dve.sem_inc(acc_free[0], 1)
                if t == 15:
                    dve.wait_ge(pieces_done, 16)
                    nc.vector.tensor_copy(mv[:, :, :], acc[:, 1, :].rearrange("p (a n) -> p a n", a=2)).then_inc(m_v, 1)
                    dve.wait_ge(m_v, 1)
                    dve.sem_inc(acc_free[1], 1)
                split(t + LEAD)

            if "in0" in run:
                T0 = TICK["in0"]
                dve.wait_ge(ff_whi, 1)
                nc.vector.tensor_tensor(wff_lo[:, :, :], wff[:, :, :], wff_hi[:, :, :].bitcast(F32),
                                        ALU.subtract).then_inc(ff_wlo, 1)

                def heads(x, p):
                    return x[:, 2 * p:2 * p + 2, :].rearrange("p a t -> p (a t)")

                def level(u):
                    n, r = divmod(u, 2)
                    if r == 0 and 1 <= n <= 4 * LEVELS:
                        p, l = divmod(n - 1, LEVELS)
                        dve.wait_ge(hg_scores, n)
                        if l == 0:
                            dve.wait_ge(lmask_ready, 1)
                            dve.wait_ge(hg_zero, 1)
                            if p:
                                dve.wait_ge(hg_o, p)
                        else:
                            dve.wait_ge(hg_merged, n - 1)
                        if l < 8:
                            last = nc.vector.copy_predicated(AT[:, 0:4, :], lmask[:, l:l + 1, :].broadcast_to([P, 4, P]),
                                                             att[:, (n - 1) % 2, :].rearrange("p (a t) -> p a t", a=4))
                        else:
                            last = nc.vector.tensor_copy(AT[:, 4:6, :], att[:, (n - 1) % 2, 0:T].rearrange("p (a t) -> p a t", a=2))
                        last.then_inc(hg_merged, 1)
                    p, l = divmod(n, LEVELS)
                    m = p * 8 + l - 1
                    if r == 0 and n < 4 * LEVELS and l > 0:
                        dve.wait_ge(hg_b, p // 2 + 1)
                        if m >= 2:
                            dve.wait_ge(hg_qd, m - 1)
                            dve.wait_ge(hg_kd, m - 1)
                        e = decay[:, m % 2, :]
                        b = heads(hb, p)
                        if l < 8:
                            h = 1 << (l - 1)
                            ev = e.rearrange("p (n a h) -> p n a h", a=2, h=h)
                            bv = b.rearrange("p (n a h) -> p n a h", a=2, h=h)
                            mid = bv[:, :, 0, h - 1:h].broadcast_to([P, T // h, h])
                            nc.vector.tensor_tensor(ev[:, :, 0, :], mid, bv[:, :, 0, :], ALU.subtract)
                            last = nc.vector.tensor_tensor(ev[:, :, 1, :], bv[:, :, 1, :], mid, ALU.subtract)
                        else:
                            ev = e.rearrange("p (n a h) -> p n a h", a=2, h=P)
                            bv = b.rearrange("p (n a h) -> p n a h", a=2, h=P)
                            mid = bv[:, :, 0, P - 1:P].broadcast_to([P, 2, P])
                            nc.vector.tensor_tensor(ev[:, :, 0, :], mid, bv[:, :, 0, :], ALU.subtract)
                            last = nc.vector.tensor_copy(ev[:, :, 1, :], bv[:, :, 1, :])
                        last.then_inc(hg_diff, 1)
                    if r == 1 and n < 4 * LEVELS and l > 0:
                        dve.wait_ge(hg_decay, m + 1)
                        if m >= 2:
                            dve.wait_ge(hg_scores, (m - 2) // 8 * 9 + (m - 2) % 8 + 2)
                        nc.vector.tensor_tensor(kd[:, m % 2, :], heads(hz, p), decay[:, m % 2, :],
                                                ALU.mult).then_inc(hg_kd, 1)
                    if r == 1 and n >= LEVELS and n % LEVELS == 0:
                        o = n // LEVELS - 1
                        dve.wait_ge(hg_o, o + 1)
                        nc.vector.tensor_copy(heads(hq, o), att[:, 2, :]).then_inc(hg_oraw, 1)
                    if r == 0 and n >= LEVELS and n % LEVELS == 2:
                        o = n // LEVELS - 1
                        dve.wait_ge(hg_orms, o + 1)
                        nc.vector.reciprocal(att[:, 3, :], att[:, 3, :]).then_inc(hg_orinv, 1)
                        dve.wait_ge(hg_orinv, o + 1)
                        dve.wait_ge(hg_oraw, o + 1)
                        nc.vector.scalar_tensor_tensor(out=heads(hq, o), in0=heads(hq, o), scalar=S[:, S_HO:S_HO + 1],
                                                       in1=att[:, 3, :], op0=ALU.mult, op1=ALU.mult).then_inc(hg_onorm, 1)

                for b, name in enumerate(IN0):
                    for j in range(8):
                        t = T0 + 8 * b + j
                        par = b % 2
                        done = IN0[b - 1] if b else None
                        k = b - 1 - IN0.index(done) if b else 0
                        kk = b - IN0.index(name)
                        if j == 7:
                            if name in ("fq", "fk"):
                                hn_take(HN[name + str(kk)], b, (fq if name == "fq" else fk)[:, 4 * kk:4 * kk + 4, :], t)
                            if name in ("hf", "hi", "fv"):
                                dve.wait_ge(pieces_done, t + 1)
                                if name == "hf":
                                    last = nc.vector.tensor_copy(hz[:, 4 * kk:4 * kk + 4, :].rearrange("p a t -> p (a t)"),
                                                                 acc[:, par, :])
                                    ready = hg_z
                                else:
                                    dst, ready = (hv, hg_v) if name == "hi" else (fv, f_v)
                                    last = nc.vector.tensor_copy(dst[:, :, kk * NB:(kk + 1) * NB],
                                                                 acc[:, par, :].rearrange("p (a n) -> p a n", a=2))
                                last.then_inc(ready, 1)
                                dve.wait_ge(ready, kk + 1)
                                dve.sem_inc(acc_free[par], 1)
                            if name in ("hq", "hg"):
                                dve.wait_ge(hg_q if name == "hq" else hg_gate, kk + 1)
                                dve.sem_inc(acc_free[par], 1)
                        if j == 1 and done == "hf":
                            v = hb[:, 4 * k:4 * k + 4, :]
                            z = hz[:, 4 * k:4 * k + 4, :]
                            dve.wait_ge(hg_abs, 3 * k + 3)
                            nc.vector.scalar_tensor_tensor(out=v, in0=z, scalar=0.0, in1=v, op0=ALU.min,
                                                           op1=ALU.subtract).then_inc(hg_lf, 1)
                            dve.wait_ge(hg_lf, k + 1)
                            nc.vector.tensor_tensor(z, v, z, ALU.subtract).then_inc(hg_kin, 1)
                            dve.wait_ge(hg_kin, k + 1)
                            for i in range(8):
                                bl = hb[:, 4 * k + i // 2, i % 2 * P:(i % 2 + 1) * P]
                                last = nc.vector.tensor_tensor_scan(bl, ones[:, :], bl, 0.0, ALU.mult, ALU.add)
                            last.then_inc(hg_b, 1)
                        if b == 1 and j == 7:
                            dve.wait_ge(ff_sum, 1)
                            nc.vector.tensor_copy(lf[:, 0, :], att[:, 0, 0:16]).then_inc(ff_z, 1)
                        if b == 2 and j == 1:
                            dve.wait_ge(ff_l, 3)
                            nc.vector.scalar_tensor_tensor(out=lf[:, 2, :], in0=lf[:, 0, :], scalar=0.0,
                                                           in1=lf[:, 1, :], op0=ALU.min,
                                                           op1=ALU.subtract).then_inc(ff_lf, 1)
                        if b == 3 and j == 0:
                            dve.wait_ge(ff_c, 1)
                            nc.vector.tensor_scalar(cneg[:, :], att[0:FOX_HEADS, 1, 0:T], -1.0, None,
                                                    ALU.mult).then_inc(ff_cneg, 1)
                        if done in ("fq", "fk") and j == 3:
                            hn_scale(HN[done + str(k)], b - 1, (fq if done == "fq" else fk)[:, 4 * k:4 * k + 4, :],
                                     S_FQ if done == "fq" else S_FK)
                            dve.wait_ge(hn_out, HN[done + str(k)] + 1)
                            dve.sem_inc(acc_free[(b - 1) % 2], 1)
                        if 8 * b + j >= HG_START:
                            level(8 * b + j - HG_START)
                        split(t + LEAD)
                for u in range(112 - HG_START, HG_TICKS):
                    level(u)

            if "out0" in run:
                def fox_max(u):
                    dve.wait_ge(f_s, u + 1)
                    if u >= 2:
                        dve.wait_ge(f_t, u - 1)
                        dve.wait_ge(f_nmax, u - 1)
                    st = fst[:, u % 2, :]
                    for a, w, cs in ((0, P, slice(0, P)), (1, T, slice(P, 384))):
                        last = nc.vector.tensor_tensor_reduce(fp[:, u % 2, cs], att[:, u % 2, cs],
                                                              fmask[:, T - w:T], 1.0, NEG, ALU.add, ALU.max,
                                                              st[:, a:a + 1])
                    last.then_inc(f_max, 1)
                    dve.wait_ge(f_max, u + 1)
                    nc.vector.tensor_scalar(st[:, 2:4], st[:, 0:2], -1.0, None, ALU.mult).then_inc(f_nmax, 1)

                def fox_rz(u):
                    dve.wait_ge(f_exp, u + 1)
                    nc.vector.reciprocal(fst[:, u % 2, 6:8], fst[:, u % 2, 4:6]).then_inc(f_rz, 1)

                def fox_take(u):
                    dve.wait_ge(f_o, u + 1)
                    nc.vector.tensor_copy(fq[:, u, :], att[:, 3, 0:T]).then_inc(f_out, 1)

                dve.wait_ge(fmask_ready, 2)
                for u in range(FOX_HEADS + 2):
                    if u < FOX_HEADS:
                        fox_max(u)
                    if 1 <= u <= FOX_HEADS:
                        fox_rz(u - 1)
                    if u >= 2:
                        fox_take(u - 2)
                    if u % 2 == 1 and u < FOX_HEADS:
                        c = 4 + u // 2
                        h_low(1, c, hq[:, 2 * c - 8:2 * c - 6, :])
                for c in range(4):
                    dve.wait_ge(f_out, 2 * c + 2)
                    h_low(1, c, fq[:, 2 * c:2 * c + 2, :])

            def residual(k, b, last_t):
                dve.wait_ge(pieces_done, last_t + 1)
                v = xT[:, 4 * k:4 * k + 4, :].rearrange("p a t -> p (a t)")
                nc.vector.tensor_tensor(v, v, acc[:, b % 2, :], ALU.add).then_inc(x_ready, 1)

            def freed(b, ready, count):
                dve.wait_ge(ready, count)
                dve.sem_inc(acc_free[b % 2], 1)

            def memory(l):
                n0 = 3 * l
                for t in range(32):
                    if t % 8 == 7:
                        b = BLOCK[f"out{l}"] + t // 8
                        residual(t // 8, b, TICK[f"out{l}"] + t)
                        freed(b, x_ready, 4 * (n0 + 1) + t // 8 + 1)
                    split(TICK[f"out{l}"] + t + LEAD)
                norm(n0 + 1, FILL[f"wq{l}"], G_MEM + KT * l)
                if f"wq{l}" not in run:
                    return
                for t in range(8):
                    if t == 7:
                        hn_take(HN[f"mq{l}"], BLOCK[f"wq{l}"], mq[:, :, :], TICK[f"wq{l}"] + 7)
                    split(TICK[f"wq{l}"] + t + LEAD)
                hn_scale(HN[f"mq{l}"], BLOCK[f"wq{l}"], mq[:, :, :], S_MQ + l)
                freed(BLOCK[f"wq{l}"], hn_out, HN[f"mq{l}"] + 1)

                def m_maxes(u):
                    n = MEM_HEADS * l + u
                    dve.wait_ge(m_s, n + 1)
                    if u >= 2:
                        dve.wait_ge(m_t, n - 1)
                    st = mst[:, u % 2, :]
                    nc.vector.tensor_copy(mp[:, u % 2, :, :], att[:, u % 2, :].rearrange("p (a t) -> p a t", a=2)).then_inc(m_max, 1)
                    dve.wait_ge(m_max, n + 1)
                    nc.vector.tensor_reduce(st[:, 2:4], mp[:, u % 2, :, :], AX_X, ALU.max, negate=True).then_inc(m_nmax, 1)

                def m_inv(u):
                    dve.wait_ge(m_exp, MEM_HEADS * l + u + 1)
                    nc.vector.reciprocal(mst[:, u % 2, 6:8], mst[:, u % 2, 4:6]).then_inc(m_rz, 1)

                def m_low(u):
                    dve.wait_ge(m_ohi, MEM_HEADS * l + u + 1)
                    nc.vector.tensor_tensor(mo_lo[:, u, :], att[:, 3, 0:T], mo_hi[:, u, :].bitcast(F32),
                                            ALU.subtract).then_inc(m_out, 1)

                for u in range(MEM_HEADS + 2):
                    if u < MEM_HEADS:
                        m_maxes(u)
                    if 1 <= u <= MEM_HEADS:
                        m_inv(u - 1)
                    if u >= 2:
                        m_low(u - 2)
                for t in range(8):
                    if t % 2 == 1:
                        b = BLOCK[f"wo{l}"] + t // 2
                        residual(t // 2, b, TICK[f"wo{l}"] + t)
                        freed(b, x_ready, 4 * (n0 + 2) + t // 2 + 1)
                    split(TICK[f"wo{l}"] + t + LEAD)
                norm(n0 + 2, FILL[f"up{l}"], G_FFN + KT * l)
                if f"up{l}" not in run:
                    return
                t0, b0 = TICK[f"up{l}"], BLOCK[f"up{l}"]
                flat = tmp[:, :, :].rearrange("p k t -> p (k t)")
                with dve.Fori(0, FB) as i:
                    for t in range(16):
                        if t == 7:
                            dve.wait_ge(u_silu, i + FB * l + 1)
                            dve.sem_inc(acc_free[b0 % 2], 1)
                        if t == 15:
                            dve.wait_ge(pieces_done, i * 16 + t0 + 16)
                            nc.vector.tensor_tensor(flat, flat, acc[:, (b0 + 1) % 2, :], ALU.mult).then_inc(u_prod, 1)
                            dve.wait_ge(u_prod, i + FB * l + 1)
                            dve.sem_inc(acc_free[(b0 + 1) % 2], 1)
                        split(t0 + t + LEAD, i * 16)
                if f"dn{l}" not in run:
                    return
                for half in range(2):
                    t0, b0 = TICK[f"dn{l}"] + 44 * half, BLOCK[f"dn{l}"] + 2 * half
                    for t in range(4):
                        split(t0 + t + LEAD)
                    with dve.Fori(0, 4) as i:
                        for t in range(8):
                            split(t0 + 4 + t + LEAD, i * 8)
                    for t in range(8):
                        if t == 7:
                            for b in range(2):
                                residual(2 * half + b, b0 + b, t0 + 43)
                                freed(b0 + b, x_ready, 4 * (n0 + 3) + 2 * half + b + 1)
                        split(t0 + 36 + t + LEAD)

            if "out0" in run:
                memory(0)
            if "kcvc" in run:
                norm(3, 4, G_MIX + KT)
                for t in range(16):
                    if t % 8 == 7:
                        b = BLOCK["kcvc"] + t // 8
                        dve.wait_ge(pieces_done, TICK["kcvc"] + t + 1)
                        nc.vector.tensor_copy((kcT, vcT)[t // 8][:, :, :].rearrange("p a t -> p (a t)"),
                                              acc[:, b % 2, :]).then_inc(c_in, 1)
                        freed(b, c_in, t // 8 + 1)
                    split(TICK["kcvc"] + t + LEAD)
                dve.wait_ge(n_whi, 1)
                nc.vector.tensor_tensor(wgt_lo[:, :, :], wgt[:, :, :], wgt_hi[:, :, :].bitcast(F32),
                                        ALU.subtract).then_inc(n_wlo, 1)
            if "cmp" in run:
                for v, src in enumerate((kcT, vcT)):
                    if v:
                        dve.wait_ge(c_lo, 1)
                    for l in range(CMP_L):
                        last = nc.vector.tensor_scalar(
                            xc[:, l, 0:CMP_COLS].rearrange("p (g n) -> p g n", g=4),
                            src[:, :, l:l + CMP_S * (N_CMP - 1) + 1:CMP_S], S[:, (S_PEK, S_PEV)[v] + l:(S_PEK, S_PEV)[v] + l + 1],
                            None, ALU.add)
                    last.then_inc(c_x, 1)
                    dve.wait_ge(c_hi, v + 1)
                    nc.vector.tensor_tensor(xc_lo[v][:, :, 0:CMP_COLS], xc[:, :, 0:CMP_COLS],
                                            xc_hi[v][:, :, 0:CMP_COLS].bitcast(F32), ALU.subtract).then_inc(c_lo, 1)
                for t in range(16):
                    if t % 8 == 7:
                        freed(BLOCK["cmp"] + t // 8, c_hid, t // 8 + 1)
                    split(TICK["cmp"] + t + LEAD)
                dve.wait_ge(c_ksum, 1)
                nc.vector.tensor_copy(kcmp[:, 0:CMP_COLS], att[:, 1, 0:CMP_COLS]).then_inc(c_kraw, 1)
                dve.wait_ge(c_krms, 1)
                nc.vector.reciprocal(kcr[:, 0:CMP_COLS], kcr[:, 0:CMP_COLS]).then_inc(c_krinv, 1)
                dve.wait_ge(c_krinv, 1)
                nc.vector.scalar_tensor_tensor(out=kcmp[:, 0:CMP_COLS], in0=kcmp[:, 0:CMP_COLS],
                                               scalar=S[:, S_NK:S_NK + 1], in1=kcr[:, 0:CMP_COLS],
                                               op0=ALU.mult, op1=ALU.mult).then_inc(c_kout, 1)
                dve.wait_ge(c_v, 1)
                nc.vector.tensor_copy(vcmp[:, :, :], att[0:N_CMP, 3, :].rearrange("p (g d) -> p g d", g=4)).then_inc(c_vout, 1)
                mem_scale(1)
            if "kvs" in run:
                for t in range(32):
                    b = BLOCK["kvs"] + t // 8
                    if 1 <= t < 9:
                        mem_low(1, t - 1)
                    if t in (7, 15):
                        hn_take(HN[("kw", "ks")[t // 8]], b, (kw, ks)[t // 8][:, :, :], TICK["kvs"] + t)
                    if t in (11, 19):
                        k = t // 8 - 1
                        hn_scale(HN[("kw", "ks")[k]], b - 1, (kw, ks)[k][:, :, :], (S_NK + 2, S_NK + 1)[k])
                        freed(b - 1, hn_out, HN[("kw", "ks")[k]] + 1)
                    if t in (23, 31):
                        dve.wait_ge(pieces_done, TICK["kvs"] + t + 1)
                        nc.vector.tensor_copy((vw, vs)[t // 8 - 2][:, :, :],
                                              acc[:, b % 2, :].rearrange("p (a n) -> p a n", a=2)).then_inc(n_v, 1)
                        freed(b, n_v, t // 8 - 1)
                    split(TICK["kvs"] + t + LEAD)

            def nsa_max(u):
                slope = 2.0 ** (-8.0 * (u + 1) / NSA_HEADS)
                dve.wait_ge(n_s, u + 1)
                if u:
                    dve.wait_ge(n_t, 2 * u)
                    dve.wait_ge(n_tc, u)
                    dve.wait_ge(n_nmax, u)
                for br in range(2):
                    nc.vector.scalar_tensor_tensor(out=np_[:, br, :], in0=dm[:, :], scalar=slope,
                                                   in1=att[:, br, 0:384], op0=ALU.mult, op1=ALU.add)
                last = nc.vector.scalar_tensor_tensor(out=npc[:, :, 0:N_CMP], in0=dmc[:, :, 0:N_CMP], scalar=slope,
                                                      in1=att[:, 0, 384:416].rearrange("p (a n) -> p a n", a=2)[:, :, 0:N_CMP],
                                                      op0=ALU.mult, op1=ALU.add)
                last.then_inc(n_p, 1)
                dve.wait_ge(n_p, u + 1)
                for a, cs in ((0, slice(0, P)), (1, slice(P, 384))):
                    for br in range(2):
                        c = 3 * a + 2 - br
                        nc.vector.tensor_reduce(nst[:, 0, c:c + 1], np_[:, br, cs], AX_X, ALU.max)
                    last = nc.vector.tensor_reduce(nst[:, 0, 3 * a:3 * a + 1], npc[:, a, 0:N_CMP], AX_X, ALU.max)
                last.then_inc(n_max, 1)
                dve.wait_ge(n_max, u + 1)
                nc.vector.tensor_scalar(nst[:, 1, 0:6], nst[:, 0, 0:6], -1e20, -1.0, ALU.max,
                                        ALU.mult).then_inc(n_nmax, 1)

            def nsa_rz(u):
                dve.wait_ge(n_exp, u + 1)
                nc.vector.tensor_scalar(nst[:, 2, 0:6], nst[:, 2, 0:6], 1e-30, None, ALU.max).then_inc(n_rzs, 1)
                dve.wait_ge(n_rzs, 2 * u + 1)
                nc.vector.reciprocal(nst[:, 2, 0:6], nst[:, 2, 0:6]).then_inc(n_rzs, 1)
                dve.wait_ge(n_rzs, 2 * u + 2)
                nc.vector.tensor_tensor(nst[:, 3, 0:6].rearrange("p (a b) -> p a b", a=2),
                                        nst[:, 2, 0:6].rearrange("p (a b) -> p a b", a=2),
                                        gate[:, :, 3 * u:3 * u + 3], ALU.mult).then_inc(n_rz, 1)

            def nsa_ptc(u):
                dve.wait_ge(n_tc, u + 1)
                nc.vector.tensor_copy(nptc[:, :, :], att[0:N_CMP, 3, T:2 * T].rearrange("p (a q) -> p a q", a=2)).then_inc(n_ptc, 1)

            def nsa_take(u):
                dve.wait_ge(n_o, u + 1)
                nc.vector.tensor_copy(nq[:, u, :], att[:, 3, 0:T]).then_inc(n_out, 1)

            def nsa(v):
                u, r = divmod(v, 3)
                if r == 2 and u:
                    nsa_take(u - 1)
                if u < NSA_HEADS:
                    if r == 0:
                        nsa_max(u)
                    if r == 1:
                        nsa_rz(u)
                    if r == 2:
                        nsa_ptc(u)

            if "q" in run:
                dve.wait_ge(n_mask, 7)
                for t in range(48):
                    if t % 8 == 7 and t < 32:
                        k = t // 8
                        hn_take(HN[f"q{k}"], BLOCK["q"] + k, nq[:, 4 * k:4 * k + 4, :], TICK["q"] + t)
                    if t % 8 == 3 and 8 <= t < 40:
                        k = t // 8 - 1
                        hn_scale(HN[f"q{k}"], BLOCK["q"] + k, nq[:, 4 * k:4 * k + 4, :], S_NQ)
                        freed(BLOCK["q"] + k, hn_out, HN[f"q{k}"] + 1)
                    if t == 39:
                        hn_take(HN["mk1"], BLOCK["kv1"], mk[:, :, :], TICK["q"] + t)
                    if t == 43:
                        hn_scale(HN["mk1"], BLOCK["kv1"], mk[:, :, :], S_MK + 1)
                        freed(BLOCK["kv1"], hn_out, HN["mk1"] + 1)
                    if t == 47:
                        dve.wait_ge(pieces_done, TICK["q"] + 48)
                        nc.vector.tensor_copy(mv[:, :, :], acc[:, (BLOCK["kv1"] + 1) % 2, :].rearrange("p (a n) -> p a n", a=2)).then_inc(m_v, 1)
                        freed(BLOCK["kv1"] + 1, m_v, 2)
                    if t >= NSA_START:
                        nsa(t - NSA_START)
                    if TICK["q"] + t + LEAD < last_tick:
                        split(TICK["q"] + t + LEAD)
                for v in range(48 - NSA_START, 3 * NSA_HEADS + 3):
                    nsa(v)
            if "out1" in run:
                for c in range(8):
                    h_low(5, c, nq[:, 2 * c:2 * c + 2, :])
                memory(1)
            if dbg is not None:
                dve.wait_ge(x_ready, {"out0": 8, "wo0": 12, "dn0": 16, "out1": 20, "wo1": 24}[stop])
                dve.sem_inc(dbg_done, 1)

        @block.tensor
        def _(pe):
            def sums3(o, lhi, llo, rhi, rlo, start, stop):
                nc.tensor.matmul(o, lhi, rhi, start=start, stop=False, skip_group_check=True)
                nc.tensor.matmul(o, lhi, rlo, start=False, stop=False, skip_group_check=True)
                return nc.tensor.matmul(o, llo, rhi, start=False, stop=stop, skip_group_check=True)

            def piece(p, par, kts, x_hi, x_lo, first, last, tokens_out=False, more=0):
                pe.wait_ge(lo_ready, p + 1 + more)
                s = p % LEAD
                for k in range(2):
                    start, stop = first and k == 0, last and k == 1
                    if tokens_out:
                        for a in range(2):
                            mm = sums3(acc[:, par, a * NB:(a + 1) * NB], x_hi(kts + k, a), x_lo(kts + k, a),
                                       w_hi[:, s, k, :], w_lo[:, s, k, :], start, stop)
                    else:
                        for n in range(4):
                            cs = slice(n * P, (n + 1) * P)
                            mm = sums3(acc[:, par, n * T:(n + 1) * T], w_hi[:, s, k, cs], w_lo[:, s, k, cs],
                                       x_hi(kts + k), x_lo(kts + k), start and n % 2 == 0, stop)
                mm.then_inc(pieces_done, 1)

            def tile_of(x):
                def get(kt, a=None):
                    return x[:, kt, :] if a is None else x[:, kt, a * P:(a + 1) * P]
                return get

            HH, HL = tile_of(h_hi), tile_of(h_lo)

            def claim(b):
                if b >= 2:
                    pe.wait_ge(acc_free[b % 2], b // 2)

            def norm_sum(n, c):
                pe.wait_ge(sq_ready, 8 * n + c + 1)
                for k in range(2):
                    mm = nc.tensor.matmul(att[:, 3, 0:T], ones[:, :], tmp[:, 2 * (c % 2) + k, :],
                                          start=(c == 0 and k == 0), stop=(c == 7 and k == 1))
                mm.then_inc(sq_used, 1)

            def hn_total(i, b):
                pe.wait_ge(hn_sq, i + 1)
                for a in range(2):
                    mm = nc.tensor.matmul(acc[:, b % 2, a * NB:(a + 1) * NB], ones[:, :],
                                          tmp[:, 2 * a:2 * a + 2, :].rearrange("p k t -> p (k t)"), start=True, stop=True)
                mm.then_inc(hn_sum, 1)

            def mem_turn(l, c):
                pe.wait_ge(m_scaled, 2 * l + 2)
                if c >= 4:
                    pe.wait_ge(m_ready, 8 * l + c - 3)
                for k in range(2):
                    for a in range(2):
                        mm = nc.tensor.transpose(att[:, c % 4, k * T + a * P:k * T + (a + 1) * P],
                                                 mtok[l][:, a, (2 * c + k) * P:(2 * c + k + 1) * P], ident[:, :])
                mm.then_inc(m_turn, 1)

            pe.wait_ge(consts, 7)
            pe.wait_ge(small_in, 16 * 13)
            nc.tensor.transpose(att[:, 0, 0:P], g_rows[:, :], ident[:, :]).then_inc(gains_t, 1)
            nc.tensor.transpose(att[:, 1, 0:S_ROWS], s_rows[:, :], ident[0:S_ROWS, 0:S_ROWS]).then_inc(gains_t, 1)
            for c in range(8):
                mem_turn(0, c)
            pe.wait_ge(xtok_in, 16)
            for c in range(8):
                pe.wait_ge(m_ready, min(5 + c, 8))
                if c >= 4:
                    pe.wait_ge(x_copied, c - 3)
                for k in range(2):
                    for a in range(2):
                        mm = nc.tensor.transpose(att[:, c % 4, k * T + a * P:k * T + (a + 1) * P],
                                                 xtok[:, a, (2 * c + k) * P:(2 * c + k + 1) * P], ident[:, :])
                mm.then_inc(x_turn, 1)
            MH, ML = tile_of(memn[0][0]), tile_of(memn[0][1])
            for t in range(16):
                j = t % 8
                piece(t, t // 8, 2 * j, MH, ML, j == 0, j == 7, tokens_out=t >= 8)
                if t < 4:
                    if t == 0:
                        pe.wait_ge(x_ready, 4)
                    norm_sum(0, 2 * t)
                    norm_sum(0, 2 * t + 1)
                if t == 9:
                    hn_total(0, 0)

            def fox_gates():
                pe.wait_ge(ff_wlo, 1)
                for a in range(2):
                    o = att[:, 0, 8 * a:8 * a + 8]
                    for kt in range(KT):
                        sums3(o, HH(kt, a), HL(kt, a), wff_hi[:, kt, :], wff_lo[:, kt, :], kt == 0 and a == 0, False)
                    mm = nc.tensor.matmul(o, ones[0:1, :], fbias[0:1, :], start=False, stop=True, skip_group_check=True)
                mm.then_inc(ff_sum, 1)

            def fox_cumulate():
                pe.wait_ge(ff_lf, 1)
                pe.wait_ge(upper_ready, 2)
                c = att[0:FOX_HEADS, 1, :]
                nc.tensor.matmul(c[:, 0:P], lf[:, 2, 0:8], upper[:, :], start=True, stop=True)
                nc.tensor.matmul(c[:, P:T], lf[:, 2, 0:8], ones[:, :], start=True, stop=False)
                nc.tensor.matmul(c[:, P:T], lf[:, 2, 8:16], upper[:, :], start=False, stop=True).then_inc(ff_c, 1)

            def level(u):
                n, r = divmod(u, 2)
                p, l = divmod(n, LEVELS)
                if r == 1 and n < 4 * LEVELS:
                    m = p * 8 + l - 1
                    if n >= 2:
                        pe.wait_ge(hg_merged, n - 1)
                    if l == 0:
                        pe.wait_ge(hg_k, p // 2 + 1)
                        pe.wait_ge(hg_q, p // 2 + 1)
                        pe.wait_ge(ff_cneg, 1)
                        kx, qx = hz[:, 2 * p:2 * p + 2, :].rearrange("p a t -> p (a t)"), hq[:, 2 * p:2 * p + 2, :].rearrange("p a t -> p (a t)")
                    else:
                        pe.wait_ge(hg_kd, m + 1)
                        pe.wait_ge(hg_qd, m + 1)
                        kx, qx = kd[:, m % 2, :], qd[:, m % 2, :]
                    for a in range(2):
                        if l < 8:
                            for b in range(2):
                                c = a * T + b * P
                                mm = nc.tensor.matmul(att[:, n % 2, c:c + P], kx[:, c:c + P], qx[:, c:c + P],
                                                      start=True, stop=True)
                        else:
                            mm = nc.tensor.matmul(att[:, n % 2, a * P:(a + 1) * P], kx[:, a * T:a * T + P],
                                                  qx[:, a * T + P:(a + 1) * T], start=True, stop=True)
                    mm.then_inc(hg_scores, 1)
                if r == 0 and n >= LEVELS and n % LEVELS == 0:
                    o = n // LEVELS - 1
                    pe.wait_ge(hg_merged, n)
                    pe.wait_ge(hg_v, o // 2 + 1)
                    if o:
                        pe.wait_ge(hg_oraw, o)
                    for a in range(2):
                        h = 2 * o + a
                        v0, v1 = hv[:, 0, h * P:(h + 1) * P], hv[:, 1, h * P:(h + 1) * P]
                        nc.tensor.matmul(att[:, 2, a * T:a * T + P], v0, AT[:, 2 * a, :], start=True, stop=True)
                        nc.tensor.matmul(att[:, 2, a * T + P:(a + 1) * T], v0, AT[:, 4 + a, :], start=True, stop=False)
                        mm = nc.tensor.matmul(att[:, 2, a * T + P:(a + 1) * T], v1, AT[:, 2 * a + 1, :],
                                              start=False, stop=True)
                    mm.then_inc(hg_o, 1)
                if r == 0 and n >= LEVELS and n % LEVELS == 1:
                    o = n // LEVELS - 1
                    pe.wait_ge(hg_osq, o + 1)
                    if o:
                        pe.wait_ge(hg_onorm, o)
                    nc.tensor.matmul(att[:, 3, :], ones[:, :], tmp[:, 0:2, :].rearrange("p k t -> p (k t)"),
                                     start=True, stop=True).then_inc(hg_osum, 1)

            if "in0" in run:
                T0 = TICK["in0"]
                for b, name in enumerate(IN0):
                    claim(b + 2)
                    done = IN0[b - 1] if b else None
                    k = b - 1 - IN0.index(done) if b else 0
                    for j in range(8):
                        if b == 0:
                            pe.wait_ge(h_ready, j + 1)
                        piece(T0 + 8 * b + j, b % 2, 2 * j, HH, HL, j == 0, j == 7, name in ("hi", "fv"))
                        if b == 1 and j == 0:
                            fox_gates()
                        if b == 2 and j == 6:
                            fox_cumulate()
                        if done in ("fq", "fk") and j == 1:
                            hn_total(HN[done + str(k)], b - 1)
                        if 8 * b + j >= HG_START:
                            level(8 * b + j - HG_START)
                for u in range(112 - HG_START, HG_TICKS):
                    level(u)

            if "out0" in run:
                def fox_scores(u):
                    if u == 0:
                        pe.wait_ge(hn_out, HN["fk1"] + 1)
                        pe.wait_ge(ff_cneg, 1)
                        pe.wait_ge(hg_merged, 4 * LEVELS)
                    if u >= 2:
                        pe.wait_ge(f_max, u - 1)
                    pick = ident[0:FOX_HEADS, u:u + 1].broadcast_to([FOX_HEADS, P])
                    for a, cs, w in ((0, slice(0, P), P), (1, slice(P, 384), T)):
                        nc.tensor.matmul(att[:, u % 2, cs], fq[:, u, a * P:(a + 1) * P], fk[:, u, 0:w],
                                         start=True, stop=False)
                        mm = nc.tensor.matmul(att[:, u % 2, cs], pick, cneg[:, 0:w], start=False, stop=True)
                    mm.then_inc(f_s, 1)

                def fox_turn(u):
                    pe.wait_ge(f_pn, u + 1)
                    if u:
                        pe.wait_ge(f_pt, u)
                    else:
                        pe.wait_ge(hg_oraw, 4)
                    for i in range(3):
                        mm = nc.tensor.transpose(att[:, 2, i * P:(i + 1) * P], fp[:, u % 2, i * P:(i + 1) * P], ident[:, :])
                    mm.then_inc(f_t, 1)

                def fox_values(u):
                    pe.wait_ge(f_pt, u + 1)
                    if u:
                        pe.wait_ge(f_out, u)
                    else:
                        pe.wait_ge(hg_onorm, 4)
                        pe.wait_ge(f_v, 2)
                    v0, v1 = fv[:, 0, u * P:(u + 1) * P], fv[:, 1, u * P:(u + 1) * P]
                    pt = fpt[:, u % 2, :]
                    nc.tensor.matmul(att[:, 3, 0:P], v0, pt[:, 0:P], start=True, stop=True)
                    nc.tensor.matmul(att[:, 3, P:T], v0, pt[:, P:T], start=True, stop=False)
                    nc.tensor.matmul(att[:, 3, P:T], v1, pt[:, T:384], start=False, stop=True).then_inc(f_o, 1)

                for u in range(FOX_HEADS + 1):
                    if u < FOX_HEADS:
                        fox_scores(u)
                    if u >= 1:
                        fox_turn(u - 1)
                        fox_values(u - 1)

            def memory(l):
                n0 = 3 * l
                f = FILL[f"out{l}"]
                t0 = TICK[f"out{l}"]
                for t in range(32):
                    b, j = divmod(t, 8)
                    if j == 0:
                        claim(BLOCK[f"out{l}"] + b)
                    if b == 0:
                        pe.wait_ge(h_ready, 8 * f + j + 1)
                    piece(t0 + t, (BLOCK[f"out{l}"] + b) % 2, 2 * FILL_ORDER[f][j], HH, HL, j == 0, j == 7)
                    if b and j == 1:
                        if b == 1:
                            pe.wait_ge(f_out if l == 0 else n_out, FOX_HEADS if l == 0 else NSA_HEADS)
                        norm_sum(n0 + 1, 2 * b - 2)
                        norm_sum(n0 + 1, 2 * b - 1)
                norm_sum(n0 + 1, 6)
                norm_sum(n0 + 1, 7)
                if f"wq{l}" not in run:
                    return
                claim(BLOCK[f"wq{l}"])
                for j in range(8):
                    pe.wait_ge(h_ready, 8 * FILL[f"wq{l}"] + j + 1)
                    piece(TICK[f"wq{l}"] + j, BLOCK[f"wq{l}"] % 2, 2 * j, HH, HL, j == 0, j == 7)
                hn_total(HN[f"mq{l}"], BLOCK[f"wq{l}"])

                def m_scores(u):
                    n = MEM_HEADS * l + u
                    if u == 0:
                        pe.wait_ge(hn_out, HN[f"mq{l}"] + 1)
                        pe.wait_ge(m_v, l + 1)
                    if u >= 2:
                        pe.wait_ge(m_max, n - 1)
                    for a in range(2):
                        mm = nc.tensor.matmul(att[:, u % 2, a * T:(a + 1) * T], mq[:, u, a * P:(a + 1) * P], mk[:, u, :],
                                              start=True, stop=True)
                    mm.then_inc(m_s, 1)

                def m_turns(u):
                    n = MEM_HEADS * l + u
                    pe.wait_ge(m_pn, n + 1)
                    if u:
                        pe.wait_ge(m_pt, n)
                    for k in range(2):
                        for a in range(2):
                            mm = nc.tensor.transpose(att[:, 2, k * T + a * P:k * T + (a + 1) * P],
                                                     mp[:, u % 2, a, k * P:(k + 1) * P], ident[:, :])
                    mm.then_inc(m_t, 1)

                def m_values(u):
                    n = MEM_HEADS * l + u
                    pe.wait_ge(m_pt, n + 1)
                    if u:
                        pe.wait_ge(m_out, n)
                    else:
                        pe.wait_ge(rms_ready, n0 + 2)
                    for k in range(2):
                        mm = nc.tensor.matmul(att[:, 3, 0:T], mv[:, k, u * P:(u + 1) * P], mpt[:, u % 2, k, :],
                                              start=(k == 0), stop=(k == 1))
                    mm.then_inc(m_o, 1)

                for u in range(MEM_HEADS + 1):
                    if u < MEM_HEADS:
                        m_scores(u)
                    if u >= 1:
                        m_turns(u - 1)
                        m_values(u - 1)
                MOH, MOL = tile_of(mo_hi), tile_of(mo_lo)
                for b in range(4):
                    claim(BLOCK[f"wo{l}"] + b)
                    for j in range(2):
                        if b == 0:
                            pe.wait_ge(m_out, MEM_HEADS * l + 2 * j + 2)
                        piece(TICK[f"wo{l}"] + 2 * b + j, (BLOCK[f"wo{l}"] + b) % 2, 2 * j, MOH, MOL, j == 0, j == 1)
                    if b:
                        norm_sum(n0 + 2, 2 * b - 2)
                        norm_sum(n0 + 2, 2 * b - 1)
                norm_sum(n0 + 2, 6)
                norm_sum(n0 + 2, 7)
                if f"up{l}" not in run:
                    return
                t0, b0 = TICK[f"up{l}"], BLOCK[f"up{l}"]
                for j in range(8):
                    pe.wait_ge(h_ready, 8 * FILL[f"up{l}"] + j + 1)
                with pe.Fori(0, FB) as i:
                    for b in range(2):
                        pe.wait_ge(acc_free[(b0 + b) % 2], i + (b0 + b) // 2)
                        for j in range(8):
                            piece(t0 + 8 * b + j, (b0 + b) % 2, 2 * j, HH, HL, j == 0, j == 7, more=i * 16)
                if f"dn{l}" not in run:
                    return

                def hidden(x, i):
                    flat = x[:, :, :].rearrange("p k t -> p (k t)")

                    def get(kt):
                        return flat[:, bass.ds(i * 8 * T + kt * T, T)]
                    return get

                pe.wait_ge(u_ready, FB * (l + 1))
                for half in range(2):
                    t0, b0 = TICK[f"dn{l}"] + 44 * half, BLOCK[f"dn{l}"] + 2 * half
                    XH, XL = tile_of(hid_hi), tile_of(hid_lo)
                    for b in range(2):
                        claim(b0 + b)
                        for j in range(2):
                            piece(t0 + 2 * b + j, (b0 + b) % 2, 2 * j, XH, XL, j == 0, False)
                        if l == 0 and half:
                            norm_sum(3, 2 * b)
                            norm_sum(3, 2 * b + 1)
                    with pe.Fori(0, 4) as i:
                        for g in range(2):
                            for b in range(2):
                                for j in range(2):
                                    piece(t0 + 4 + 4 * g + 2 * b + j, (b0 + b) % 2, 4 + 4 * g + 2 * j,
                                          hidden(hid_hi, i), hidden(hid_lo, i), False, False, more=i * 8)
                    for g in range(2):
                        for b in range(2):
                            for j in range(2):
                                piece(t0 + 36 + 4 * g + 2 * b + j, (b0 + b) % 2, 36 + 4 * g + 2 * j,
                                      XH, XL, False, g == 1 and j == 1)
                    if l == 0 and half:
                        for c in range(4, 8):
                            norm_sum(3, c)

            if "out0" in run:
                memory(0)
            if "kcvc" in run:
                for t in range(16):
                    b, j = divmod(t, 8)
                    if j == 0:
                        claim(BLOCK["kcvc"] + b)
                    if b == 0:
                        pe.wait_ge(h_ready, 8 * 4 + j + 1)
                    piece(TICK["kcvc"] + t, (BLOCK["kcvc"] + b) % 2, 2 * j, HH, HL, j == 0, j == 7)
                pe.wait_ge(n_wlo, 1)
                for a in range(2):
                    for kt in range(KT):
                        mm = sums3(att[:, 0, 48 * a:48 * a + 48], HH(kt, a), HL(kt, a), wgt_hi[:, kt, :],
                                   wgt_lo[:, kt, :], kt == 0 and a == 0, kt == KT - 1)
                mm.then_inc(n_gsum, 1)
            if "cmp" in run:
                for t in range(16):
                    v, j = divmod(t, 8)
                    par = (BLOCK["cmp"] + v) % 2
                    if j == 0:
                        claim(BLOCK["cmp"] + v)
                        pe.wait_ge(c_lo, v + 1)
                    p = TICK["cmp"] + t
                    pe.wait_ge(lo_ready, p + 1)
                    wh = w_hi[:, p % LEAD, :, :].rearrange("p a (b m) -> p (a b) m", m=256)
                    wl = w_lo[:, p % LEAD, :, :].rearrange("p a (b m) -> p (a b) m", m=256)
                    for i in range(4):
                        l = 4 * j + i
                        for m in range(2):
                            ms = slice(m * P, (m + 1) * P)
                            mm = sums3(acc[:, par, 64 * m:64 * m + CMP_COLS], wh[:, i, ms], wl[:, i, ms],
                                       xc_hi[v][:, l, 0:CMP_COLS], xc_lo[v][:, l, 0:CMP_COLS],
                                       l == 0 and m == 0, l == CMP_L - 1)
                    mm.then_inc(pieces_done, 1)
                pe.wait_ge(c_w2, 32)
                pe.wait_ge(c_hid, 2)
                for m in range(2):
                    mm = nc.tensor.matmul(att[:, 1, 0:CMP_COLS], w2c[:, 0, m, :], hidc[:, 0, m, 0:CMP_COLS],
                                          start=(m == 0), stop=(m == 1))
                mm.then_inc(c_ksum, 1)
                for g in range(4):
                    for m in range(2):
                        mm = nc.tensor.matmul(att[0:N_CMP, 3, g * P:(g + 1) * P], hidc[:, 1, m, g * N_CMP:(g + 1) * N_CMP],
                                              w2c[:, 1, m, :], start=(m == 0), stop=(m == 1))
                mm.then_inc(c_v, 1)
                pe.wait_ge(c_ksq, 1)
                nc.tensor.matmul(att[:, 2, 0:CMP_COLS], ones[:, :], kcr[:, 0:CMP_COLS], start=True, stop=True).then_inc(c_ksum, 1)
            if "kvs" in run:
                for t in range(32):
                    b, j = divmod(t, 8)
                    if j == 0:
                        claim(BLOCK["kvs"] + b)
                    piece(TICK["kvs"] + t, (BLOCK["kvs"] + b) % 2, 2 * j, HH, HL, j == 0, j == 7, b >= 2)
                    if t < 8:
                        mem_turn(1, t)
                    if t in (9, 17):
                        hn_total(HN[("kw", "ks")[b - 1]], BLOCK["kvs"] + b - 1)

            def nsa_scores(u):
                g = u // 4
                if u == 0:
                    pe.wait_ge(m_ready, 16)
                    pe.wait_ge(c_kout, 1)
                    pe.wait_ge(c_vout, 1)
                    pe.wait_ge(n_v, 2)
                else:
                    pe.wait_ge(n_p, u)
                if u % 4 == 0:
                    pe.wait_ge(hn_out, HN[f"q{g}"] + 1)
                for br, kx in ((0, kw), (1, ks)):
                    nc.tensor.matmul(att[:, br, 0:P], nq[:, u, 0:P], kx[:, g, 0:P], start=True, stop=True)
                    nc.tensor.matmul(att[:, br, P:384], nq[:, u, P:T], kx[:, g, :], start=True, stop=True)
                for a in range(2):
                    mm = nc.tensor.matmul(att[:, 0, 384 + 16 * a:384 + 16 * a + N_CMP], nq[:, u, a * P:(a + 1) * P],
                                          kcmp[:, g * N_CMP:(g + 1) * N_CMP], start=True, stop=True)
                mm.then_inc(n_s, 1)

            def nsa_turn(u, br):
                if br == 0:
                    pe.wait_ge(n_pn, u + 1)
                if 2 * u + br >= 1:
                    pe.wait_ge(n_pt, 2 * u + br)
                for i in range(3):
                    mm = nc.tensor.transpose(att[:, 2, i * P:(i + 1) * P], np_[:, br, i * P:(i + 1) * P], ident[:, :])
                mm.then_inc(n_t, 1)

            def nsa_turn_cmp(u):
                if u:
                    pe.wait_ge(n_out, u)
                for a in range(2):
                    mm = nc.tensor.transpose(att[0:N_CMP, 3, T + a * P:T + (a + 1) * P], npc[:, a, 0:N_CMP], ident[:, :])
                mm.then_inc(n_tc, 1)

            def nsa_values(u):
                g = u // 4
                gs = slice(g * P, (g + 1) * P)
                pe.wait_ge(n_ptc, u + 1)
                for a in range(2):
                    nc.tensor.matmul(att[:, 3, a * P:(a + 1) * P], vcmp[:, g, :], nptc[:, a, :], start=(a == 0),
                                     stop=False, skip_group_check=True)
                for br, vx in ((0, vw), (1, vs)):
                    pe.wait_ge(n_pt, 2 * u + br + 1)
                    pt = npt[:, br, :]
                    nc.tensor.matmul(att[:, 3, 0:P], vx[:, 0, gs], pt[:, 0:P], start=False, stop=br == 1, skip_group_check=True)
                    nc.tensor.matmul(att[:, 3, P:T], vx[:, 0, gs], pt[:, P:T], start=False, stop=False, skip_group_check=True)
                    mm = nc.tensor.matmul(att[:, 3, P:T], vx[:, 1, gs], pt[:, T:384], start=False, stop=br == 1, skip_group_check=True)
                mm.then_inc(n_o, 1)

            def nsa(v):
                u, r = divmod(v, 3)
                if r == 0 and u:
                    nsa_turn(u - 1, 1)
                if r == 1 and u:
                    nsa_values(u - 1)
                if u < NSA_HEADS:
                    if r == 0:
                        nsa_scores(u)
                    if r == 2:
                        nsa_turn(u, 0)
                        nsa_turn_cmp(u)

            if "q" in run:
                NH, NL = tile_of(memn[1][0]), tile_of(memn[1][1])
                for t in range(48):
                    b, j = divmod(t, 8)
                    if j == 0:
                        claim(BLOCK["q"] + b)
                    if TICK["q"] + t < last_tick:
                        if t == 32:
                            pe.wait_ge(m_ready, 16)
                        piece(TICK["q"] + t, (BLOCK["q"] + b) % 2, 2 * j, HH if t < 32 else NH, HL if t < 32 else NL,
                              j == 0, j == 7, t >= 40)
                    if t % 8 == 1 and 8 <= t < 40:
                        hn_total(HN[f"q{b - 1}"], BLOCK["q"] + b - 1)
                    if t == 41:
                        hn_total(HN["mk1"], BLOCK["kv1"])
                    if t >= NSA_START:
                        nsa(t - NSA_START)
                for v in range(48 - NSA_START, 3 * NSA_HEADS + 3):
                    nsa(v)
            if "out1" in run:
                memory(1)
            if stop is None:
                for g in range(8):
                    b, a = divmod(g, 2)
                    pe.wait_ge(x_ready, 24 + b + 1)
                    if g >= 4:
                        pe.wait_ge(out_copied, g - 3)
                    else:
                        pe.wait_ge(rms_ready, 6)
                    for k in range(4):
                        mm = nc.tensor.transpose(att[:, g % 4, k * P:(k + 1) * P], xT[:, 4 * b + k, a * P:(a + 1) * P], ident[:, :])
                    mm.then_inc(out_turn, 1)


NSA_START = 12
FILL_ORDER = [list(range(8)), [4, 5, 6, 7, 0, 1, 2, 3]] + [list(range(8))] * 6


_INS = ["x", "mem", "norm_mix", "norm_mem", "norm_ffn", "mem_in_gain", "even_w_in", "even_w_out", "fox_f_bias",
        "fox_q_gain", "fox_k_gain", "hgrn_lb_logits", "hgrn_o_gain", "odd_w_in", "odd_w_out", "nsa_q_gain",
        "nsa_k_gain", "cmp_pe_k", "cmp_w1_k", "cmp_w2_k", "cmp_pe_v", "cmp_w1_v", "cmp_w2_v", "mem_wq",
        "mem_wkv", "mem_wo", "mem_q_gain", "mem_k_gain", "ffn_w1", "ffn_w3", "ffn_w2"]
_STOP = None


def kernel(**inputs):
    import numpy as _np
    import concourse.bacc as _bacc
    from concourse import mybir as _mybir
    from concourse.bass_utils import run_bass_kernel_spmd as _run

    nc = _bacc.Bacc("TRN2", target_bir_lowering=False, num_devices=1)
    arrays, args = {}, {}
    for name in _INS:
        a = _np.ascontiguousarray(inputs[name])
        arrays[f"in_{name}"] = a
        args[name] = nc.dram_tensor(f"in_{name}", a.shape, _mybir.dt.from_np(a.dtype), kind="ExternalInput").ap()
    shape = inputs["x"].shape
    if _STOP is None:
        out = nc.dram_tensor("out_0", shape, _mybir.dt.float32, kind="ExternalOutput").ap()
        trunk(nc, args, out)
        return _run(nc, [arrays], core_ids=[0]).results[0]["out_0"]
    out = nc.dram_tensor("out_0", (2048, 256), _mybir.dt.float32, kind="ExternalOutput").ap()
    trunk(nc, args, None, stop=_STOP, dbg=out)
    return _run(nc, [arrays], core_ids=[0]).results[0]["out_0"]
```

```python
import concourse.bass as bass
from concourse import mybir
from contextlib import ExitStack

F32 = mybir.dt.float32
F32R = mybir.dt.float32r
U8 = mybir.dt.uint8
ALU = mybir.AluOpType
ACT = mybir.ActivationFunctionType
AX_X = mybir.AxisListType.X

P = 128
T = 256
D = 2048
KT = D // P
HD = 128
NB = 512
LEAD = 4
RAW = 4
FFN = 5632
FB = FFN // NB
FT = FFN // P
EPS = 1e-6
NEG = -1e30
FOX_HEADS = 8
HG_HEADS = 8
NSA_HEADS = 16
MEM_HEADS = 4
CMP_L = 32
CMP_S = 16
N_CMP = (T - CMP_L) // CMP_S + 1
CMP_COLS = 4 * N_CMP
LEVELS = 9

SECTIONS = [("in0", 14, 112), ("out0", 4, 32), ("kvk0", 1, 8), ("wq0", 1, 8), ("kvv0", 1, 8), ("wo0", 4, 8),
            ("up0", 22, 176), ("dn0", 4, 88),
            ("kcvc", 2, 16), ("cmp", 2, 16), ("kvs", 4, 32), ("q", 4, 32),
            ("out1", 4, 32), ("kvk1", 1, 8), ("wq1", 1, 8), ("kvv1", 1, 8), ("wo1", 4, 8),
            ("up1", 22, 176), ("dn1", 4, 88)]
TICK, BLOCK = {}, {}
_t = _b = 0
for _name, _nb, _nt in SECTIONS:
    TICK[_name], BLOCK[_name] = _t, _b
    _t += _nt
    _b += _nb
TICKS = _t

IN0 = ["hq", "hf", "hq", "hf", "hi", "hg", "hi", "hg", "fq", "fq", "fk", "fk", "fv", "fv"]
IN0_COL = {"fq": 0, "fk": 1024, "fv": 2048, "hq": 3080, "hf": 4104, "hi": 5128, "hg": 6152}
KTH = [IN0[:b].count(name) for b, name in enumerate(IN0)]
FF_COL = 3072
ODD_COL = {"q": 0, "kc": 2048, "vc": 2560, "ks": 3072, "vs": 3584, "kw": 4096, "vw": 4608}
GT_COL = 5120
ADDED = [0, 5, 5, 3, 5, 5]
USED = [sum(8 - a for a in ADDED[:n]) for n in range(7)]
HG_START = 20
FOX_START = 104
FOX_TICKS = FOX_HEADS + 4

S_PEK, S_PEV, S_FQ, S_FK, S_HO, S_NQ, S_NK, S_MQ, S_MK = 0, 32, 64, 65, 66, 67, 68, 71, 73
S_ROWS = 75
G_MIX, G_MEM, G_FFN, G_IN = 0, 32, 64, 96


def nsa_ticks(t):
    if t < 12:
        return [32 + t - NSA_START]
    return list(range(44 - NSA_START, 2 * NSA_HEADS + 4)) if t == 12 else []


def trunk(nc, A, out):
    ctx = ExitStack()
    with ctx:
        def sem(name):
            return ctx.enter_context(nc.semaphore(name))

        base = (nc.sbuf_base + 63) // 64 * 64
        top = [base]

        def place(name, shape, dt=F32):
            n = 1
            for s in shape[1:]:
                n *= s
            at = top[0]
            top[0] += (n * (1 if dt == U8 else 4) + 31) // 32 * 32
            return nc.alloc_sbuf_tensor_at(name, shape, dt, offset=at)

        raw = place("raw", [P, RAW, 4, NB])
        w_hi = place("w_hi", [P, LEAD, 2, NB], F32R)
        w_lo = place("w_lo", [P, LEAD, 2, NB], F32R)
        xT = place("xT", [P, KT, T])
        h_hi_at = top[0]
        h_hi = place("h_hi", [P, KT, T], F32R)
        h_lo = place("h_lo", [P, KT, T], F32R)
        tmp = place("tmp", [P, 4, T])
        ident = place("ident", [P, P])
        ones = place("ones", [P, P])
        G = place("G", [P, P])
        S = place("S", [P, S_ROWS])
        rinv = place("rinv", [P, T])
        cneg = place("cneg", [FOX_HEADS, T])
        eps = place("eps", [P, 2])
        R = top[0]
        K = 1024

        def at(name, shape, off, dt=F32):
            return nc.alloc_sbuf_tensor_at(name, shape, dt, offset=R + off)

        hid_hi = at("hid_hi", [P, FT, T], 0, F32R)
        hid_lo = at("hid_lo", [P, FT, T], 44 * K, F32R)
        mk = at("mk", [P, MEM_HEADS, T], 0)
        mv = at("mv", [P, 2, NB], 4 * K)
        hq = at("hq", [P, 8, T], 8 * K)
        hz = at("hz", [P, 8, T], 16 * K)
        hb = at("hb", [P, 8, T], 24 * K)
        hv = at("hv", [P, 2, 1024], 32 * K)
        hg = at("hg", [P, 8, T], 40 * K)
        fq = at("fq", [P, 8, T], 48 * K)
        fk = at("fk", [P, 8, T], 56 * K)
        fv = at("fv", [P, 2, 1024], 64 * K)
        decay = at("decay", [P, 2, 512], 72 * K)
        kd = at("kd", [P, 2, 512], 76 * K)
        qd = at("qd", [P, 2, 512], 80 * K)
        AT = at("AT", [P, 6, P], 84 * K)
        lmask = at("lmask", [P, 8, P], 87 * K, U8)
        memn = [(at("memn_hi0", [P, KT, T], 32 * K, F32R), at("memn_lo0", [P, KT, T], 56 * K, F32R)),
                (at("memn_hi1", [P, KT, T], 56 * K, F32R), at("memn_lo1", [P, KT, T], 72 * K, F32R))]
        mtok = [at("mtok0", [P, 2, D], 16 * K), at("mtok1", [P, 2, D], 8 * K)]
        xtok = at("xtok", [P, 2, D], 8 * K)
        maskf = at("maskf", [P, 8, P], 72 * K)
        g_rows = at("g_rows", [P, P], 80 * K)
        s_rows = at("s_rows", [S_ROWS, P], 81 * K)
        mss = at("mss", [P, 4], 82 * K)
        wff = at("wff", [P, KT, 8], 64 * K)
        wff_hi = at("wff_hi", [P, KT, 8], 64 * K + 512, F32R)
        wff_lo = at("wff_lo", [P, KT, 8], 65 * K, F32R)
        fbias = at("fbias", [1, 8], 65 * K + 512)
        lf = at("lf", [FOX_HEADS, 2, T], 66 * K)
        fp = at("fp", [P, 4, 384], 72 * K)
        fpt = at("fpt", [P, 2, 384], 78 * K)
        fmask = at("fmask", [P, T], 81 * K)
        fst = at("fst", [P, 4, 8], 82 * K)
        mq = at("mq", [P, MEM_HEADS, T], 8 * K)
        mp = at("mp", [P, MEM_HEADS, 2, T], 12 * K)
        mst = at("mst", [P, MEM_HEADS, 8], 20 * K)
        mo_hi = at("mo_hi", [P, MEM_HEADS, T], 24 * K, F32R)
        mo_lo = at("mo_lo", [P, MEM_HEADS, T], 28 * K, F32R)
        mpt = at("mpt", [P, MEM_HEADS, 2, T], 48 * K)
        otok = nc.alloc_sbuf_tensor_at("otok", [P, 2, D], F32, offset=h_hi_at)
        nq = at("nq", [P, NSA_HEADS, T], 8 * K)
        kw = at("kw", [P, 4, T], 24 * K)
        ks = at("ks", [P, 4, T], 28 * K)
        vw = at("vw", [P, 2, NB], 32 * K)
        vs = at("vs", [P, 2, NB], 36 * K)
        kcT = at("kcT", [P, 4, T], 56 * K)
        vcT = at("vcT", [P, 4, T], 60 * K)
        xc = at("xc", [P, CMP_L, 64], 64 * K)
        xc_hi = [at("xck_hi", [P, CMP_L, 64], 24 * K, F32R), at("xcv_hi", [P, CMP_L, 64], 72 * K, F32R)]
        xc_lo = [at("xck_lo", [P, CMP_L, 64], 32 * K, F32R), at("xcv_lo", [P, CMP_L, 64], 80 * K, F32R)]
        hrow = at("hrow", [CMP_COLS, 2, 2 * P], 0)
        gateT = at("gateT", [48, T], 2 * K)
        hidc = at("hidc", [P, 2, 2, 64], 40 * K)
        w2c = at("w2c", [P, 2, 2, P], 41 * K)
        kcmp = at("kcmp", [P, 64], 43 * K)
        kcr = at("kcr", [P, 64], 43 * K + 256)
        vcmp = at("vcmp", [N_CMP, 4, P], 43 * K + 512)
        gate = at("gate", [P, 2, 48], 45 * K + 512)
        dm = at("dm", [P, 384], 46 * K)
        dmc = at("dmc", [P, 2, 16], 47 * K + 512)
        np_ = at("np_", [P, 2, 2, 384], 48 * K)
        npt = at("npt", [P, 2, 384], 0)
        nptc = at("nptc", [N_CMP, 2, P], 3 * K)
        npc = at("npc", [P, 2, 2, 16], 4 * K)
        nst = at("nst", [P, 2, 4, 8], 4 * K + 512)
        wgt = at("wgt", [P, KT, 48], 44 * K)
        wgt_hi = at("wgt_hi", [P, KT, 48], 47 * K, F32R)
        wgt_lo = at("wgt_lo", [P, KT, 48], 50 * K, F32R)

        acc = ctx.enter_context(nc.psum_tensor("acc", [P, 2, 2 * NB], F32))
        att = ctx.enter_context(nc.psum_tensor("att", [P, 4, NB], F32))

        raw_full = [sem(f"raw_full{i}") for i in range(RAW)]
        hi_ready = sem("hi_ready")
        lo_ready = sem("lo_ready")
        pieces_done = sem("pieces_done")
        acc_free = [sem("acc_free0"), sem("acc_free1")]
        consts = sem("consts")
        small_in = sem("small_in")
        mtok_in = sem("mtok_in")
        xtok_in = [sem(f"xtok_in{c}") for c in range(4)]
        gains_t = sem("gains_t")
        gains = sem("gains")
        m_ssq, m_rms, m_scaled = sem("m_ssq"), sem("m_rms"), sem("m_scaled")
        m_rinv = sem("m_rinv")
        m_turn, m_hi, m_ready = sem("m_turn"), sem("m_hi"), sem("m_ready")
        x_turn, x_copied, x_ready = sem("x_turn"), sem("x_copied"), sem("x_ready")
        sq_ready, sq_added, sq_used = sem("sq_ready"), sem("sq_added"), sem("sq_used")
        rms_ready, rinv_ready = sem("rms_ready"), sem("rinv_ready")
        h_tmp, h_hi_ready, h_ready = sem("h_tmp"), sem("h_hi_ready"), sem("h_ready")
        hn_raw, hn_sq, hn_sum = sem("hn_raw"), sem("hn_sq"), sem("hn_sum")
        hn_rms, hn_rinv, hn_out = sem("hn_rms"), sem("hn_rinv"), sem("hn_out")
        ff_w, ff_whi, ff_wlo = sem("ff_w"), sem("ff_whi"), sem("ff_wlo")
        ff_sum, ff_z, ff_l, ff_lf, ff_c, ff_cneg = (sem(n) for n in
            ("ff_sum", "ff_z", "ff_l", "ff_lf", "ff_c", "ff_cneg"))
        lmask_ready, fmask_ready = sem("lmask_ready"), sem("fmask_ready")
        hg_q, hg_z, hg_abs, hg_lf, hg_kin, hg_k, hg_b, hg_v, hg_gate = (sem(n) for n in
            ("hg_q", "hg_z", "hg_abs", "hg_lf", "hg_kin", "hg_k", "hg_b", "hg_v", "hg_gate"))
        hg_diff, hg_decay, hg_kd, hg_qd, hg_scores, hg_merged, hg_zero = (sem(n) for n in
            ("hg_diff", "hg_decay", "hg_kd", "hg_qd", "hg_scores", "hg_merged", "hg_zero"))
        hg_o, hg_oraw, hg_osq, hg_osum, hg_orms, hg_orinv, hg_onorm, hg_out = (sem(n) for n in
            ("hg_o", "hg_oraw", "hg_osq", "hg_osum", "hg_orms", "hg_orinv", "hg_onorm", "hg_out"))
        f_v, f_s, f_max, f_nmax, f_exp, f_rz, f_pn, f_t, f_pt, f_o, f_out = (sem(n) for n in
            ("f_v", "f_s", "f_max", "f_nmax", "f_exp", "f_rz", "f_pn", "f_t", "f_pt", "f_o", "f_out"))
        m_v, m_s, m_nmax, m_exp, m_rz, m_pn, m_t, m_pt, m_o, m_ohi, m_out = (sem(n) for n in
            ("m_v", "m_s", "m_nmax", "m_exp", "m_rz", "m_pn", "m_t", "m_pt", "m_o", "m_ohi", "m_out"))
        u_silu, u_prod, u_hi, u_ready = sem("u_silu"), sem("u_prod"), sem("u_hi"), sem("u_ready")
        out_turn, out_copied, out_done = sem("out_turn"), sem("out_copied"), sem("out_done")
        n_w, n_whi, n_wlo, n_gsum, n_gateT, n_gturn, n_gate = (sem(n) for n in
            ("n_w", "n_whi", "n_wlo", "n_gsum", "n_gateT", "n_gturn", "n_gate"))
        c_in, c_x, c_hi, c_lo, c_row, c_turn, c_hid, c_w2, c_v = (sem(n) for n in
            ("c_in", "c_x", "c_hi", "c_lo", "c_row", "c_turn", "c_hid", "c_w2", "c_v"))
        c_ksum, c_kraw, c_ksq, c_krms, c_krinv, c_kout, c_vout = (sem(n) for n in
            ("c_ksum", "c_kraw", "c_ksq", "c_krms", "c_krinv", "c_kout", "c_vout"))
        n_v, n_s, n_p, n_max, n_nmax, n_exp, n_rz, n_pn = (sem(n) for n in
            ("n_v", "n_s", "n_p", "n_max", "n_nmax", "n_exp", "n_rz", "n_pn"))
        n_t, n_pt, n_o, n_out = sem("n_t"), sem("n_pt"), sem("n_o"), sem("n_out")
        n_mask, n_rzs, n_tc, n_ptc = sem("n_mask"), sem("n_rzs"), sem("n_tc"), sem("n_ptc")

        def w_rows(w):
            return w.rearrange("(k p) n -> p k n", p=P)

        w_in0 = w_rows(A["even_w_in"][0])
        w_in1 = w_rows(A["odd_w_in"][0])
        w_out = [w_rows(A["even_w_out"][0]), w_rows(A["odd_w_out"][0])]
        wq = [w_rows(A["mem_wq"][l]) for l in range(2)]
        wkv = [w_rows(A["mem_wkv"][l]) for l in range(2)]
        wo = [w_rows(A["mem_wo"][l]) for l in range(2)]
        w1 = [w_rows(A["ffn_w1"][l]) for l in range(2)]
        w3 = [w_rows(A["ffn_w3"][l]) for l in range(2)]
        w2 = [w_rows(A["ffn_w2"][l]) for l in range(2)]
        cw1 = [A[n][0].rearrange("l d m -> d l m") for n in ("cmp_w1_k", "cmp_w1_v")]

        FILL = {"in0": 0, "out0": 1, "wq0": 2, "up0": 3, "kcvc": 4, "out1": 5, "wq1": 6, "up1": 7}
        LAST_READ = {0: None, 1: TICK["out0"], 2: TICK["kvk0"], 3: TICK["kvv0"], 4: TICK["dn0"],
                     5: TICK["out1"], 6: TICK["kvk1"], 7: TICK["kvv1"]}
        HN = {"fq0": 0, "fq1": 1, "fk0": 2, "fk1": 3, "mk0": 4, "mq0": 5, "kw": 6, "ks": 7,
              "q0": 8, "q1": 9, "q2": 10, "q3": 11, "mk1": 12, "mq1": 13}

        block = ctx.enter_context(nc.Block())

        @block.sync
        def _(sp):
            def slab(s, src, more=0):
                if s >= RAW:
                    sp.wait_ge(lo_ready, 2 * (s - RAW) + 2 + more)
                sp.dma_start(raw[:, s % RAW, :, :], src).then_inc(raw_full[s % RAW], 16)

            def block_rows(s, w, col, rows=(0, 1, 2, 3), more=0):
                for c, r in enumerate(rows):
                    slab(s + c, w[:, 4 * r:4 * r + 4, col], more)

            def cols(n, wide=NB):
                return slice(n, n + wide)

            def up(l):
                s = TICK[f"up{l}"] // 2
                with sp.Fori(0, FB) as i:
                    block_rows(s, w1[l], bass.ds(i * NB, NB), more=i * 16)
                    block_rows(s + 4, w3[l], bass.ds(i * NB, NB), more=i * 16)

            def down(l):
                for half in range(2):
                    s = TICK[f"dn{l}"] // 2 + 22 * half
                    for b in range(2):
                        slab(s + b, w2[l][:, 0:4, cols((2 * half + b) * NB)])
                    with sp.Fori(0, 5) as i:
                        for j in range(4):
                            slab(s + 2 + j, w2[l][:, bass.ds(i * 8 + 4 + j // 2 * 4, 4),
                                                  cols((2 * half + j % 2) * NB)], i * 8)

            def memory(l):
                block_rows(TICK[f"kvk{l}"] // 2, wkv[l], cols(0))
                block_rows(TICK[f"wq{l}"] // 2, wq[l], cols(0))
                block_rows(TICK[f"kvv{l}"] // 2, wkv[l], cols(NB))
                for b in range(4):
                    slab(TICK[f"wo{l}"] // 2 + b, wo[l][:, 0:4, cols(b * NB)])
                up(l)
                down(l)

            for c in range(4):
                sp.dma_start(xtok[:, :, cols(c * NB)],
                             A["x"][0].rearrange("(a p) f -> p a f", p=P)[:, :, cols(c * NB)]).then_inc(xtok_in[c], 16)
            sp.wait_ge(small_in, 16 * 13)
            seen = {}
            for b, name in enumerate(IN0):
                n = seen.get(name, 0)
                seen[name] = n + 1
                block_rows(TICK["in0"] // 2 + 4 * b, w_in0, cols(IN0_COL[name] + n * NB))
            def output(l, order):
                s = TICK[f"out{l}"] // 2
                for c, r in enumerate(order):
                    for b in range(2):
                        slab(s + 2 * c + b, w_out[l][:, 4 * r:4 * r + 4, cols(b * NB)])
                for b in range(2, 4):
                    block_rows(s + 4 * b, w_out[l], cols(b * NB), order)

            output(0, (2, 3, 0, 1))
            memory(0)
            for b, name in enumerate(("kc", "vc")):
                block_rows(TICK["kcvc"] // 2 + 4 * b, w_in1, cols(ODD_COL[name]))
            for b in range(2):
                for c in range(4):
                    s = TICK["cmp"] // 2 + 4 * b + c
                    sp.wait_ge(lo_ready, 2 * (s - RAW) + 2)
                    sp.dma_start(raw[:, s % RAW, :, :].rearrange("p a (b m) -> p (a b) m", m=256),
                                 cw1[b][:, 8 * c:8 * c + 8, :]).then_inc(raw_full[s % RAW], 16)
            for b, name in enumerate(("kw", "ks", "vw", "vs")):
                block_rows(TICK["kvs"] // 2 + 4 * b, w_in1, cols(ODD_COL[name]))
            for b in range(4):
                block_rows(TICK["q"] // 2 + 4 * b, w_in1, cols(b * NB))
            output(1, (0, 1, 2, 3))
            memory(1)
            for b in range(4):
                sp.wait_ge(out_copied, 2 * b + 2)
                sp.dma_start(out[0].rearrange("(a p) f -> p a f", p=P)[:, :, cols(b * NB)],
                             otok[:, :, b * NB:(b + 1) * NB]).then_inc(out_done, 16)
            sp.wait_ge(out_done, 64)

        @block.gpsimd
        def _(pool):
            nc.gpsimd.memset(ident[:, :], 0.0).then_inc(consts, 1)
            nc.gpsimd.memset(ones[:, :], 1.0).then_inc(consts, 1)
            nc.gpsimd.memset(eps[:, 0:1], EPS).then_inc(consts, 1)
            nc.gpsimd.memset(eps[:, 1:2], EPS * HD).then_inc(consts, 1)
            nc.gpsimd.memset(maskf[:, :, :], 0.0).then_inc(consts, 1)
            pool.wait_ge(consts, 5)
            nc.gpsimd.affine_select(out=ident[:, :], in_=ident[:, :], compare_op=ALU.not_equal, fill=1.0,
                                    base=0, pattern=[[-1, P]], channel_multiplier=1).then_inc(consts, 1)
            nc.gpsimd.affine_select(out=maskf[:, 0, :], in_=maskf[:, 0, :], compare_op=ALU.not_equal, fill=1.0,
                                    base=0, pattern=[[-1, P]], channel_multiplier=1).then_inc(consts, 1)
            def right(l):
                return maskf[:, l, :].rearrange("p (n a h) -> p n a h", a=2, h=1 << (l - 1))[:, :, 1, :]

            pool.wait_ge(consts, 7)
            for l in range(1, 8):
                nc.gpsimd.memset(right(l), 1.0).then_inc(consts, 1)
            pool.wait_ge(consts, 14)
            for l in range(1, 8):
                h = 1 << (l - 1)
                nc.gpsimd.affine_select(out=right(l), in_=right(l), compare_op=ALU.is_ge, fill=0.0, base=0,
                                        pattern=[[-2 * h, P // (2 * h)], [0, h]],
                                        channel_multiplier=1).then_inc(consts, 1)
            pool.wait_ge(consts, 21)
            for l in range(1, 8):
                h = 1 << (l - 1)
                nc.gpsimd.affine_select(out=right(l), in_=right(l), compare_op=ALU.is_ge, fill=0.0, base=h - 1,
                                        pattern=[[2 * h, P // (2 * h)], [0, h]],
                                        channel_multiplier=-1).then_inc(consts, 1)
            pool.wait_ge(consts, 28)
            nc.gpsimd.tensor_copy(lmask[:, :, :], maskf[:, :, :]).then_inc(lmask_ready, 1)
            for n in range(4 * LEVELS + 6):
                p, l = divmod(n, LEVELS)
                if n < 4 * LEVELS and l > 0:
                    m = p * 8 + l - 1
                    pool.wait_ge(hg_decay, m + 1)
                    if m >= 2:
                        pool.wait_ge(hg_scores, (m - 2) // 8 * 9 + (m - 2) % 8 + 2)
                    nc.gpsimd.tensor_tensor(qd[:, m % 2, :], hq[:, 2 * p:2 * p + 2, :].rearrange("p a t -> p (a t)"),
                                            decay[:, m % 2, :], ALU.mult).then_inc(hg_qd, 1)
                if n >= LEVELS + 5 and (n - 5) % LEVELS == 0:
                    o = (n - 5) // LEVELS - 1
                    pool.wait_ge(hg_onorm, o + 1)
                    pool.wait_ge(hg_gate, o // 2 + 1)
                    nc.gpsimd.tensor_tensor(hq[:, 2 * o:2 * o + 2, :], hq[:, 2 * o:2 * o + 2, :],
                                            hg[:, 2 * o:2 * o + 2, :], ALU.mult).then_inc(hg_out, 1)
            pool.wait_ge(hg_o, 4)
            nc.gpsimd.memset(fmask[:, :], 0.0).then_inc(fmask_ready, 1)
            pool.wait_ge(fmask_ready, 1)
            nc.gpsimd.affine_select(out=fmask[:, P:T], in_=fmask[:, P:T], compare_op=ALU.is_ge, fill=NEG,
                                    base=0, pattern=[[-1, P]], channel_multiplier=1).then_inc(fmask_ready, 1)
            for u in range(FOX_HEADS):
                pool.wait_ge(f_rz, u + 1)
                nc.gpsimd.tensor_scalar(fp[:, u % 4, 0:P], fp[:, u % 4, 0:P], fst[:, u % 4, 6:7], None,
                                        ALU.mult)
                nc.gpsimd.tensor_scalar(fp[:, u % 4, P:384], fp[:, u % 4, P:384], fst[:, u % 4, 7:8], None,
                                        ALU.mult).then_inc(f_pn, 1)

            def add_squares(n):
                for c in range(1, ADDED[n] + 1):
                    pool.wait_ge(sq_ready, 8 * n + c + 1)
                    if c > 1:
                        pool.wait_ge(sq_added, sum(ADDED[:n]) + c - 1)
                    v, w = tmp[:, 2 * (c % 2):2 * (c % 2) + 2, :], tmp[:, 2 * ((c + 1) % 2):2 * ((c + 1) % 2) + 2, :]
                    nc.gpsimd.tensor_tensor(v, v, w, ALU.add).then_inc(sq_added, 1)

            def memory(l):
                add_squares(3 * l + 1)
                for u in range(MEM_HEADS):
                    n = MEM_HEADS * l + u
                    pool.wait_ge(m_rz, n + 1)
                    for a in range(2):
                        last = nc.gpsimd.tensor_scalar(mp[:, u, a, :], mp[:, u, a, :],
                                                       mst[:, u, 6 + a:7 + a], None, ALU.mult)
                    last.then_inc(m_pn, 1)
                add_squares(3 * l + 2)

            def up(l):
                with pool.Fori(0, FB) as i:
                    pool.wait_ge(u_prod, i + FB * l + 1)
                    flat = hid_hi[:, :, :].rearrange("p k t -> p (k t)")
                    flat_lo = hid_lo[:, :, :].rearrange("p k t -> p (k t)")
                    nc.gpsimd.tensor_copy(flat[:, bass.ds(i * 1024, 1024)],
                                          tmp[:, :, :].rearrange("p k t -> p (k t)")).then_inc(u_hi, 1)
                    pool.wait_ge(u_hi, i + FB * l + 1)
                    nc.gpsimd.tensor_tensor(flat_lo[:, bass.ds(i * 1024, 1024)],
                                            tmp[:, :, :].rearrange("p k t -> p (k t)"),
                                            flat[:, bass.ds(i * 1024, 1024)].bitcast(F32),
                                            ALU.subtract).then_inc(u_ready, 1)

            memory(0)
            up(0)
            add_squares(3)
            for v, (src, pos) in enumerate(((kcT, S_PEK), (vcT, S_PEV))):
                pool.wait_ge(c_in, v + 1)
                if v:
                    pool.wait_ge(c_lo, 1)
                for g in range(4):
                    for a in range(2):
                        ls = slice(CMP_S * a, CMP_S * (a + 1))
                        last = nc.gpsimd.tensor_tensor(
                            xc[:, ls, g * N_CMP:(g + 1) * N_CMP],
                            src[:, g, CMP_S * a:CMP_S * (a + N_CMP)].rearrange("p (n i) -> p i n", i=CMP_S),
                            S[:, pos + CMP_S * a:pos + CMP_S * (a + 1)].rearrange("p (i o) -> p i o", o=1)
                            .broadcast_to([P, CMP_S, N_CMP]), ALU.add)
                last.then_inc(c_x, 1)
                pool.wait_ge(c_hi, v + 1)
                nc.gpsimd.tensor_tensor(xc_lo[v][:, :, 0:CMP_COLS], xc[:, :, 0:CMP_COLS],
                                        xc_hi[v][:, :, 0:CMP_COLS].bitcast(F32), ALU.subtract).then_inc(c_lo, 1)
            pool.wait_ge(n_gate, 1)
            nc.gpsimd.iota(dm[:, 0:P], pattern=[[1, P]], base=0, channel_multiplier=-1,
                           allow_small_or_imprecise_dtypes=True).then_inc(n_mask, 1)
            nc.gpsimd.iota(dm[:, P:384], pattern=[[1, T]], base=-P, channel_multiplier=-1,
                           allow_small_or_imprecise_dtypes=True).then_inc(n_mask, 1)
            nc.gpsimd.iota(dmc[:, :, 0:N_CMP], pattern=[[-2 * P, 2], [2 * CMP_S, N_CMP]], base=CMP_L - 1,
                           channel_multiplier=-2, allow_small_or_imprecise_dtypes=True).then_inc(n_mask, 1)
            pool.wait_ge(n_mask, 3)
            nc.gpsimd.affine_select(out=dm[:, 0:P], in_=dm[:, 0:P], compare_op=ALU.is_ge, fill=NEG, base=0,
                                    pattern=[[-1, P]], channel_multiplier=1).then_inc(n_mask, 1)
            nc.gpsimd.affine_select(out=dm[:, P:384], in_=dm[:, P:384], compare_op=ALU.is_ge, fill=NEG,
                                    base=P, pattern=[[-1, T]], channel_multiplier=1).then_inc(n_mask, 1)
            nc.gpsimd.tensor_scalar(dmc[:, :, 0:N_CMP], dmc[:, :, 0:N_CMP], 0.5, None,
                                    ALU.mult).then_inc(n_mask, 1)
            pool.wait_ge(n_mask, 6)
            nc.gpsimd.affine_select(out=dmc[:, :, 0:N_CMP], in_=dmc[:, :, 0:N_CMP], compare_op=ALU.is_ge,
                                    fill=NEG, base=-(CMP_L - 1), pattern=[[P, 2], [-CMP_S, N_CMP]],
                                    channel_multiplier=1).then_inc(n_mask, 1)
            for u in range(NSA_HEADS):
                pool.wait_ge(n_rz, u + 1)
                for br in range(2):
                    for a, cs in ((0, slice(0, P)), (1, slice(P, 384))):
                        c = 3 * a + 2 - br
                        nc.gpsimd.tensor_scalar(np_[:, u % 2, br, cs], np_[:, u % 2, br, cs], nst[:, u % 2, 3, c:c + 1], None,
                                                ALU.mult)
                for a in range(2):
                    last = nc.gpsimd.tensor_scalar(npc[:, u % 2, a, 0:N_CMP], npc[:, u % 2, a, 0:N_CMP],
                                                   nst[:, u % 2, 3, 3 * a:3 * a + 1], None, ALU.mult)
                last.then_inc(n_pn, 1)
            memory(1)
            up(1)

        @block.scalar
        def _(act):
            for v, name in enumerate(("norm_mix", "norm_mem", "norm_ffn", "mem_in_gain")):
                act.dma_start(g_rows[32 * v:32 * v + 32, :],
                              A[name].rearrange("l (k p) -> (l k) p", p=P)).then_inc(small_in, 16)
            for row, name in ((S_PEK, "cmp_pe_k"), (S_PEV, "cmp_pe_v"), (S_NK, "nsa_k_gain")):
                act.dma_start(s_rows[row:row + A[name].shape[1], :], A[name][0]).then_inc(small_in, 16)
            for row, name in ((S_FQ, "fox_q_gain"), (S_FK, "fox_k_gain"), (S_HO, "hgrn_o_gain"),
                              (S_NQ, "nsa_q_gain"), (S_MQ, "mem_q_gain"), (S_MK, "mem_k_gain")):
                act.dma_start(s_rows[row:row + A[name].shape[0], :], A[name]).then_inc(small_in, 16)

            def load_mtok(l):
                act.dma_start(mtok[l][:, :, :], A["mem"][0].rearrange("(a p) f -> p a f", p=P)).then_inc(mtok_in, 16)

            act.dma_start(wff[:, :, :], w_in0[:, :, FF_COL:FF_COL + 8]).then_inc(ff_w, 16)
            act.dma_start(fbias[0:1, :], A["fox_f_bias"]).then_inc(ff_w, 16)

            def split(p, more=0):
                if isinstance(more, int) and p >= TICKS:
                    return
                if p % 2 == 0:
                    act.wait_ge(raw_full[p // 2 % RAW], 16 * (p // 2 // RAW + 1) + more * 2)
                if p >= LEAD:
                    act.wait_ge(pieces_done, p - LEAD + 1 + more)
                nc.scalar.activation(w_hi[:, p % LEAD, :, :], raw[:, p // 2 % RAW, 2 * (p % 2):2 * (p % 2) + 2, :],
                                     ACT.Copy).then_inc(hi_ready, 1)

            TMP_FREE = {1: (hg_osum, 4), 2: (hn_sum, 6), 3: (u_ready, FB), 4: (hn_sum, 12), 5: (hn_sum, 14)}

            def square(n, c):
                if n == 0:
                    act.wait_ge(x_copied, c + 1)
                else:
                    act.wait_ge(x_ready, 4 * n + c // 2 + 1)
                if c == 0 and n in TMP_FREE:
                    act.wait_ge(*TMP_FREE[n])
                if c >= 2:
                    if c - 1 <= ADDED[n]:
                        act.wait_ge(sq_added, sum(ADDED[:n]) + c - 1)
                    else:
                        act.wait_ge(sq_used, USED[n] + c - 1 - ADDED[n])
                nc.scalar.activation(tmp[:, 2 * (c % 2):2 * (c % 2) + 2, :], xT[:, 2 * c:2 * c + 2, :],
                                     ACT.Square).then_inc(sq_ready, 1)

            def rms(n):
                act.wait_ge(sq_used, USED[n + 1])
                if n:
                    act.wait_ge(h_tmp, 8 * n)
                nc.scalar.activation(rinv[:, :], att[:, 3, 0:T], ACT.Sqrt, bias=eps[:, 0:1],
                                     scale=1.0 / D).then_inc(rms_ready, 1)

            def h_high(f, c, n):
                act.wait_ge(h_tmp, 8 * n + c + 1)
                nc.scalar.activation(h_hi[:, 2 * c:2 * c + 2, :], tmp[:, 2 * (c % 2):2 * (c % 2) + 2, :],
                                     ACT.Copy).then_inc(h_hi_ready, 1)

            def whole_norm(n, f):
                for c in range(8):
                    square(n, c)
                rms(n)
                for c in range(8):
                    h_high(f, c, n)

            def hn_square(i, src):
                act.wait_ge(hn_raw, i + 1)
                if i:
                    act.wait_ge(hn_sum, i)
                nc.scalar.activation(tmp[:, :, :], src, ACT.Square).then_inc(hn_sq, 1)

            def hn_root(i, b, query):
                act.wait_ge(hn_sum, i + 1)
                nc.scalar.activation(acc[:, b % 2, :], acc[:, b % 2, :], ACT.Sqrt,
                                     bias=eps[:, 1:2] if query else eps[:, 0:1],
                                     scale=1.0 if query else 1.0 / HD).then_inc(hn_rms, 1)

            def mem_squares(l, a):
                if a == 0:
                    act.wait_ge(mtok_in, 16 * (l + 1))
                else:
                    act.wait_ge(m_ssq, 2 * l + 1)
                nc.scalar.activation(memn[l][0][:, 0:8, :].rearrange("p k t -> p (k t)"), mtok[l][:, a, :],
                                     ACT.Square, accum_out=mss[:, a:a + 1]).then_inc(m_ssq, 1)

            def mem_rms(l):
                act.wait_ge(m_ssq, 2 * l + 2)
                nc.scalar.activation(mss[:, 2:4], mss[:, 0:2], ACT.Sqrt, bias=eps[:, 0:1],
                                     scale=1.0 / D).then_inc(m_rms, 1)

            def mem_high(l, c):
                act.wait_ge(m_turn, 8 * l + c + 1)
                for k in range(2):
                    g = G_IN + KT * l + 2 * c + k
                    last = nc.scalar.activation(memn[l][0][:, 2 * c + k, :], att[:, c % 2, k * T:(k + 1) * T],
                                                ACT.Copy, scale=G[:, g:g + 1])
                last.then_inc(m_hi, 1)

            act.wait_ge(consts, 7)
            for c in range(8):
                square(0, c)
            rms(0)
            for c in range(8):
                if c in (1, 3, 5):
                    split((c + 1) // 2)
                h_high(0, c, 0)
                if c == 0:
                    split(0)

            T0 = TICK["in0"]
            act.wait_ge(ff_w, 32)
            nc.scalar.activation(wff_hi[:, :, :], wff[:, :, :], ACT.Copy).then_inc(ff_whi, 1)

            def level(u):
                n, r = divmod(u, 2)
                p, l = divmod(n, LEVELS)
                if r == 0 and n < 4 * LEVELS and l > 0:
                    m = p * 8 + l - 1
                    act.wait_ge(hg_diff, m + 1)
                    nc.scalar.activation(decay[:, m % 2, :], decay[:, m % 2, :], ACT.Exp).then_inc(hg_decay, 1)
                o, r = divmod(u - 4, 2 * LEVELS)
                o -= 1
                if r == 1 and o >= 0:
                    act.wait_ge(hg_oraw, o + 1)
                    if o == 0:
                        act.wait_ge(h_ready, 8)
                    if o >= 2:
                        act.wait_ge(hn_sum, (1, 4)[o - 2])
                    nc.scalar.activation(tmp[:, 0:2, :], hq[:, 2 * o:2 * o + 2, :], ACT.Square).then_inc(hg_osq, 1)
                if r == 3 and o >= 0:
                    act.wait_ge(hg_osum, o + 1)
                    nc.scalar.activation(att[:, 3, :], att[:, 3, :], ACT.Sqrt, bias=eps[:, 0:1],
                                         scale=1.0 / HD).then_inc(hg_orms, 1)

            def fox_exp(u):
                act.wait_ge(f_nmax, u + 1)
                for a, cs in ((0, slice(0, P)), (1, slice(P, 384))):
                    last = nc.scalar.activation(fp[:, u % 4, cs], fp[:, u % 4, cs], ACT.Exp,
                                                bias=fst[:, u % 4, 2 + a:3 + a],
                                                accum_out=fst[:, u % 4, 4 + a:5 + a])
                last.then_inc(f_exp, 1)

            def fox_pt(u):
                act.wait_ge(f_t, u + 1)
                if u >= 2:
                    act.wait_ge(f_o, u - 1)
                nc.scalar.activation(fpt[:, u % 2, :], att[:, 2, 0:384], ACT.Copy).then_inc(f_pt, 1)

            def fox(v):
                if 0 <= v < FOX_HEADS:
                    fox_exp(v)
                if 0 <= v - 3 < FOX_HEADS:
                    fox_pt(v - 3)

            def fox_high(c):
                act.wait_ge(pieces_done, LAST_READ[1])
                if c >= 4:
                    act.wait_ge(hg_out, c - 3)
                    src = hq[:, 2 * c - 8:2 * c - 6, :]
                else:
                    act.wait_ge(f_out, 2 * c + 2)
                    src = fq[:, 2 * c:2 * c + 2, :]
                nc.scalar.activation(h_hi[:, 2 * c:2 * c + 2, :], src, ACT.Copy).then_inc(h_hi_ready, 1)

            for b, name in enumerate(IN0):
                for j in range(8):
                    t = T0 + 8 * b + j
                    done = IN0[b - 1] if b else None
                    k = KTH[b - 1] if b else 0
                    if j == 7 and name in ("hq", "hg"):
                        act.wait_ge(pieces_done, t + 1)
                        dst, ready = (hq, hg_q) if name == "hq" else (hg, hg_gate)
                        nc.scalar.activation(dst[:, 4 * KTH[b]:4 * KTH[b] + 4, :].rearrange("p a t -> p (a t)"),
                                             acc[:, b % 2, :], ACT.Silu).then_inc(ready, 1)
                    if done in ("fq", "fk") and j == 0:
                        act.wait_ge(hg_osum, {"fq0": 2, "fq1": 3, "fk0": 3, "fk1": 3}[done + str(k)])
                        hn_square(HN[done + str(k)], (fq if done == "fq" else fk)[:, 4 * k:4 * k + 4, :])
                    split(t + LEAD)
                    if j == 0 and done == "hf":
                        v = hb[:, 4 * k:4 * k + 4, :]
                        act.wait_ge(hg_z, k + 1)
                        nc.scalar.activation(v, hz[:, 4 * k:4 * k + 4, :], ACT.Abs).then_inc(hg_abs, 1)
                        act.wait_ge(hg_abs, 3 * k + 1)
                        nc.scalar.activation(v, v, ACT.Exp, scale=-1.0).then_inc(hg_abs, 1)
                        act.wait_ge(hg_abs, 3 * k + 2)
                        nc.scalar.activation(v, v, ACT.Ln, bias=1.0).then_inc(hg_abs, 1)
                    if j == 2 and done == "hf":
                        act.wait_ge(hg_kin, k + 1)
                        nc.scalar.activation(hz[:, 4 * k:4 * k + 4, :], hz[:, 4 * k:4 * k + 4, :],
                                             ACT.Exp).then_inc(hg_k, 1)
                    if b == 2 and j == 0:
                        act.wait_ge(ff_z, 1)
                        nc.scalar.activation(lf[:, 1, :], lf[:, 0, :], ACT.Abs).then_inc(ff_l, 1)
                        act.wait_ge(ff_l, 1)
                        nc.scalar.activation(lf[:, 1, :], lf[:, 1, :], ACT.Exp, scale=-1.0).then_inc(ff_l, 1)
                        act.wait_ge(ff_l, 2)
                        nc.scalar.activation(lf[:, 1, :], lf[:, 1, :], ACT.Ln, bias=1.0).then_inc(ff_l, 1)
                    if done in ("fq", "fk") and j == 2:
                        hn_root(HN[done + str(k)], b + 1, done == "fq")
                    if 8 * b + j >= HG_START:
                        level(8 * b + j - HG_START)
                    fox(8 * b + j - FOX_START)

            def nsa_exp(u):
                act.wait_ge(n_nmax, u + 1)
                for a, cs in ((0, slice(0, P)), (1, slice(P, 384))):
                    for br in range(2):
                        c = 3 * a + 2 - br
                        nc.scalar.activation(np_[:, u % 2, br, cs], np_[:, u % 2, br, cs], ACT.Exp,
                                             bias=nst[:, u % 2, 1, c:c + 1], accum_out=nst[:, u % 2, 2, c:c + 1])
                    last = nc.scalar.activation(npc[:, u % 2, a, 0:N_CMP], npc[:, u % 2, a, 0:N_CMP], ACT.Exp,
                                                bias=nst[:, u % 2, 1, 3 * a:3 * a + 1],
                                                accum_out=nst[:, u % 2, 2, 3 * a:3 * a + 1])
                last.then_inc(n_exp, 1)

            def nsa_pt(u, br):
                act.wait_ge(n_t, 2 * u + br + 1)
                if u:
                    act.wait_ge(n_o, u)
                nc.scalar.activation(npt[:, br, :], att[:, 2, 0:384], ACT.Copy).then_inc(n_pt, 1)

            def nsa(v):
                u, r = divmod(v, 2)
                if r == 0 and 0 <= u - 2 < NSA_HEADS:
                    nsa_pt(u - 2, 1)
                if r == 0 and 0 <= u < NSA_HEADS:
                    nsa_exp(u)
                if r == 1 and 0 <= u - 1 < NSA_HEADS:
                    nsa_pt(u - 1, 0)

            def nsa_high(c):
                act.wait_ge(n_out, 2 * c + 2)
                act.wait_ge(pieces_done, LAST_READ[5])
                nc.scalar.activation(h_hi[:, 2 * c:2 * c + 2, :], nq[:, 2 * c:2 * c + 2, :],
                                     ACT.Copy).then_inc(h_hi_ready, 1)

            def memory(l):
                n0 = 3 * l
                t0 = TICK[f"out{l}"]
                if l == 0:
                    fox_high(4)
                    fox_high(5)
                for t in range(32):
                    split(t0 + t + LEAD)
                    if l == 0:
                        fox(112 + t - FOX_START)
                        if t in FOX_CHUNK:
                            fox_high(FOX_CHUNK[t])
                        if t == 0:
                            act.wait_ge(hg_merged, 4 * LEVELS)
                            load_mtok(0)
                        if t == 6:
                            act.wait_ge(hg_out, 4)
                            mem_squares(0, 0)
                        if t == 7:
                            mem_squares(0, 1)
                            mem_rms(0)
                        if 0 <= t - MEM_START < 8:
                            mem_high(0, t - MEM_START)
                    else:
                        if t == 0:
                            hn_root(HN["q3"], BLOCK["q"] + 3, True)
                        for v in nsa_ticks(t):
                            nsa(v)
                        if t in NSA_CHUNK:
                            nsa_high(NSA_CHUNK[t])
                    if t in OUT_SQUARES:
                        square(n0 + 1, OUT_SQUARES[t])
                        square(n0 + 1, OUT_SQUARES[t] + 1)
                for t in range(8):
                    if t == 0:
                        square(n0 + 1, 6)
                        square(n0 + 1, 7)
                    split(TICK[f"kvk{l}"] + t + LEAD)
                    if t == 0:
                        rms(n0 + 1)
                    if t in NORM_CHUNKS:
                        for c in range(*NORM_CHUNKS[t]):
                            h_high(FILL[f"wq{l}"], c, n0 + 1)
                for t in range(8):
                    if t == 0:
                        act.wait_ge(h_ready, 8 * FILL[f"wq{l}"] + 8)
                        hn_square(HN[f"mk{l}"], mk[:, :, :])
                    split(TICK[f"wq{l}"] + t + LEAD)
                    if t == 1:
                        hn_root(HN[f"mk{l}"], BLOCK[f"kvk{l}"], False)
                    if t == 7:
                        hn_square(HN[f"mq{l}"], mq[:, :, :])

                def m_exps(u):
                    act.wait_ge(m_nmax, MEM_HEADS * l + u + 1)
                    for a in range(2):
                        last = nc.scalar.activation(mp[:, u, a, :], att[:, u % 2, a * T:(a + 1) * T], ACT.Exp,
                                                    bias=mst[:, u, 2 + a:3 + a],
                                                    accum_out=mst[:, u, 4 + a:5 + a])
                    last.then_inc(m_exp, 1)

                def m_turned(u):
                    act.wait_ge(m_t, MEM_HEADS * l + u + 1)
                    nc.scalar.activation(mpt[:, u, :, :], att[:, (2, 0)[u % 2], :].rearrange("p (a q) -> p a q", a=2),
                                         ACT.Copy).then_inc(m_pt, 1)

                def m_high(u):
                    act.wait_ge(m_o, MEM_HEADS * l + u + 1)
                    nc.scalar.activation(mo_hi[:, u, :], att[:, (3, 1)[u % 2], 0:T], ACT.Copy).then_inc(m_ohi, 1)

                for t in range(MEM_TICKS):
                    if t < 8:
                        split(TICK[f"kvv{l}"] + t + LEAD)
                    if t == 0:
                        hn_root(HN[f"mq{l}"], BLOCK[f"wq{l}"], True)
                    if 0 <= t - 3 < MEM_HEADS:
                        m_exps(t - 3)
                    if 0 <= t - 6 < MEM_HEADS:
                        m_turned(t - 6)
                    if 0 <= t - 8 < MEM_HEADS:
                        m_high(t - 8)
                t0 = TICK[f"wo{l}"]
                for t in range(8):
                    if t % 2 == 0 and t:
                        square(n0 + 2, t - 2)
                        square(n0 + 2, t - 1)
                    split(t0 + t + LEAD)
                square(n0 + 2, 6)
                square(n0 + 2, 7)
                rms(n0 + 2)
                for c in range(8):
                    h_high(FILL[f"up{l}"], c, n0 + 2)
                t0 = TICK[f"up{l}"]
                b0 = BLOCK[f"up{l}"]
                act.wait_ge(h_ready, 8 * FILL[f"up{l}"] + 8)

                def silu(more):
                    act.wait_ge(pieces_done, t0 + 8 + more * 16)
                    if l or not isinstance(more, int):
                        act.wait_ge(u_ready, FB * l + more)
                    nc.scalar.activation(tmp[:, :, :].rearrange("p k t -> p (k t)"), acc[:, b0 % 2, :],
                                         ACT.Silu).then_inc(u_silu, 1)

                for t in range(16):
                    if t == 7:
                        silu(0)
                    split(t0 + t + LEAD)
                with act.Fori(1, FB) as i:
                    for t in range(16):
                        if t == 7:
                            silu(i)
                        split(t0 + t + LEAD, i * 16)
                for half in range(2):
                    t0 = TICK[f"dn{l}"] + 44 * half
                    for t in range(4):
                        if l == 0 and half and t % 2 == 0:
                            square(3, t)
                            square(3, t + 1)
                        split(t0 + t + LEAD)
                    with act.Fori(0, 4) as i:
                        for t in range(8):
                            split(t0 + 4 + t + LEAD, i * 8)
                    for t in range(8):
                        if l == 0 and half and t == 6:
                            square(3, 4)
                        split(t0 + 36 + t + LEAD)
                    if l == 0 and half:
                        for c in range(5, 8):
                            square(3, c)

            memory(0)
            rms(3)
            for c in range(8):
                h_high(4, c, 3)
            act.wait_ge(pieces_done, TICK["kcvc"])
            load_mtok(1)
            act.dma_start(w2c[:, 0, :, :], A["cmp_w2_k"][0].rearrange("(a p) d -> p a d", p=P)).then_inc(c_w2, 16)
            act.dma_start(w2c[:, 1, :, :], A["cmp_w2_v"][0].rearrange("(a p) d -> p a d", p=P)).then_inc(c_w2, 16)
            act.dma_start(wgt[:, :, :], w_in1[:, :, GT_COL:GT_COL + 48]).then_inc(n_w, 16)
            for t in range(16):
                if t == 3:
                    act.wait_ge(n_w, 16)
                    nc.scalar.activation(wgt_hi[:, :, :], wgt[:, :, :], ACT.Copy).then_inc(n_whi, 1)
                if t == 9:
                    act.wait_ge(n_gsum, 1)
                    nc.scalar.activation(gateT[:, :], att[0:48, 0, 0:T], ACT.Sigmoid).then_inc(n_gateT, 1)
                if t == 12:
                    act.wait_ge(c_x, 1)
                    nc.scalar.activation(xc_hi[0][:, :, 0:CMP_COLS], xc[:, :, 0:CMP_COLS], ACT.Copy).then_inc(c_hi, 1)
                split(TICK["kcvc"] + t + LEAD)
            for t in range(16):
                if t == 4:
                    act.wait_ge(c_x, 2)
                    nc.scalar.activation(xc_hi[1][:, :, 0:CMP_COLS], xc[:, :, 0:CMP_COLS], ACT.Copy).then_inc(c_hi, 1)
                if t % 8 == 7:
                    b = BLOCK["cmp"] + t // 8
                    act.wait_ge(pieces_done, TICK["cmp"] + t + 1)
                    nc.scalar.activation(hrow[:, t // 8, :], acc[0:CMP_COLS, b % 2, 0:2 * P],
                                         ACT.Gelu_apprx_tanh).then_inc(c_row, 1)
                if t == 10:
                    act.wait_ge(c_kraw, 1)
                    nc.scalar.activation(kcr[:, 0:CMP_COLS], kcmp[:, 0:CMP_COLS], ACT.Square).then_inc(c_ksq, 1)
                if t == 11:
                    act.wait_ge(c_ksum, 2)
                    nc.scalar.activation(kcr[:, 0:CMP_COLS], att[:, 2, 256:256 + CMP_COLS], ACT.Sqrt,
                                         bias=eps[:, 0:1], scale=1.0 / HD).then_inc(c_krms, 1)
                if t == 12:
                    mem_squares(1, 0)
                if t == 13:
                    mem_squares(1, 1)
                    mem_rms(1)
                split(TICK["cmp"] + t + LEAD)
            act.wait_ge(h_ready, 8 * 4 + 8)
            for t in range(32):
                b = BLOCK["kvs"] + t // 8 - 1
                if 1 <= t < 9:
                    mem_high(1, t - 1)
                for k, name, dst in ((1, "kw", kw), (2, "ks", ks)):
                    if t == 8 * k:
                        hn_square(HN[name], dst[:, :, :])
                    if t == 8 * k + 2:
                        hn_root(HN[name], b, False)
                split(TICK["kvs"] + t + LEAD)

            for t in range(32):
                split(TICK["q"] + t + LEAD)
                if t % 8 == 0 and t:
                    hn_root(HN[f"q{t // 8 - 1}"], BLOCK["q"] + t // 8 - 1, True)
                if t == 31:
                    nsa_high(0)
                    nsa_high(1)
                if t % 8 == 7:
                    hn_square(HN[f"q{t // 8}"], nq[:, t // 2 - 3:t // 2 + 1, :])
                nsa(t - NSA_START)
            memory(1)
            for g in range(8):
                act.wait_ge(out_turn, g + 1)
                b, a = divmod(g, 2)
                nc.scalar.activation(otok[:, a, b * NB:(b + 1) * NB], att[:, g % 4, :],
                                     ACT.Copy).then_inc(out_copied, 1)

        @block.vector
        def _(dve):
            def split(p, more=0):
                if isinstance(more, int) and p >= TICKS:
                    return
                dve.wait_ge(hi_ready, p + 1 + more)
                nc.vector.tensor_tensor(w_lo[:, p % LEAD, :, :],
                                        raw[:, p // 2 % RAW, 2 * (p % 2):2 * (p % 2) + 2, :],
                                        w_hi[:, p % LEAD, :, :].bitcast(F32), ALU.subtract).then_inc(lo_ready, 1)

            def invert(n):
                dve.wait_ge(rms_ready, n + 1)
                nc.vector.reciprocal(rinv[:, :], rinv[:, :]).then_inc(rinv_ready, 1)
                dve.wait_ge(rinv_ready, n + 1)

            def h_scaled(n, c, gain):
                for k in range(2):
                    kt = 2 * c + k
                    last = nc.vector.scalar_tensor_tensor(out=tmp[:, 2 * (c % 2) + k, :], in0=xT[:, kt, :],
                                                          scalar=G[:, gain + kt:gain + kt + 1], in1=rinv[:, :],
                                                          op0=ALU.mult, op1=ALU.mult)
                last.then_inc(h_tmp, 1)

            def h_low(f, c, src):
                dve.wait_ge(h_hi_ready, 8 * f + FILL_ORDER[f].index(c) + 1)
                nc.vector.tensor_tensor(h_lo[:, 2 * c:2 * c + 2, :], src, h_hi[:, 2 * c:2 * c + 2, :].bitcast(F32),
                                        ALU.subtract).then_inc(h_ready, 1)

            def norm(n, f, gain, lo=0, hi=8):
                if lo == 0:
                    invert(n)
                    if LAST_READ[f]:
                        dve.wait_ge(pieces_done, LAST_READ[f])
                for c in range(lo, hi + (hi == 8)):
                    if c < 8:
                        if c >= 2:
                            dve.wait_ge(h_ready, 8 * f + c - 1)
                        h_scaled(n, c, gain)
                    if c:
                        h_low(f, c - 1, tmp[:, 2 * ((c - 1) % 2):2 * ((c - 1) % 2) + 2, :])

            def freed(b, ready, count):
                dve.wait_ge(ready, count)
                dve.sem_inc(acc_free[b % 2], 1)

            def hn_take(i, b, dst, last_t):
                dve.wait_ge(pieces_done, last_t + 1)
                nc.vector.tensor_copy(dst.rearrange("p a t -> p (a t)"), acc[:, b % 2, :]).then_inc(hn_raw, 1)

            def hn_scale(i, b, half, dst, gain):
                rms = acc[:, b % 2, half * NB:(half + 1) * NB]
                v = dst[:, 2 * half:2 * half + 2, :].rearrange("p a t -> p (a t)")
                dve.wait_ge(hn_rms, i + 1)
                nc.vector.reciprocal(rms, rms).then_inc(hn_rinv, 1)
                dve.wait_ge(hn_rinv, 2 * i + half + 1)
                nc.vector.scalar_tensor_tensor(out=v, in0=v, scalar=S[:, gain:gain + 1], in1=rms, op0=ALU.mult,
                                               op1=ALU.mult).then_inc(hn_out, 1)
                if half:
                    freed(b, hn_out, 2 * i + 2)

            def mem_scale(l, a):
                if a == 0:
                    dve.wait_ge(m_rms, l + 1)
                    nc.vector.reciprocal(mss[:, 2:4], mss[:, 2:4]).then_inc(m_rinv, 1)
                    dve.wait_ge(m_rinv, l + 1)
                nc.vector.tensor_scalar(mtok[l][:, a, :], mtok[l][:, a, :], mss[:, 2 + a:3 + a], None,
                                        ALU.mult).then_inc(m_scaled, 1)

            def mem_low(l, c):
                dve.wait_ge(m_hi, 8 * l + c + 1)
                for k in range(2):
                    g = G_IN + KT * l + 2 * c + k
                    last = nc.vector.scalar_tensor_tensor(out=memn[l][1][:, 2 * c + k, :],
                                                          in0=att[:, c % 2, k * T:(k + 1) * T],
                                                          scalar=G[:, g:g + 1],
                                                          in1=memn[l][0][:, 2 * c + k, :].bitcast(F32),
                                                          op0=ALU.mult, op1=ALU.subtract)
                last.then_inc(m_ready, 1)

            for c in range(8):
                dve.wait_ge(x_turn, c + 1)
                nc.vector.tensor_copy(xT[:, 2 * c:2 * c + 2, :],
                                      att[:, c % 3, :].rearrange("p (k t) -> p k t", k=2)).then_inc(x_copied, 1)
                if c % 2:
                    dve.wait_ge(x_copied, c + 1)
                    dve.sem_inc(x_ready, 1)
            dve.wait_ge(gains_t, 2)
            nc.vector.tensor_copy(G[:, :], att[:, 0, 0:P]).then_inc(gains, 1)
            nc.vector.tensor_copy(S[:, :], att[:, 1, 0:S_ROWS]).then_inc(gains, 1)
            dve.wait_ge(gains, 2)
            norm(0, 0, G_MIX, 0, 1)
            split(0)
            norm(0, 0, G_MIX, 1, 2)
            for p in (1, 2, 3):
                split(p)
                norm(0, 0, G_MIX, 2 * p, 2 * p + 2)
            nc.vector.memset(AT[:, :, :], 0.0).then_inc(hg_zero, 1)

            T0 = TICK["in0"]
            dve.wait_ge(ff_whi, 1)
            nc.vector.tensor_tensor(wff_lo[:, :, :], wff[:, :, :], wff_hi[:, :, :].bitcast(F32),
                                    ALU.subtract).then_inc(ff_wlo, 1)

            def heads(x, p):
                return x[:, 2 * p:2 * p + 2, :].rearrange("p a t -> p (a t)")

            def level(u):
                n, r = divmod(u, 2)
                if r == 0 and 2 <= n <= 4 * LEVELS + 1:
                    n -= 1
                    p, l = divmod(n - 1, LEVELS)
                    dve.wait_ge(hg_scores, n)
                    if l == 0:
                        dve.wait_ge(lmask_ready, 1)
                        dve.wait_ge(hg_zero, 1)
                        if p:
                            dve.wait_ge(hg_o, p)
                    else:
                        dve.wait_ge(hg_merged, n - 1)
                    if l < 8:
                        last = nc.vector.copy_predicated(AT[:, 0:4, :], lmask[:, l:l + 1, :].broadcast_to([P, 4, P]),
                                                         att[:, (n - 1) % 2, :].rearrange("p (a t) -> p a t", a=4))
                    else:
                        last = nc.vector.tensor_copy(AT[:, 4:6, :], att[:, (n - 1) % 2, 0:T].rearrange("p (a t) -> p a t", a=2))
                    last.then_inc(hg_merged, 1)
                    n += 1
                p, l = divmod(n, LEVELS)
                m = p * 8 + l - 1
                if r == 0 and n < 4 * LEVELS and l > 0:
                    dve.wait_ge(hg_b, p // 2 + 1)
                    if m == 0:
                        dve.wait_ge(lmask_ready, 1)
                    if m >= 2:
                        dve.wait_ge(hg_qd, m - 1)
                        dve.wait_ge(hg_kd, m - 1)
                    e = decay[:, m % 2, :]
                    b = heads(hb, p)
                    if l < 8:
                        h = 1 << (l - 1)
                        ev = e.rearrange("p (n a h) -> p n a h", a=2, h=h)
                        bv = b.rearrange("p (n a h) -> p n a h", a=2, h=h)
                        mid = bv[:, :, 0, h - 1:h].broadcast_to([P, T // h, h])
                        nc.vector.tensor_tensor(ev[:, :, 0, :], mid, bv[:, :, 0, :], ALU.subtract)
                        last = nc.vector.tensor_tensor(ev[:, :, 1, :], bv[:, :, 1, :], mid, ALU.subtract)
                    else:
                        ev = e.rearrange("p (n a h) -> p n a h", a=2, h=P)
                        bv = b.rearrange("p (n a h) -> p n a h", a=2, h=P)
                        mid = bv[:, :, 0, P - 1:P].broadcast_to([P, 2, P])
                        nc.vector.tensor_tensor(ev[:, :, 0, :], mid, bv[:, :, 0, :], ALU.subtract)
                        last = nc.vector.tensor_copy(ev[:, :, 1, :], bv[:, :, 1, :])
                    last.then_inc(hg_diff, 1)
                if r == 1 and n < 4 * LEVELS and l > 0:
                    dve.wait_ge(hg_decay, m + 1)
                    if m >= 2:
                        dve.wait_ge(hg_scores, (m - 2) // 8 * 9 + (m - 2) % 8 + 2)
                    nc.vector.tensor_tensor(kd[:, m % 2, :], heads(hz, p), decay[:, m % 2, :],
                                            ALU.mult).then_inc(hg_kd, 1)
                o, r = divmod(u - 4, 2 * LEVELS)
                o -= 1
                if r == 1 and o >= 0:
                    dve.wait_ge(hg_o, o + 1)
                    nc.vector.tensor_copy(heads(hq, o), att[:, 2, :]).then_inc(hg_oraw, 1)
                if r == 4 and o >= 0:
                    dve.wait_ge(hg_orms, o + 1)
                    nc.vector.reciprocal(att[:, 3, :], att[:, 3, :]).then_inc(hg_orinv, 1)
                    dve.wait_ge(hg_orinv, o + 1)
                    dve.wait_ge(hg_oraw, o + 1)
                    nc.vector.scalar_tensor_tensor(out=heads(hq, o), in0=heads(hq, o), scalar=S[:, S_HO:S_HO + 1],
                                                   in1=att[:, 3, :], op0=ALU.mult, op1=ALU.mult).then_inc(hg_onorm, 1)

            def fox_max(u):
                if u == 0:
                    dve.wait_ge(fmask_ready, 2)
                dve.wait_ge(f_s, u + 1)
                if u >= 4:
                    dve.wait_ge(f_t, u - 3)
                st = fst[:, u % 4, :]
                for a, w, cs in ((0, P, slice(0, P)), (1, T, slice(P, 384))):
                    last = nc.vector.tensor_tensor_reduce(fp[:, u % 4, cs], att[:, u % 2, cs],
                                                          fmask[:, T - w:T], 1.0, NEG, ALU.add, ALU.max,
                                                          st[:, a:a + 1])
                last.then_inc(f_max, 1)
                dve.wait_ge(f_max, u + 1)
                nc.vector.tensor_scalar(st[:, 2:4], st[:, 0:2], -1.0, None, ALU.mult).then_inc(f_nmax, 1)

            def fox_rz(u):
                dve.wait_ge(f_exp, u + 1)
                nc.vector.reciprocal(fst[:, u % 4, 6:8], fst[:, u % 4, 4:6]).then_inc(f_rz, 1)

            def fox_take(u):
                dve.wait_ge(f_o, u + 1)
                nc.vector.tensor_copy(fq[:, u, :], att[:, 3, 0:T]).then_inc(f_out, 1)

            def fox(v):
                if 0 <= v < FOX_HEADS:
                    fox_max(v)
                if 0 <= v - 1 < FOX_HEADS:
                    fox_rz(v - 1)
                if 0 <= v - 4 < FOX_HEADS:
                    fox_take(v - 4)

            def fox_low(c):
                h_low(1, c, hq[:, 2 * c - 8:2 * c - 6, :] if c >= 4 else fq[:, 2 * c:2 * c + 2, :])

            for b, name in enumerate(IN0):
                for j in range(8):
                    t = T0 + 8 * b + j
                    par = b % 2
                    done = IN0[b - 1] if b else None
                    k = KTH[b - 1] if b else 0
                    kk = KTH[b]
                    if j == 7:
                        if name in ("fq", "fk"):
                            hn_take(HN[name + str(kk)], b, (fq if name == "fq" else fk)[:, 4 * kk:4 * kk + 4, :], t)
                        if name in ("hf", "hi", "fv"):
                            dve.wait_ge(pieces_done, t + 1)
                            if name == "hf":
                                last = nc.vector.tensor_copy(hz[:, 4 * kk:4 * kk + 4, :].rearrange("p a t -> p (a t)"),
                                                             acc[:, par, :])
                                ready = hg_z
                            else:
                                dst, ready = (hv, hg_v) if name == "hi" else (fv, f_v)
                                last = nc.vector.tensor_copy(dst[:, :, kk * NB:(kk + 1) * NB],
                                                             acc[:, par, :].rearrange("p (a n) -> p a n", a=2))
                            last.then_inc(ready, 1)
                            dve.wait_ge(ready, kk + 1)
                            dve.sem_inc(acc_free[par], 1)
                        if name in ("hq", "hg"):
                            dve.wait_ge(hg_q if name == "hq" else hg_gate, kk + 1)
                            dve.sem_inc(acc_free[par], 1)
                    if j == 1 and done == "hf":
                        v = hb[:, 4 * k:4 * k + 4, :]
                        z = hz[:, 4 * k:4 * k + 4, :]
                        dve.wait_ge(hg_abs, 3 * k + 3)
                        nc.vector.scalar_tensor_tensor(out=v, in0=z, scalar=0.0, in1=v, op0=ALU.min,
                                                       op1=ALU.subtract).then_inc(hg_lf, 1)
                        dve.wait_ge(hg_lf, k + 1)
                        nc.vector.tensor_tensor(z, v, z, ALU.subtract).then_inc(hg_kin, 1)
                        dve.wait_ge(hg_kin, k + 1)
                        for i in range(8):
                            bl = hb[:, 4 * k + i // 2, i % 2 * P:(i % 2 + 1) * P]
                            last = nc.vector.tensor_tensor_scan(bl, ones[:, :], bl, 0.0, ALU.mult, ALU.add)
                        last.then_inc(hg_b, 1)
                    if b == 1 and j == 7:
                        dve.wait_ge(ff_sum, 1)
                        nc.vector.tensor_copy(lf[:, 0, :], att[0:FOX_HEADS, 0, 0:T]).then_inc(ff_z, 1)
                    if b == 2 and j == 1:
                        dve.wait_ge(ff_l, 3)
                        nc.vector.scalar_tensor_tensor(out=lf[:, 1, :], in0=lf[:, 0, :], scalar=0.0,
                                                       in1=lf[:, 1, :], op0=ALU.min,
                                                       op1=ALU.subtract).then_inc(ff_lf, 1)
                    if b == 3 and j == 0:
                        dve.wait_ge(ff_lf, 1)
                        nc.vector.tensor_tensor_scan(lf[:, 0, :], ones[0:FOX_HEADS, 0:1].broadcast_to([FOX_HEADS, T]),
                                                     lf[:, 1, :], 0.0, ALU.mult, ALU.add).then_inc(ff_c, 1)
                        dve.wait_ge(ff_c, 1)
                        nc.vector.tensor_scalar(cneg[:, :], lf[:, 0, :], -1.0, None,
                                                ALU.mult).then_inc(ff_cneg, 1)
                    if done in ("fq", "fk") and j in (3, 5):
                        hn_scale(HN[done + str(k)], b - 1, j // 4, (fq if done == "fq" else fk)[:, 4 * k:4 * k + 4, :],
                                 S_FQ if done == "fq" else S_FK)
                    if 8 * b + j >= HG_START:
                        level(8 * b + j - HG_START)
                    fox(8 * b + j - FOX_START)
                    split(t + LEAD)

            def residual(k, b, last_t):
                dve.wait_ge(pieces_done, last_t + 1)
                v = xT[:, 4 * k:4 * k + 4, :].rearrange("p a t -> p (a t)")
                nc.vector.tensor_tensor(v, v, acc[:, b % 2, :], ALU.add).then_inc(x_ready, 1)

            def nsa_max(u):
                slope = 2.0 ** (-8.0 * (u + 1) / NSA_HEADS)
                dve.wait_ge(n_s, u + 1)
                if u >= 2:
                    dve.wait_ge(n_t, 2 * u - 2)
                    dve.wait_ge(n_tc, u - 1)
                for br in range(2):
                    nc.vector.scalar_tensor_tensor(out=np_[:, u % 2, br, :], in0=dm[:, :], scalar=slope,
                                                   in1=att[:, br, 0:384], op0=ALU.mult, op1=ALU.add)
                last = nc.vector.scalar_tensor_tensor(out=npc[:, u % 2, :, 0:N_CMP], in0=dmc[:, :, 0:N_CMP], scalar=slope,
                                                      in1=att[:, 0, 384:416].rearrange("p (a n) -> p a n", a=2)[:, :, 0:N_CMP],
                                                      op0=ALU.mult, op1=ALU.add)
                last.then_inc(n_p, 1)
                dve.wait_ge(n_p, u + 1)
                for a, cs in ((0, slice(0, P)), (1, slice(P, 384))):
                    for br in range(2):
                        c = 3 * a + 2 - br
                        nc.vector.tensor_reduce(nst[:, u % 2, 0, c:c + 1], np_[:, u % 2, br, cs], AX_X, ALU.max)
                    last = nc.vector.tensor_reduce(nst[:, u % 2, 0, 3 * a:3 * a + 1], npc[:, u % 2, a, 0:N_CMP], AX_X, ALU.max)
                last.then_inc(n_max, 1)
                dve.wait_ge(n_max, u + 1)
                nc.vector.tensor_scalar(nst[:, u % 2, 1, 0:6], nst[:, u % 2, 0, 0:6], -1e20, -1.0, ALU.max,
                                        ALU.mult).then_inc(n_nmax, 1)

            def nsa_rz(u):
                dve.wait_ge(n_exp, u + 1)
                nc.vector.tensor_scalar(nst[:, u % 2, 2, 0:6], nst[:, u % 2, 2, 0:6], 1e-30, None, ALU.max).then_inc(n_rzs, 1)
                dve.wait_ge(n_rzs, 2 * u + 1)
                nc.vector.reciprocal(nst[:, u % 2, 2, 0:6], nst[:, u % 2, 2, 0:6]).then_inc(n_rzs, 1)
                dve.wait_ge(n_rzs, 2 * u + 2)
                nc.vector.tensor_tensor(nst[:, u % 2, 3, 0:6].rearrange("p (a b) -> p a b", a=2),
                                        nst[:, u % 2, 2, 0:6].rearrange("p (a b) -> p a b", a=2),
                                        gate[:, :, 3 * u:3 * u + 3], ALU.mult).then_inc(n_rz, 1)

            def nsa_ptc(u):
                dve.wait_ge(n_tc, u + 1)
                nc.vector.tensor_copy(nptc[:, :, :], att[0:N_CMP, 3, T:2 * T].rearrange("p (a q) -> p a q", a=2)).then_inc(n_ptc, 1)

            def nsa_take(u):
                dve.wait_ge(n_o, u + 1)
                nc.vector.tensor_copy(nq[:, u, :], att[:, 3, 0:T]).then_inc(n_out, 1)

            def nsa(v):
                u, r = divmod(v, 2)
                if r == 0 and 0 <= u < NSA_HEADS:
                    nsa_max(u)
                if r == 0 and 0 <= u - 2 < NSA_HEADS:
                    nsa_ptc(u - 2)
                if r == 1 and 0 <= u < NSA_HEADS:
                    nsa_rz(u)
                if r == 1 and 0 <= u - 2 < NSA_HEADS:
                    nsa_take(u - 2)

            def nsa_low(c):
                h_low(5, c, nq[:, 2 * c:2 * c + 2, :])

            def q_scale(k, half):
                hn_scale(HN[f"q{k}"], BLOCK["q"] + k, half, nq[:, 4 * k:4 * k + 4, :], S_NQ)

            def memory(l):
                n0 = 3 * l
                if l == 0:
                    fox_low(4)
                    fox_low(5)
                for t in range(32):
                    if l == 0:
                        fox(112 + t - FOX_START)
                        if t in FOX_CHUNK:
                            fox_low(FOX_CHUNK[t])
                        if t in (8, 9):
                            mem_scale(0, t - 8)
                        if 0 <= t - MEM_START < 8:
                            mem_low(0, t - MEM_START)
                    else:
                        if t < 2:
                            q_scale(3, t)
                        for v in nsa_ticks(t):
                            nsa(v)
                        if t in NSA_CHUNK:
                            nsa_low(NSA_CHUNK[t])
                    if t in OUT_LAST:
                        k = OUT_LAST.index(t)
                        b = BLOCK[f"out{l}"] + k
                        residual(k, b, TICK[f"out{l}"] + t)
                        freed(b, x_ready, 4 * (n0 + 1) + k + 1)
                    split(TICK[f"out{l}"] + t + LEAD)
                for t in range(8):
                    if t < 7:
                        split(TICK[f"kvk{l}"] + t + LEAD)
                    if t in NORM_CHUNKS:
                        norm(n0 + 1, FILL[f"wq{l}"], G_MEM + KT * l, *NORM_CHUNKS[t])
                    if t == 7:
                        hn_take(HN[f"mk{l}"], BLOCK[f"kvk{l}"], mk[:, :, :], TICK[f"kvk{l}"] + 7)
                        split(TICK[f"kvk{l}"] + t + LEAD)
                for t in range(8):
                    if t in (1, 3):
                        hn_scale(HN[f"mk{l}"], BLOCK[f"kvk{l}"], t // 2, mk[:, :, :], S_MK + l)
                    if t == 7:
                        hn_take(HN[f"mq{l}"], BLOCK[f"wq{l}"], mq[:, :, :], TICK[f"wq{l}"] + 7)
                    split(TICK[f"wq{l}"] + t + LEAD)

                def m_maxes(u):
                    n = MEM_HEADS * l + u
                    dve.wait_ge(m_s, n + 1)
                    nc.vector.tensor_reduce(mst[:, u, 2:4], att[:, u % 2, :].rearrange("p (a t) -> p a t", a=2), AX_X,
                                            ALU.max, negate=True).then_inc(m_nmax, 1)

                def m_inv(u):
                    dve.wait_ge(m_exp, MEM_HEADS * l + u + 1)
                    nc.vector.reciprocal(mst[:, u, 6:8], mst[:, u, 4:6]).then_inc(m_rz, 1)

                def m_low(u):
                    dve.wait_ge(m_ohi, MEM_HEADS * l + u + 1)
                    nc.vector.tensor_tensor(mo_lo[:, u, :], att[:, (3, 1)[u % 2], 0:T], mo_hi[:, u, :].bitcast(F32),
                                            ALU.subtract).then_inc(m_out, 1)

                for t in range(MEM_TICKS):
                    if t in (0, 2):
                        hn_scale(HN[f"mq{l}"], BLOCK[f"wq{l}"], t // 2, mq[:, :, :], S_MQ + l)
                    if t == 7:
                        dve.wait_ge(pieces_done, TICK[f"kvv{l}"] + 8)
                        nc.vector.tensor_copy(mv[:, :, :], acc[:, BLOCK[f"kvv{l}"] % 2, :].rearrange("p (a n) -> p a n", a=2)).then_inc(m_v, 1)
                        freed(BLOCK[f"kvv{l}"], m_v, l + 1)
                    if 0 <= t - 3 < MEM_HEADS:
                        m_maxes(t - 3)
                    if 0 <= t - 4 < MEM_HEADS:
                        m_inv(t - 4)
                    if 0 <= t - 8 < MEM_HEADS:
                        m_low(t - 8)
                    if t < 8:
                        split(TICK[f"kvv{l}"] + t + LEAD)
                for t in range(8):
                    if t % 2 == 1:
                        b = BLOCK[f"wo{l}"] + t // 2
                        residual(t // 2, b, TICK[f"wo{l}"] + t)
                        freed(b, x_ready, 4 * (n0 + 2) + t // 2 + 1)
                    split(TICK[f"wo{l}"] + t + LEAD)
                norm(n0 + 2, FILL[f"up{l}"], G_FFN + KT * l)
                t0, b0 = TICK[f"up{l}"], BLOCK[f"up{l}"]
                flat = tmp[:, :, :].rearrange("p k t -> p (k t)")
                with dve.Fori(0, FB) as i:
                    for t in range(16):
                        if t == 7:
                            dve.wait_ge(u_silu, i + FB * l + 1)
                            dve.sem_inc(acc_free[b0 % 2], 1)
                        if t == 15:
                            dve.wait_ge(pieces_done, i * 16 + t0 + 16)
                            nc.vector.tensor_tensor(flat, flat, acc[:, (b0 + 1) % 2, :], ALU.mult).then_inc(u_prod, 1)
                            dve.wait_ge(u_prod, i + FB * l + 1)
                            dve.sem_inc(acc_free[(b0 + 1) % 2], 1)
                        split(t0 + t + LEAD, i * 16)
                for half in range(2):
                    t0, b0 = TICK[f"dn{l}"] + 44 * half, BLOCK[f"dn{l}"] + 2 * half
                    for t in range(4):
                        split(t0 + t + LEAD)
                    with dve.Fori(0, 4) as i:
                        for t in range(8):
                            split(t0 + 4 + t + LEAD, i * 8)
                    for t in range(8):
                        if t in (5, 7):
                            b = t // 7
                            residual(2 * half + b, b0 + b, t0 + 36 + t)
                            freed(b0 + b, x_ready, 4 * (n0 + 3) + 2 * half + b + 1)
                        split(t0 + 36 + t + LEAD)

            def hidden_turned(v):
                dve.wait_ge(c_turn, v + 1)
                nc.vector.tensor_copy(hidc[:, v, :, 0:CMP_COLS],
                                      att[:, 2, 0:128].rearrange("p (a n) -> p a n", a=2)[:, :, 0:CMP_COLS]).then_inc(c_hid, 1)

            memory(0)
            norm(3, 4, G_MIX + KT)
            for t in range(16):
                if t == 3:
                    dve.wait_ge(n_whi, 1)
                    nc.vector.tensor_tensor(wgt_lo[:, :, :], wgt[:, :, :], wgt_hi[:, :, :].bitcast(F32),
                                            ALU.subtract).then_inc(n_wlo, 1)
                if t == 11:
                    dve.wait_ge(n_gturn, 1)
                    nc.vector.tensor_copy(gate[:, :, :].rearrange("p a n -> p (a n)"),
                                          att[:, 1, 0:96]).then_inc(n_gate, 1)
                if t % 8 == 7:
                    b = BLOCK["kcvc"] + t // 8
                    dve.wait_ge(pieces_done, TICK["kcvc"] + t + 1)
                    nc.vector.tensor_copy((kcT, vcT)[t // 8][:, :, :].rearrange("p a t -> p (a t)"),
                                          acc[:, b % 2, :]).then_inc(c_in, 1)
                    freed(b, c_in, t // 8 + 1)
                split(TICK["kcvc"] + t + LEAD)
            for t in range(16):
                if t % 8 == 7:
                    freed(BLOCK["cmp"] + t // 8, c_row, t // 8 + 1)
                if t == 8:
                    hidden_turned(0)
                if t == 9:
                    dve.wait_ge(c_ksum, 1)
                    nc.vector.tensor_copy(kcmp[:, 0:CMP_COLS], att[:, 1, 0:CMP_COLS]).then_inc(c_kraw, 1)
                if t == 12:
                    dve.wait_ge(c_krms, 1)
                    nc.vector.reciprocal(kcr[:, 0:CMP_COLS], kcr[:, 0:CMP_COLS]).then_inc(c_krinv, 1)
                    dve.wait_ge(c_krinv, 1)
                    nc.vector.scalar_tensor_tensor(out=kcmp[:, 0:CMP_COLS], in0=kcmp[:, 0:CMP_COLS],
                                                   scalar=S[:, S_NK:S_NK + 1], in1=kcr[:, 0:CMP_COLS],
                                                   op0=ALU.mult, op1=ALU.mult).then_inc(c_kout, 1)
                if t >= 14:
                    mem_scale(1, t - 14)
                split(TICK["cmp"] + t + LEAD)
            for t in range(32):
                b = BLOCK["kvs"] + t // 8
                if t == 0:
                    hidden_turned(1)
                if t == 2:
                    dve.wait_ge(c_v, 1)
                    nc.vector.tensor_copy(vcmp[:, :, :], att[0:N_CMP, 3, :].rearrange("p (g d) -> p g d", g=4)).then_inc(c_vout, 1)
                if 1 <= t < 9:
                    mem_low(1, t - 1)
                if t in (7, 15):
                    hn_take(HN[("kw", "ks")[t // 8]], b, (kw, ks)[t // 8][:, :, :], TICK["kvs"] + t)
                if t in (11, 13, 19, 21):
                    k = t // 8 - 1
                    hn_scale(HN[("kw", "ks")[k]], b - 1, t % 8 // 4, (kw, ks)[k][:, :, :], (S_NK + 2, S_NK + 1)[k])
                if t in (23, 31):
                    dve.wait_ge(pieces_done, TICK["kvs"] + t + 1)
                    nc.vector.tensor_copy((vw, vs)[t // 8 - 2][:, :, :],
                                          acc[:, b % 2, :].rearrange("p (a n) -> p a n", a=2)).then_inc(n_v, 1)
                    freed(b, n_v, t // 8 - 1)
                split(TICK["kvs"] + t + LEAD)

            dve.wait_ge(n_mask, 7)
            for t in range(32):
                if t % 8 == 7:
                    k = t // 8
                    hn_take(HN[f"q{k}"], BLOCK["q"] + k, nq[:, 4 * k:4 * k + 4, :], TICK["q"] + t)
                if t == 31:
                    nsa_low(0)
                    nsa_low(1)
                if (t - NSA_START) % 2 == 0:
                    nsa(t - NSA_START)
                split(TICK["q"] + t + LEAD)
                if t % 8 in (1, 3) and t >= 8:
                    q_scale(t // 8 - 1, t % 8 // 2)
                if (t - NSA_START) % 2:
                    nsa(t - NSA_START)
            memory(1)

        @block.tensor
        def _(pe):
            def sums3(o, lhi, llo, rhi, rlo, start, stop):
                nc.tensor.matmul(o, lhi, rhi, start=start, stop=False, skip_group_check=True)
                nc.tensor.matmul(o, lhi, rlo, start=False, stop=False, skip_group_check=True)
                return nc.tensor.matmul(o, llo, rhi, start=False, stop=stop, skip_group_check=True)

            def piece(p, par, kts, x_hi, x_lo, first, last, tokens_out=False, more=0):
                pe.wait_ge(lo_ready, p + 1 + more)
                s = p % LEAD
                for k in range(2):
                    start, stop = first and k == 0, last and k == 1
                    if tokens_out:
                        for a in range(2):
                            mm = sums3(acc[:, par, a * NB:(a + 1) * NB], x_hi(kts + k, a), x_lo(kts + k, a),
                                       w_hi[:, s, k, :], w_lo[:, s, k, :], start, stop)
                    else:
                        for n in range(4):
                            cs = slice(n * P, (n + 1) * P)
                            mm = sums3(acc[:, par, n * T:(n + 1) * T], w_hi[:, s, k, cs], w_lo[:, s, k, cs],
                                       x_hi(kts + k), x_lo(kts + k), start and n % 2 == 0, stop)
                mm.then_inc(pieces_done, 1)

            def tile_of(x):
                def get(kt, a=None):
                    return x[:, kt, :] if a is None else x[:, kt, a * P:(a + 1) * P]
                return get

            HH, HL = tile_of(h_hi), tile_of(h_lo)

            def claim(b):
                if b >= 2:
                    pe.wait_ge(acc_free[b % 2], b // 2)

            def norm_sum(n, c):
                if c < ADDED[n]:
                    return
                if c == ADDED[n] and c:
                    pe.wait_ge(sq_added, sum(ADDED[:n + 1]))
                else:
                    pe.wait_ge(sq_ready, 8 * n + c + 1)
                for k in range(2):
                    mm = nc.tensor.matmul(att[:, 3, 0:T], ones[:, :], tmp[:, 2 * (c % 2) + k, :],
                                          start=(c == ADDED[n] and k == 0), stop=(c == 7 and k == 1))
                mm.then_inc(sq_used, 1)

            def hn_total(i, b):
                pe.wait_ge(hn_sq, i + 1)
                for a in range(2):
                    mm = nc.tensor.matmul(acc[:, b % 2, a * NB:(a + 1) * NB], ones[:, :],
                                          tmp[:, 2 * a:2 * a + 2, :].rearrange("p k t -> p (k t)"), start=True, stop=True)
                mm.then_inc(hn_sum, 1)

            def mem_turn(l, c):
                pe.wait_ge(m_scaled, 2 * l + 2)
                if l == 0 and c == 0:
                    pe.wait_ge(f_max, FOX_HEADS)
                if c >= 2:
                    pe.wait_ge(m_ready, 8 * l + c - 1)
                for k in range(2):
                    for a in range(2):
                        mm = nc.tensor.transpose(att[:, c % 2, k * T + a * P:k * T + (a + 1) * P],
                                                 mtok[l][:, a, (2 * c + k) * P:(2 * c + k + 1) * P], ident[:, :])
                mm.then_inc(m_turn, 1)

            pe.wait_ge(consts, 7)
            for c in range(10):
                if c < 8:
                    if c % 2 == 0:
                        pe.wait_ge(xtok_in[c // 2], 16)
                    if c >= 3:
                        pe.wait_ge(x_copied, c - 2)
                    for k in range(2):
                        for a in range(2):
                            mm = nc.tensor.transpose(att[:, c % 3, k * T + a * P:k * T + (a + 1) * P],
                                                     xtok[:, a, (2 * c + k) * P:(2 * c + k + 1) * P], ident[:, :])
                    mm.then_inc(x_turn, 1)
                if c >= 2:
                    norm_sum(0, c - 2)
            pe.wait_ge(small_in, 16 * 13)
            pe.wait_ge(x_copied, 8)
            nc.tensor.transpose(att[:, 0, 0:P], g_rows[:, :], ident[:, :]).then_inc(gains_t, 1)
            nc.tensor.transpose(att[:, 1, 0:S_ROWS], s_rows[:, :], ident[0:S_ROWS, 0:S_ROWS]).then_inc(gains_t, 1)

            def fox_gates():
                pe.wait_ge(ff_wlo, 1)
                o = att[0:FOX_HEADS, 0, 0:T]
                for kt in range(KT):
                    sums3(o, wff_hi[:, kt, :], wff_lo[:, kt, :], HH(kt), HL(kt), kt == 0, False)
                for a in range(2):
                    mm = nc.tensor.matmul(o[:, a * P:(a + 1) * P], fbias[0:1, :], ones[0:1, :], start=False,
                                          stop=a == 1, skip_group_check=True)
                mm.then_inc(ff_sum, 1)

            def level(u):
                n, r = divmod(u - 2, 2)
                p, l = divmod(n, LEVELS)
                if r == 1 and 0 <= n < 4 * LEVELS:
                    m = p * 8 + l - 1
                    if n >= 2:
                        pe.wait_ge(hg_merged, n - 1)
                    if l == 0:
                        pe.wait_ge(hg_k, p // 2 + 1)
                        pe.wait_ge(hg_q, p // 2 + 1)
                        pe.wait_ge(ff_z, 1)
                        kx, qx = hz[:, 2 * p:2 * p + 2, :].rearrange("p a t -> p (a t)"), hq[:, 2 * p:2 * p + 2, :].rearrange("p a t -> p (a t)")
                    else:
                        pe.wait_ge(hg_kd, m + 1)
                        pe.wait_ge(hg_qd, m + 1)
                        kx, qx = kd[:, m % 2, :], qd[:, m % 2, :]
                    for a in range(2):
                        if l < 8:
                            for b in range(2):
                                c = a * T + b * P
                                mm = nc.tensor.matmul(att[:, n % 2, c:c + P], kx[:, c:c + P], qx[:, c:c + P],
                                                      start=True, stop=True)
                        else:
                            mm = nc.tensor.matmul(att[:, n % 2, a * P:(a + 1) * P], kx[:, a * T:a * T + P],
                                                  qx[:, a * T + P:(a + 1) * T], start=True, stop=True)
                    mm.then_inc(hg_scores, 1)
                o, r = divmod(u - 4, 2 * LEVELS)
                o -= 1
                if r == 0 and o >= 0:
                    pe.wait_ge(hg_merged, LEVELS * (o + 1))
                    pe.wait_ge(hg_v, o // 2 + 1)
                    if o:
                        pe.wait_ge(hg_oraw, o)
                    for a in range(2):
                        h = 2 * o + a
                        v0, v1 = hv[:, 0, h * P:(h + 1) * P], hv[:, 1, h * P:(h + 1) * P]
                        nc.tensor.matmul(att[:, 2, a * T:a * T + P], v0, AT[:, 2 * a, :], start=True, stop=True)
                        nc.tensor.matmul(att[:, 2, a * T + P:(a + 1) * T], v0, AT[:, 4 + a, :], start=True, stop=False)
                        mm = nc.tensor.matmul(att[:, 2, a * T + P:(a + 1) * T], v1, AT[:, 2 * a + 1, :],
                                              start=False, stop=True)
                    mm.then_inc(hg_o, 1)
                if r == 2 and o >= 0:
                    pe.wait_ge(hg_osq, o + 1)
                    if o:
                        pe.wait_ge(hg_onorm, o)
                    nc.tensor.matmul(att[:, 3, :], ones[:, :], tmp[:, 0:2, :].rearrange("p k t -> p (k t)"),
                                     start=True, stop=True).then_inc(hg_osum, 1)

            T0 = TICK["in0"]
            def fox_scores(u):
                if u == 0:
                    pe.wait_ge(hn_out, 2 * HN["fk0"] + 2)
                    pe.wait_ge(ff_cneg, 1)
                    pe.wait_ge(hg_merged, 4 * LEVELS)
                if u == 4:
                    pe.wait_ge(hn_out, 2 * HN["fk1"] + 2)
                if u >= 2:
                    pe.wait_ge(f_max, u - 1)
                pick = ident[0:FOX_HEADS, u:u + 1].broadcast_to([FOX_HEADS, P])
                for a, cs, w in ((0, slice(0, P), P), (1, slice(P, 384), T)):
                    nc.tensor.matmul(att[:, u % 2, cs], fq[:, u, a * P:(a + 1) * P], fk[:, u, 0:w],
                                     start=True, stop=False)
                    mm = nc.tensor.matmul(att[:, u % 2, cs], pick, cneg[:, 0:w], start=False, stop=True)
                mm.then_inc(f_s, 1)

            def fox_turn(u):
                pe.wait_ge(f_pn, u + 1)
                if u:
                    pe.wait_ge(f_pt, u)
                else:
                    pe.wait_ge(hg_oraw, 4)
                for i in range(3):
                    mm = nc.tensor.transpose(att[:, 2, i * P:(i + 1) * P], fp[:, u % 4, i * P:(i + 1) * P], ident[:, :])
                mm.then_inc(f_t, 1)

            def fox_values(u):
                pe.wait_ge(f_pt, u + 1)
                if u:
                    pe.wait_ge(f_out, u)
                else:
                    pe.wait_ge(hg_onorm, 4)
                    pe.wait_ge(f_v, 1)
                if u == 4:
                    pe.wait_ge(f_v, 2)
                v0, v1 = fv[:, 0, u * P:(u + 1) * P], fv[:, 1, u * P:(u + 1) * P]
                pt = fpt[:, u % 2, :]
                nc.tensor.matmul(att[:, 3, 0:P], v0, pt[:, 0:P], start=True, stop=True)
                nc.tensor.matmul(att[:, 3, P:T], v0, pt[:, P:T], start=True, stop=False)
                nc.tensor.matmul(att[:, 3, P:T], v1, pt[:, T:384], start=False, stop=True).then_inc(f_o, 1)

            def fox(v):
                if 0 <= v < FOX_HEADS:
                    fox_scores(v)
                if 0 <= v - 3 < FOX_HEADS:
                    fox_turn(v - 3)
                if 0 <= v - 4 < FOX_HEADS:
                    fox_values(v - 4)

            for b, name in enumerate(IN0):
                claim(b)
                done = IN0[b - 1] if b else None
                k = KTH[b - 1] if b else 0
                for j in range(8):
                    if b == 0:
                        pe.wait_ge(h_ready, j + 1)
                    piece(T0 + 8 * b + j, b % 2, 2 * j, HH, HL, j == 0, j == 7, name in ("hi", "fv"))
                    if b == 1 and j == 0:
                        fox_gates()
                    if done in ("fq", "fk") and j == 1:
                        hn_total(HN[done + str(k)], b - 1)
                    if 8 * b + j >= HG_START:
                        level(8 * b + j - HG_START)
                    fox(8 * b + j - FOX_START)

            def nsa_scores(u):
                g = u // 4
                if u == 0:
                    pe.wait_ge(m_ready, 16)
                    pe.wait_ge(c_kout, 1)
                    pe.wait_ge(c_vout, 1)
                    pe.wait_ge(n_v, 2)
                else:
                    pe.wait_ge(n_p, u)
                if u % 2 == 0:
                    pe.wait_ge(hn_out, 2 * HN[f"q{g}"] + u % 4 // 2 + 1)
                for br, kx in ((0, kw), (1, ks)):
                    nc.tensor.matmul(att[:, br, 0:P], nq[:, u, 0:P], kx[:, g, 0:P], start=True, stop=True)
                    nc.tensor.matmul(att[:, br, P:384], nq[:, u, P:T], kx[:, g, :], start=True, stop=True)
                for a in range(2):
                    mm = nc.tensor.matmul(att[:, 0, 384 + 16 * a:384 + 16 * a + N_CMP], nq[:, u, a * P:(a + 1) * P],
                                          kcmp[:, g * N_CMP:(g + 1) * N_CMP], start=True, stop=True)
                mm.then_inc(n_s, 1)

            def nsa_turn(u, br):
                if br == 0:
                    pe.wait_ge(n_pn, u + 1)
                if 2 * u + br >= 1:
                    pe.wait_ge(n_pt, 2 * u + br)
                for i in range(3):
                    mm = nc.tensor.transpose(att[:, 2, i * P:(i + 1) * P], np_[:, u % 2, br, i * P:(i + 1) * P], ident[:, :])
                mm.then_inc(n_t, 1)

            def nsa_turn_cmp(u):
                if u:
                    pe.wait_ge(n_out, u)
                for a in range(2):
                    mm = nc.tensor.transpose(att[0:N_CMP, 3, T + a * P:T + (a + 1) * P], npc[:, u % 2, a, 0:N_CMP], ident[:, :])
                mm.then_inc(n_tc, 1)

            def nsa_values(u):
                g = u // 4
                gs = slice(g * P, (g + 1) * P)
                pe.wait_ge(n_ptc, u + 1)
                for a in range(2):
                    nc.tensor.matmul(att[:, 3, a * P:(a + 1) * P], vcmp[:, g, :], nptc[:, a, :], start=(a == 0),
                                     stop=False, skip_group_check=True)
                for br, vx in ((0, vw), (1, vs)):
                    pe.wait_ge(n_pt, 2 * u + br + 1)
                    pt = npt[:, br, :]
                    nc.tensor.matmul(att[:, 3, 0:P], vx[:, 0, gs], pt[:, 0:P], start=False, stop=br == 1, skip_group_check=True)
                    nc.tensor.matmul(att[:, 3, P:T], vx[:, 0, gs], pt[:, P:T], start=False, stop=False, skip_group_check=True)
                    mm = nc.tensor.matmul(att[:, 3, P:T], vx[:, 1, gs], pt[:, T:384], start=False, stop=br == 1, skip_group_check=True)
                mm.then_inc(n_o, 1)

            def nsa(v):
                u, r = divmod(v, 2)
                if r == 1 and 0 <= u - 2 < NSA_HEADS:
                    nsa_values(u - 2)
                if r == 0 and 0 <= u < NSA_HEADS:
                    nsa_scores(u)
                if r == 1 and 0 <= u - 1 < NSA_HEADS:
                    nsa_turn(u - 1, 0)
                if r == 0 and 0 <= u - 2 < NSA_HEADS:
                    nsa_turn(u - 2, 1)
                    nsa_turn_cmp(u - 2)

            def memory(l):
                n0 = 3 * l
                f = FILL[f"out{l}"]
                MH, ML = tile_of(memn[l][0]), tile_of(memn[l][1])
                t0 = TICK[f"out{l}"]
                for t in range(32):
                    if t < 16:
                        b, j = t // 2 % 2, t // 4 * 2 + t % 2
                    else:
                        b, j = divmod(t, 8)
                    if j == 0:
                        claim(BLOCK[f"out{l}"] + b)
                    if b == 0:
                        pe.wait_ge(h_ready, 8 * f + j + 1)
                    piece(t0 + t, (BLOCK[f"out{l}"] + b) % 2, 2 * FILL_ORDER[f][j], HH, HL, j == 0, j == 7)
                    if l == 0:
                        fox(112 + t - FOX_START)
                        if 0 <= t - MEM_START < 8:
                            mem_turn(0, t - MEM_START)
                    else:
                        for v in nsa_ticks(t):
                            nsa(v)
                        if t == 0:
                            hn_total(HN["q3"], BLOCK["q"] + 3)
                    if t - 2 in OUT_SQUARES:
                        if t == 16:
                            pe.wait_ge(f_out if l == 0 else n_out, FOX_HEADS if l == 0 else NSA_HEADS)
                        norm_sum(n0 + 1, OUT_SQUARES[t - 2])
                        norm_sum(n0 + 1, OUT_SQUARES[t - 2] + 1)
                claim(BLOCK[f"kvk{l}"])
                for j in range(8):
                    pe.wait_ge(m_ready, 8 * l + 8)
                    piece(TICK[f"kvk{l}"] + j, BLOCK[f"kvk{l}"] % 2, 2 * j, MH, ML, j == 0, j == 7)
                    if j == 0:
                        norm_sum(n0 + 1, 6)
                        norm_sum(n0 + 1, 7)
                claim(BLOCK[f"wq{l}"])
                for j in range(8):
                    pe.wait_ge(h_ready, 8 * FILL[f"wq{l}"] + j + 1)
                    piece(TICK[f"wq{l}"] + j, BLOCK[f"wq{l}"] % 2, 2 * j, HH, HL, j == 0, j == 7)
                    if j == 0:
                        hn_total(HN[f"mk{l}"], BLOCK[f"kvk{l}"])

                def m_scores(u):
                    n = MEM_HEADS * l + u
                    if u == 0:
                        pe.wait_ge(hn_out, 2 * HN[f"mq{l}"] + 1)
                    if u >= 2:
                        pe.wait_ge(hn_out, 2 * HN[f"mq{l}"] + 2)
                        pe.wait_ge(m_exp, n - 1)
                    for a in range(2):
                        mm = nc.tensor.matmul(att[:, u % 2, a * T:(a + 1) * T], mq[:, u, a * P:(a + 1) * P], mk[:, u, :],
                                              start=True, stop=True)
                    mm.then_inc(m_s, 1)

                def m_turns(u):
                    n = MEM_HEADS * l + u
                    pe.wait_ge(m_pn, n + 1)
                    if u == 1:
                        pe.wait_ge(m_exp, n + 2)
                    if u >= 2:
                        pe.wait_ge(m_pt, n - 1)
                    for k in range(2):
                        for a in range(2):
                            mm = nc.tensor.transpose(att[:, (2, 0)[u % 2], k * T + a * P:k * T + (a + 1) * P],
                                                     mp[:, u, a, k * P:(k + 1) * P], ident[:, :])
                    mm.then_inc(m_t, 1)

                def m_values(u):
                    n = MEM_HEADS * l + u
                    pe.wait_ge(m_pt, n + 1)
                    if u == 1:
                        pe.wait_ge(m_exp, n + 3)
                    if u >= 2:
                        pe.wait_ge(m_out, n - 1)
                    if u == 0:
                        pe.wait_ge(rms_ready, n0 + 2)
                        pe.wait_ge(m_v, l + 1)
                    for k in range(2):
                        mm = nc.tensor.matmul(att[:, (3, 1)[u % 2], 0:T], mv[:, k, u * P:(u + 1) * P], mpt[:, u, k, :],
                                              start=(k == 0), stop=(k == 1))
                    mm.then_inc(m_o, 1)

                claim(BLOCK[f"kvv{l}"])
                for t in range(MEM_TICKS):
                    if t < 8:
                        piece(TICK[f"kvv{l}"] + t, BLOCK[f"kvv{l}"] % 2, 2 * t, MH, ML, t == 0, t == 7, True)
                    if t == 0:
                        hn_total(HN[f"mq{l}"], BLOCK[f"wq{l}"])
                    if 0 <= t - 3 < MEM_HEADS:
                        m_scores(t - 3)
                    if 0 <= t - 6 < MEM_HEADS:
                        m_turns(t - 6)
                    if 0 <= t - 8 < MEM_HEADS:
                        m_values(t - 8)
                MOH, MOL = tile_of(mo_hi), tile_of(mo_lo)
                for b in range(4):
                    claim(BLOCK[f"wo{l}"] + b)
                    for j in range(2):
                        if b == 0:
                            pe.wait_ge(m_out, MEM_HEADS * l + 2 * j + 2)
                        piece(TICK[f"wo{l}"] + 2 * b + j, (BLOCK[f"wo{l}"] + b) % 2, 2 * j, MOH, MOL, j == 0, j == 1)
                    if b:
                        norm_sum(n0 + 2, 2 * b - 2)
                        norm_sum(n0 + 2, 2 * b - 1)
                norm_sum(n0 + 2, 6)
                norm_sum(n0 + 2, 7)
                t0, b0 = TICK[f"up{l}"], BLOCK[f"up{l}"]
                for b in range(2):
                    claim(b0 + b)
                    for j in range(8):
                        if b == 0:
                            pe.wait_ge(h_ready, 8 * FILL[f"up{l}"] + j + 1)
                        piece(t0 + 8 * b + j, (b0 + b) % 2, 2 * j, HH, HL, j == 0, j == 7)
                with pe.Fori(1, FB) as i:
                    for b in range(2):
                        pe.wait_ge(acc_free[(b0 + b) % 2], i + (b0 + b) // 2)
                        for j in range(8):
                            piece(t0 + 8 * b + j, (b0 + b) % 2, 2 * j, HH, HL, j == 0, j == 7, more=i * 16)

                def hidden(x, i):
                    flat = x[:, :, :].rearrange("p k t -> p (k t)")

                    def get(kt):
                        return flat[:, bass.ds(i * 8 * T + kt * T, T)]
                    return get

                pe.wait_ge(u_ready, FB * (l + 1))
                for half in range(2):
                    t0, b0 = TICK[f"dn{l}"] + 44 * half, BLOCK[f"dn{l}"] + 2 * half
                    XH, XL = tile_of(hid_hi), tile_of(hid_lo)
                    for b in range(2):
                        claim(b0 + b)
                        for j in range(2):
                            piece(t0 + 2 * b + j, (b0 + b) % 2, 2 * j, XH, XL, j == 0, False)
                    with pe.Fori(0, 4) as i:
                        for g in range(2):
                            for b in range(2):
                                for j in range(2):
                                    piece(t0 + 4 + 4 * g + 2 * b + j, (b0 + b) % 2, 4 + 4 * g + 2 * j,
                                          hidden(hid_hi, i), hidden(hid_lo, i), False, False, more=i * 8)
                    for g in range(2):
                        for b in range(2):
                            for j in range(2):
                                if l == 0 and half and g == 1 and b == 1 and j == 1:
                                    norm_sum(3, 3)
                                    norm_sum(3, 4)
                                piece(t0 + 36 + 4 * g + 2 * b + j, (b0 + b) % 2, 36 + 4 * g + 2 * j,
                                      XH, XL, False, g == 1 and j == 1)
                    if l == 0 and half:
                        for c in range(5, 8):
                            norm_sum(3, c)

            memory(0)
            for t in range(16):
                b, j = divmod(t, 8)
                if j == 0:
                    claim(BLOCK["kcvc"] + b)
                if b == 0:
                    pe.wait_ge(h_ready, 8 * 4 + j + 1)
                piece(TICK["kcvc"] + t, (BLOCK["kcvc"] + b) % 2, 2 * j, HH, HL, j == 0, j == 7)
                if t == 8:
                    pe.wait_ge(n_wlo, 1)
                    for kt in range(KT):
                        mm = sums3(att[0:48, 0, 0:T], wgt_hi[:, kt, :], wgt_lo[:, kt, :], HH(kt), HL(kt),
                                   kt == 0, kt == KT - 1)
                    mm.then_inc(n_gsum, 1)
                if t == 10:
                    pe.wait_ge(n_gateT, 1)
                    for a in range(2):
                        mm = nc.tensor.transpose(att[:, 1, 48 * a:48 * a + 48], gateT[:, a * P:(a + 1) * P],
                                                 ident[0:48, 0:48])
                    mm.then_inc(n_gturn, 1)
            def hidden_turn(v):
                pe.wait_ge(c_row, v + 1)
                for m in range(2):
                    mm = nc.tensor.transpose(att[:, 2, 64 * m:64 * m + CMP_COLS], hrow[:, v, m * P:(m + 1) * P],
                                             ident[0:CMP_COLS, 0:CMP_COLS])
                mm.then_inc(c_turn, 1)

            for t in range(16):
                v, j = divmod(t, 8)
                par = (BLOCK["cmp"] + v) % 2
                if j == 0:
                    claim(BLOCK["cmp"] + v)
                    pe.wait_ge(c_lo, v + 1)
                p = TICK["cmp"] + t
                pe.wait_ge(lo_ready, p + 1)
                wh = w_hi[:, p % LEAD, :, :].rearrange("p a (b m) -> p (a b) m", m=256)
                wl = w_lo[:, p % LEAD, :, :].rearrange("p a (b m) -> p (a b) m", m=256)
                for i in range(4):
                    l = 4 * j + i
                    mm = sums3(acc[0:CMP_COLS, par, 0:2 * P], xc_hi[v][:, l, 0:CMP_COLS], xc_lo[v][:, l, 0:CMP_COLS],
                               wh[:, i, :], wl[:, i, :], l == 0, l == CMP_L - 1)
                mm.then_inc(pieces_done, 1)
                if t == 8:
                    hidden_turn(0)
                if t == 9:
                    pe.wait_ge(c_w2, 32)
                    pe.wait_ge(c_hid, 1)
                    for m in range(2):
                        mm = nc.tensor.matmul(att[:, 1, 0:CMP_COLS], w2c[:, 0, m, :], hidc[:, 0, m, 0:CMP_COLS],
                                              start=(m == 0), stop=(m == 1))
                    mm.then_inc(c_ksum, 1)
                if t == 11:
                    pe.wait_ge(c_ksq, 1)
                    nc.tensor.matmul(att[:, 2, 256:256 + CMP_COLS], ones[:, :], kcr[:, 0:CMP_COLS], start=True,
                                     stop=True).then_inc(c_ksum, 1)
            for t in range(32):
                b, j = divmod(t, 8)
                if j == 0:
                    claim(BLOCK["kvs"] + b)
                piece(TICK["kvs"] + t, (BLOCK["kvs"] + b) % 2, 2 * j, HH, HL, j == 0, j == 7, b >= 2)
                if t == 0:
                    hidden_turn(1)
                if t == 1:
                    pe.wait_ge(c_hid, 2)
                    for g in range(4):
                        for m in range(2):
                            mm = nc.tensor.matmul(att[0:N_CMP, 3, g * P:(g + 1) * P],
                                                  hidc[:, 1, m, g * N_CMP:(g + 1) * N_CMP],
                                                  w2c[:, 1, m, :], start=(m == 0), stop=(m == 1))
                    mm.then_inc(c_v, 1)
                if 1 <= t < 9:
                    mem_turn(1, t - 1)
                if t in (9, 17):
                    hn_total(HN[("kw", "ks")[b - 1]], BLOCK["kvs"] + b - 1)

            for t in range(32):
                b, j = divmod(t, 8)
                if j == 0:
                    claim(BLOCK["q"] + b)
                piece(TICK["q"] + t, (BLOCK["q"] + b) % 2, 2 * j, HH, HL, j == 0, j == 7)
                if j == 0 and t:
                    hn_total(HN[f"q{b - 1}"], BLOCK["q"] + b - 1)
                nsa(t - NSA_START)
            memory(1)
            for g in range(8):
                b, a = divmod(g, 2)
                pe.wait_ge(x_ready, 24 + b + 1)
                if g >= 4:
                    pe.wait_ge(out_copied, g - 3)
                else:
                    pe.wait_ge(rms_ready, 6)
                for k in range(4):
                    mm = nc.tensor.transpose(att[:, g % 4, k * P:(k + 1) * P], xT[:, 4 * b + k, a * P:(a + 1) * P], ident[:, :])
                mm.then_inc(out_turn, 1)


NSA_START = 11
FOX_CHUNK = {0: 6, 1: 7, 4: 0, 5: 1, 6: 2, 7: 3}
NSA_CHUNK = {1: 2, 2: 3, 3: 4, 7: 5, 11: 6, 12: 7}
MEM_START = 11
NORM_CHUNKS = {1: (0, 3), 2: (3, 6), 3: (6, 8)}
MEM_TICKS = 8 + MEM_HEADS
OUT_LAST = [13, 15, 23, 31]
OUT_SQUARES = {14: 0, 17: 2, 24: 4}
FILL_ORDER = [list(range(8)), [4, 5, 6, 7, 0, 1, 2, 3]] + [list(range(8))] * 6


_INS = ["x", "mem", "norm_mix", "norm_mem", "norm_ffn", "mem_in_gain", "even_w_in", "even_w_out", "fox_f_bias",
        "fox_q_gain", "fox_k_gain", "hgrn_lb_logits", "hgrn_o_gain", "odd_w_in", "odd_w_out", "nsa_q_gain",
        "nsa_k_gain", "cmp_pe_k", "cmp_w1_k", "cmp_w2_k", "cmp_pe_v", "cmp_w1_v", "cmp_w2_v", "mem_wq",
        "mem_wkv", "mem_wo", "mem_q_gain", "mem_k_gain", "ffn_w1", "ffn_w3", "ffn_w2"]


def kernel(**inputs):
    import numpy as _np
    import concourse.bacc as _bacc
    from concourse import mybir as _mybir
    from concourse.bass_utils import run_bass_kernel_spmd as _run

    nc = _bacc.Bacc("TRN2", target_bir_lowering=False, num_devices=1)
    arrays, args = {}, {}
    for name in _INS:
        a = _np.ascontiguousarray(inputs[name])
        arrays[f"in_{name}"] = a
        args[name] = nc.dram_tensor(f"in_{name}", a.shape, _mybir.dt.from_np(a.dtype), kind="ExternalInput").ap()
    shape = inputs["x"].shape
    out = nc.dram_tensor("out_0", shape, _mybir.dt.float32, kind="ExternalOutput").ap()
    trunk(nc, args, out)
    return _run(nc, [arrays], core_ids=[0]).results[0]["out_0"]
```
